# Optimizing a Trainium2 kernel written in Bass

```python
import jax, jax.numpy as jnp
from jax import lax
import numpy as np

D_MODEL = 1024
BATCH = 1
SEQ = 1024
DEPTH = 2

N_MIXERS = 2
PLE_DIM = 256
ROPE_THETA = 10000.0
NORM_EPS = 1e-6
Q_BLOCK = 128

MLA_HEADS = 8
MLA_Q_RANK = 256
MLA_KV_RANK = 256
MLA_NOPE_DIM = 128
MLA_ROPE_DIM = 64
MLA_V_DIM = 128
MLA_WIDTH = MLA_HEADS * MLA_V_DIM
MLA_SPLITS = [MLA_Q_RANK, MLA_Q_RANK + MLA_KV_RANK, MLA_Q_RANK + MLA_KV_RANK + MLA_ROPE_DIM]
MLA_IN = MLA_Q_RANK + MLA_KV_RANK + MLA_ROPE_DIM + MLA_WIDTH

DSA_HEADS = 8
DSA_KV_HEADS = 2
DSA_HEAD_DIM = 128
DSA_WIDTH = DSA_HEADS * DSA_HEAD_DIM
IDX_HEADS = 8
IDX_DIM = 64
TOPK_MAX = 256
DSA_SIZES = [DSA_WIDTH, DSA_KV_HEADS * DSA_HEAD_DIM, DSA_KV_HEADS * DSA_HEAD_DIM,
             IDX_HEADS * IDX_DIM, IDX_DIM, IDX_HEADS, DSA_WIDTH]
DSA_SPLITS = [int(v) for v in np.cumsum(DSA_SIZES)[:-1]]
DSA_IN = int(sum(DSA_SIZES))

N_MLA_LAYERS = (DEPTH + 1) // 2
N_DSA_LAYERS = DEPTH // 2

kernel_name = "hybrid_mla_dsa_gated_ple"

def rmsnorm(x, g):
    xf = x.astype(jnp.float32)
    y = xf * lax.rsqrt(jnp.mean(xf * xf, axis=-1, keepdims=True) + NORM_EPS)
    return (y * g.astype(jnp.float32)).astype(x.dtype)

def rope(x, pos):
    d = x.shape[-1]
    half = d // 2
    inv = 1.0 / (ROPE_THETA ** (jnp.arange(half, dtype=jnp.float32) / half))
    ang = pos.astype(jnp.float32)[..., None] * inv
    ang = ang.reshape(ang.shape[:2] + (1,) * (x.ndim - 3) + (half,))
    cos, sin = jnp.cos(ang), jnp.sin(ang)
    xf = x.astype(jnp.float32)
    x1, x2 = xf[..., :half], xf[..., half:]
    return jnp.concatenate([x1 * cos - x2 * sin, x2 * cos + x1 * sin], axis=-1).astype(x.dtype)

def sweep_query_blocks(fn, batch, seq):
    out = lax.map(fn, jnp.arange(seq // Q_BLOCK))
    out = jnp.moveaxis(out, 0, 1)
    return out.reshape((batch, seq) + out.shape[3:])

def mla_attention(q_lat, q_pe, c_kv, k_pe):
    B, S = c_kv.shape[:2]
    scale = (MLA_NOPE_DIM + MLA_ROPE_DIM) ** -0.5
    key_pos = jnp.arange(S)

    def block(i):
        start = i * Q_BLOCK
        ql = lax.dynamic_slice_in_dim(q_lat, start, Q_BLOCK, axis=1)
        qp = lax.dynamic_slice_in_dim(q_pe, start, Q_BLOCK, axis=1)
        s = (jnp.einsum('bqhc,bkc->bhqk', ql, c_kv)
             + jnp.einsum('bqhr,bkr->bhqk', qp, k_pe)).astype(jnp.float32) * scale
        qpos = start + jnp.arange(Q_BLOCK)
        causal = key_pos[None, :] <= qpos[:, None]
        s = jnp.where(causal[None, None], s, -jnp.inf)
        pr = jax.nn.softmax(s, axis=-1).astype(c_kv.dtype)
        return jnp.einsum('bhqk,bkc->bqhc', pr, c_kv)

    return sweep_query_blocks(block, B, S)

def mla_branch(h, pos, w_in, q_norm, kv_norm, w_uq, w_uk, w_uv, w_out):
    B, S, _ = h.shape
    c_q, c_kv, k_pe, z = jnp.split(h @ w_in, MLA_SPLITS, axis=-1)
    c_q = rmsnorm(c_q, q_norm)
    c_kv = rmsnorm(c_kv, kv_norm)
    q = (c_q @ w_uq).reshape(B, S, MLA_HEADS, MLA_NOPE_DIM + MLA_ROPE_DIM)
    q_nope, q_pe = q[..., :MLA_NOPE_DIM], q[..., MLA_NOPE_DIM:]
    q_pe = rope(q_pe, pos)
    k_pe = rope(k_pe, pos)
    q_lat = jnp.einsum('bshn,chn->bshc', q_nope, w_uk)
    o_lat = mla_attention(q_lat, q_pe, c_kv, k_pe)
    o = jnp.einsum('bshc,chv->bshv', o_lat, w_uv).reshape(B, S, MLA_WIDTH)
    return (o * jax.nn.silu(z)) @ w_out

def dsa_attention(q, k, v, q_idx, k_idx, w_idx, top_k):
    B, S = k.shape[:2]
    G = DSA_KV_HEADS
    R = DSA_HEADS // DSA_KV_HEADS
    scale = DSA_HEAD_DIM ** -0.5
    key_pos = jnp.arange(S)
    gather = jax.vmap(lambda a, ix: a[ix])

    def block(i):
        start = i * Q_BLOCK
        qpos = start + jnp.arange(Q_BLOCK)
        causal = key_pos[None, :] <= qpos[:, None]
        qi = lax.dynamic_slice_in_dim(q_idx, start, Q_BLOCK, axis=1)
        wi = lax.dynamic_slice_in_dim(w_idx, start, Q_BLOCK, axis=1).astype(jnp.float32)
        logits = jnp.einsum('bqhd,bkd->bqhk', qi, k_idx).astype(jnp.float32) * (IDX_DIM ** -0.5)
        score = jnp.einsum('bqhk,bqh->bqk', jax.nn.relu(logits), wi * (IDX_HEADS ** -0.5))
        score = jnp.where(causal[None], score, -jnp.inf)
        _, idx = lax.top_k(score, top_k)
        valid = idx <= qpos[None, :, None]
        k_sel = gather(k, idx)
        v_sel = gather(v, idx)
        qb = lax.dynamic_slice_in_dim(q, start, Q_BLOCK, axis=1).reshape(B, Q_BLOCK, G, R, DSA_HEAD_DIM)
        s = jnp.einsum('bqgrd,bqkgd->bqgrk', qb, k_sel).astype(jnp.float32) * scale
        s = jnp.where(valid[:, :, None, None, :], s, -jnp.inf)
        pr = jax.nn.softmax(s, axis=-1).astype(v.dtype)
        o = jnp.einsum('bqgrk,bqkgd->bqgrd', pr, v_sel)
        return o.reshape(B, Q_BLOCK, DSA_HEADS, DSA_HEAD_DIM)

    return sweep_query_blocks(block, B, S)

def dsa_branch(h, pos, w_in, w_out):
    B, S, _ = h.shape
    q, k, v, qi, ki, wi, z = jnp.split(h @ w_in, DSA_SPLITS, axis=-1)
    q = rope(q.reshape(B, S, DSA_HEADS, DSA_HEAD_DIM), pos)
    k = rope(k.reshape(B, S, DSA_KV_HEADS, DSA_HEAD_DIM), pos)
    v = v.reshape(B, S, DSA_KV_HEADS, DSA_HEAD_DIM)
    qi = rope(qi.reshape(B, S, IDX_HEADS, IDX_DIM), pos)
    ki = rope(ki, pos)
    top_k = min(TOPK_MAX, S // 4)
    o = dsa_attention(q, k, v, qi, ki, wi, top_k).reshape(B, S, DSA_WIDTH)
    return (o * jax.nn.silu(z)) @ w_out

def setup_inputs(seed: int = 0) -> dict:
    key = jax.random.key(seed)
    ks = jax.random.split(key, 20)

    def w(k, shape, fan_in):
        return jax.random.normal(k, shape, jnp.float32) * (fan_in ** -0.5)

    def gain(k, shape):
        return 1.0 + 0.02 * jax.random.normal(k, shape, jnp.float32)

    x = jax.random.normal(ks[0], (BATCH, SEQ, D_MODEL), jnp.float32)
    p = jax.random.normal(ks[1], (DEPTH, BATCH, SEQ, PLE_DIM), jnp.float32)
    offset = jax.random.randint(ks[2], (BATCH, 1), 0, 1024, dtype=jnp.int32)
    positions = jnp.arange(SEQ, dtype=jnp.int32)[None, :] + offset
    return {
        "x": x,
        "p": p,
        "positions": positions,
        "norm_in": gain(ks[3], (DEPTH, D_MODEL)),
        "mla_w_in": w(ks[4], (N_MLA_LAYERS, D_MODEL, MLA_IN), D_MODEL),
        "mla_q_norm": gain(ks[5], (N_MLA_LAYERS, MLA_Q_RANK)),
        "mla_kv_norm": gain(ks[6], (N_MLA_LAYERS, MLA_KV_RANK)),
        "mla_w_uq": w(ks[7], (N_MLA_LAYERS, MLA_Q_RANK, MLA_HEADS * (MLA_NOPE_DIM + MLA_ROPE_DIM)), MLA_Q_RANK),
        "mla_w_uk": w(ks[8], (N_MLA_LAYERS, MLA_KV_RANK, MLA_HEADS, MLA_NOPE_DIM), MLA_KV_RANK),
        "mla_w_uv": w(ks[9], (N_MLA_LAYERS, MLA_KV_RANK, MLA_HEADS, MLA_V_DIM), MLA_KV_RANK),
        "mla_w_out": w(ks[10], (N_MLA_LAYERS, MLA_WIDTH, D_MODEL), MLA_WIDTH),
        "dsa_w_in": w(ks[11], (N_DSA_LAYERS, D_MODEL, DSA_IN), D_MODEL),
        "dsa_w_out": w(ks[12], (N_DSA_LAYERS, DSA_WIDTH, D_MODEL), DSA_WIDTH),
        "ple_w_proj": w(ks[13], (DEPTH, PLE_DIM, D_MODEL), PLE_DIM),
        "ple_norm": gain(ks[14], (DEPTH, D_MODEL)),
        "ple_w_gate": w(ks[15], (DEPTH, D_MODEL, D_MODEL), D_MODEL),
        "final_norm": gain(ks[16], (D_MODEL,)),
    }

def reference(x, p, positions, norm_in, mla_w_in, mla_q_norm, mla_kv_norm, mla_w_uq,
              mla_w_uk, mla_w_uv, mla_w_out, dsa_w_in, dsa_w_out, ple_w_proj,
              ple_norm, ple_w_gate, final_norm):
    for i in range(DEPTH):
        h = rmsnorm(x, norm_in[i])
        j = i // N_MIXERS
        if i % N_MIXERS == 0:
            y = mla_branch(h, positions, mla_w_in[j], mla_q_norm[j], mla_kv_norm[j],
                           mla_w_uq[j], mla_w_uk[j], mla_w_uv[j], mla_w_out[j])
        else:
            y = dsa_branch(h, positions, dsa_w_in[j], dsa_w_out[j])
        x = x + y
        gate = jax.nn.sigmoid(rmsnorm(x, ple_norm[i]) @ ple_w_gate[i])
        x = x + (p[i] @ ple_w_proj[i]) * gate
    return rmsnorm(x, final_norm)


_drawn_inputs = setup_inputs


def setup_inputs(seed=0):
    import zlib

    import numpy as np

    out = dict(_drawn_inputs(seed))
    spreads = {}
    factors = {'norm_in': 8.0,
     'mla_q_norm': 8.0,
     'mla_kv_norm': 8.0,
     'ple_norm': 78.048,
     'final_norm': 23.399}
    for name, (base, spread) in spreads.items():
        noise = np.random.default_rng([zlib.crc32(name.encode()), seed]).standard_normal(out[name].shape)
        drawn = base * np.exp(spread * noise) if base else spread * noise
        out[name] = __import__('jax').numpy.asarray(drawn.astype(out[name].dtype))
    for name, factor in factors.items():
        out[name] = (out[name] * factor).astype(out[name].dtype)
    return out
```

```python
from contextlib import ExitStack

import numpy as np
import concourse.bass as bass
from concourse import mybir

ALU = mybir.AluOpType
ACT = mybir.ActivationFunctionType
F32 = mybir.dt.float32
F32R = mybir.dt.float32r
U32 = mybir.dt.uint32
I32 = mybir.dt.int32
AX_X = mybir.AxisListType.X

P = 128
S = 1024
D = 1024
T = S // P
KD = D // P
CW = 512
HEADS = 8
RANK = 256
NOPE, ROPE_D, VDIM = 128, 64, 128
MLA_SCALE = float(np.float32((NOPE + ROPE_D) ** -0.5))
HD = 128
DSA_SCALE = float(np.float32(HD ** -0.5))
KV_HEADS = 2
GROUP = HEADS // KV_HEADS
IDX_HEADS, IDX_DIM = 8, 64
IDX_SCALE = float(IDX_DIM ** -0.5)
W_IDX_SCALE = float(np.float32(IDX_HEADS ** -0.5))
TOPK = 256
FULL = TOPK // P
PLE = 256
EPS = 1e-6
NEG = -3.0e38
HALF = HD // 2
NFREQ = HALF
SCORE_AT = [P * t * (t + 1) // 2 for t in range(T + 1)]
SPREAD = T - FULL
TWO_PI = 2 * np.pi
RAW_SLOTS = 3


def two_pi_parts():
    c1 = 6.28125
    bits = np.frombuffer(np.float32(TWO_PI - c1).tobytes(), np.uint32)[0] & 0xFFFFF000
    c2 = float(np.frombuffer(np.uint32(bits).tobytes(), np.float32)[0])
    return c1, c2, TWO_PI - c1 - c2


SEQ = {
    0: [("z", "mla_in", 576, CW, 0), ("z", "mla_in", 1088, CW, 1), ("kpe", "mla_in", 512, 64, 0),
        ("c", "mla_in", 0, CW, 1),
        ("wo", "out0", 0, CW, 1), ("wo", "out0", CW, CW, 0),
        ("gate", "gate0", 0, CW, 1), ("gate", "gate0", CW, CW, 0)],
    1: [("kiwi", "dsa_in", 2048, 72, 1), ("qi", "dsa_in", 1536, CW, 0), ("kv", "dsa_in", 1024, CW, 1),
        ("q", "dsa_in", 0, CW, 0), ("q", "dsa_in", CW, CW, 1),
        ("z", "dsa_in", 2120, CW, 0), ("z", "dsa_in", 2632, CW, 1),
        ("wo", "out1", 0, CW, 0), ("wo", "out1", CW, CW, 1),
        ("gate", "gate1", 0, CW, 0), ("gate", "gate1", CW, CW, 1)],
}
CHUNKS = [(lay, i) + c for lay in (0, 1) for i, c in enumerate(SEQ[lay])]
DMA_SEMS = (["raw_ld%d" % i for i in range(RAW_SLOTS)] + ["x_ld%d" % t for t in range(T)] +
            ["const_ld", "gain", "z_st0", "z_st1", "z_ld", "xin0", "xin1", "p_ld0", "p_ld1",
             "x2_st", "st0", "st1", "cs_st", "cs_ld", "t2_ld", "k0_ld", "out_st"])
PLAIN_SEMS = ["a_full", "b_full", "hi", "lo", "sq", "rstd", "xn", "w", "zs", "rot_in", "rot",
              "xadd", "sg", "pp", "relu", "sc", "nb", "ex", "ri", "pn", "og", "stage", "trig",
              "csq", "consts", "vcopy", "found", "widx", "pool_chain", "dve_chain", "act_chain", "fin", "pe_in"]


class Step:
    pass


def plan():
    steps, now = [], {n: 0 for n in DMA_SEMS + PLAIN_SEMS}
    bank_free = {b: [] for b in range(8)}
    ring_at = {"A": 0, "B": 0}
    read_by = {}
    granules = [0]

    def add(kind, incs=None, ring=None, jobs=0, freed=None, wide=False, **kw):
        s = Step()
        s.kind, s.before = kind, dict(now)
        for n, k in (incs or {}).items():
            now[n] += k * (16 if n in DMA_SEMS else 1)
        s.after = dict(now)
        s.n = dict(kw)
        s.banks, s.free = [], []
        for j in range(jobs):
            if wide:
                first = (ring_at["A"] + 1) // 2 * 2 % 4
                banks = [first, first + 1]
                ring_at["A"] = first + 2
            else:
                banks = [ring_at[ring] % 4 + (4 if ring == "B" else 0)]
                ring_at[ring] += 1
            need = {}
            for b in banks:
                for n, v in bank_free[b]:
                    need[n] = max(need.get(n, 0), v)
            s.banks.append(banks[0])
            s.free.append(sorted(need.items()))
            for b in banks:
                bank_free[b] = [(n, s.before[n] + j + 1) for n in freed]
        steps.append(s)
        return s

    def w(chunk, d):
        lay, i, name, src, c0, n, buf = chunk
        res = "ring%d" % buf
        g = granules[0]
        granules[0] += 1
        s = add("w", {"w": 1, "raw_ld%d" % (g % RAW_SLOTS): 1}, src=src, d=d, c0=c0, cols=n,
                buf=buf, g=g, reader=read_by.get(res) if d == 0 else None)
        w_after[(lay, i, d)] = s.after["w"]

    w_after = {}

    def small_w(kind, res, **kw):
        pieces = 2
        for k in range(pieces):
            g = granules[0]
            granules[0] += 1
            loads = 2 if kind == "head_w" and k == 1 else 1
            s = add(kind, {"w": 1, "raw_ld%d" % (g % RAW_SLOTS): loads}, piece=k, g=g, res=res,
                    reader=read_by.get(res) if k == 0 else None, **kw)
        return s.after["w"]

    lo_at = {}

    def norm_a(t, slot, ready, gain):
        return add("norm_a", {"sq": 1, "rstd": 1, "xn": 1}, t=t, slot=slot, ready=ready, gain=gain)

    def norm_b(t, slot, xn):
        s = add("norm_b", {"b_full": 2, "hi": 2, "lo": 2}, ring="B", jobs=2, freed=["lo"],
                t=t, slot=slot, xn=xn)
        lo_at[("act", t)] = s.after["lo"]

    def gain(which):
        return add("gain", {"gain": 2 if which == "latent" else 1}, which=which,
                   reader=read_by.get("G"))

    def split4(src, slot, ready, cols=CW, **kw):
        return add("split4", {"b_full": 1, "hi": 1, "lo": 1}, ring="B", jobs=1, freed=["lo"],
                   src=src, slot=slot, ready=ready, cols=cols, **kw)

    def chunk_of(lay, i):
        return next(c for c in CHUNKS if c[:2] == (lay, i))

    def next_chunk(lay, i):
        at = [c[:2] for c in CHUNKS].index((lay, i)) + 1
        return CHUNKS[at] if at < len(CHUNKS) else None

    def proj(lay, i, job, freed, incs, jobs_note=None, **kw):
        c = chunk_of(lay, i)
        feature = c[2] == "z"
        tiles = range(4 * (job // 4), 4 * (job // 4) + 4) if feature or c[2] in ("kpe", "kiwi") else [job]
        if c[2] in ("kpe", "kiwi"):
            tiles = range(4 * job, 4 * job + 4)
        allinc = {"a_full": 1}
        allinc.update(incs)
        s = add("proj", allinc, ring="A", jobs=1, freed=freed, lay=lay, chunk=i, name=c[2], cols=c[5],
                buf=c[6], job=job, tiles=list(tiles), w_ready=[w_after[(lay, i, d)] for d in range(KD)],
                act=max(lo_at[("act", t)] for t in tiles), **kw)
        read_by["ring%d" % c[6]] = ("a_full", s.after["a_full"])
        return s

    store_at = {"st0": 0, "st1": 0}

    add("start", {"const_ld": 2, "gain": 1, "consts": 1})
    for t in range(T):
        add("load_x", {"x_ld%d" % t: 1}, t=t)
        w(chunk_of(0, 0), t)
    xs = []
    for t in range(T):
        a = norm_a(t, t % 2, ("x_ld%d" % t, 16), now["gain"])
        xs.append(a)
        if t:
            norm_b(t - 1, (t - 1) % 2, xs[t - 1].after["xn"])
    norm_b(T - 1, 1, xs[-1].after["xn"])
    read_by["G"] = ("xn", now["xn"])
    latent_gain = gain("latent").after["gain"]

    def z_chunk(lay, i, base, slots, prefetch=True, extra=None):
        for job in range(8):
            if prefetch:
                w(next_chunk(lay, i), job)
            slot = job % 2
            s = proj(lay, i, job, ["zs"], {"zs": 1, "z_st%d" % slot: 1}, slot=slot, base=base)
            if extra:
                extra(8 * (base // CW) + job)

    z_chunk(0, 0, 0, 2)
    tb = add("tables", {"stage": 4, "trig": 2, "b_full": 2, "csq": 2, "cs_st": 1},
             ring="B", jobs=2, freed=["csq"])
    z_chunk(0, 1, CW, 2)
    def rope_job(lay, i, job, slot, extra_inc=None, freed=("rot_in",), chain=0, **kw):
        inc = {"rot_in": 1, "rot": 1}
        inc.update(extra_inc or {})
        return proj(lay, i, job, list(freed), inc, slot=slot, **kw)

    kp = []
    for job in range(2):
        for d in range(4):
            w(next_chunk(0, 2), 4 * job + d)
        kp.append(rope_job(0, 2, job, job, stages=0))
    for job in range(2):
        s = split4("p1", job, ("rot", kp[job].after["rot"]), dest="kpeT", j=job)
        lo_at["kpeT"] = s.after["lo"]
    head_w = {}
    prev = None
    for t in range(T):
        if t == 0:
            head_w[0] = small_w("head_w", "headW", h=0)
        s = proj(0, 3, t, ["xn"], {"sq": 2, "rstd": 1, "xn": 1}, slot=t % 2, gain=latent_gain)
        if prev:
            split4("p1", prev[0] % 2, ("xn", prev[1]), dest="cT", t=prev[0])
        prev = (t, s.after["xn"])
    s = split4("p1", prev[0] % 2, ("xn", prev[1]), dest="cT", t=prev[0])
    lo_at["cT"] = s.after["lo"]
    read_by["G"] = ("xn", now["xn"])

    att = {"n": 0}

    def s_step(lay, h, qb, q_ready):
        n = att["n"]
        att["n"] += 1
        incs = {"a_full": 1, "nb": 1, "ex": 1}
        s = add("S", incs, ring="A", jobs=1, freed=["ex" if lay == 0 else "nb"], wide=True,
                lay=lay, h=h, qb=qb, ps=n % 3, q_ready=q_ready)
        r = add("R", {"ri": 1, "pn": 1}, ps=n % 3, qb=qb, ex=s.after["ex"])
        return r.after["pn"]

    def t_step(lay, h, qb, pn, ps):
        jobs = qb // 4 + 1
        s = add("T", {"b_full": jobs, "hi": jobs, "lo": jobs}, ring="B", jobs=jobs, freed=["lo"],
                lay=lay, qb=qb, pn=pn, ps=ps)
        return s.after["lo"]

    def pv_step(lay, h, g, pt_ready, v_ready, z_ld):
        s = add("PV", {"b_full": 1, "og": 1}, ring="B", jobs=1, freed=["og"], lay=lay, h=h, g=g,
                ready=max(pt_ready, v_ready), z_ld=z_ld)
        read_by["G"] = ("og", s.after["og"])
        return s

    def hproj(h, part):
        names = ["q", "q", "pe", "pe", "k", "k"] if part == 0 else ["v", "v"]
        for j, name in enumerate(names):
            incs = {"b_full": 1, "hi": 1, "lo": 1}
            if name == "pe":
                incs["stage"] = 1
            s = add("hproj", incs, ring="B", jobs=1, freed=["lo"], h=h, name=name, j=j % 2,
                    w_ready=head_w[h], c_ready=lo_at["cT"], csq=tb.after["csq"])
        read_by["headW"] = ("b_full", s.after["b_full"])
        read_by["ring0"] = ("b_full", s.after["b_full"]) if part else read_by["ring0"]
        return s.after["lo"]

    def z_load(lay, h):
        s = add("z_load", {"z_ld": 1}, lay=lay, h=h, reader=read_by.get("G"),
                stored=(now["z_st0"], now["z_st1"]))
        return s.after["z_ld"]

    qk_ready = hproj(0, 0)
    v_ready = hproj(0, 1)
    for h in range(HEADS):
        zl = z_load(0, h)
        if h + 1 < HEADS:
            head_w[h + 1] = small_w("head_w", "headW", h=h + 1)
        pn, lo = {}, 0
        for qb in range(T):
            ps = att["n"] % 3
            pn[qb] = (s_step(0, h, qb, max(qk_ready, lo_at["kpeT"])), ps)
            if qb >= 2:
                lo = t_step(0, h, qb - 2, *pn[qb - 2])
            if qb == 5:
                pv_step(0, h, 0, lo, v_ready, zl)
        read_by["kpe"] = ("a_full", now["a_full"])
        if h:
            w(chunk_of(0, 4), h)
        if h == 1:
            w(chunk_of(0, 4), 0)
        if h + 1 < HEADS:
            qk_next = hproj(h + 1, 0)
        t_step(0, h, 6, *pn[6])
        lo = t_step(0, h, 7, *pn[7])
        pv_step(0, h, 1, lo, v_ready, zl)
        if h + 1 < HEADS:
            v_ready = hproj(h + 1, 1)
            qk_ready = qk_next

    def tail(lay, wo0, last_gain, pa_reader):
        g1 = gain("ple%d" % lay).after["gain"]
        rows_free = now["b_full"]
        ppw = {}
        for t in range(T):
            s = add("og_split", {"hi": 1, "lo": 1}, t=t, act_free=now["b_full"])
            lo_at[("act", t)] = s.after["lo"]
        n = [0]

        def xin(t, j):
            return add("xin", {"xin%d" % (n[0] % 2): 1}, lay=lay, t=t, j=j, slot=n[0] % 2,
                       wait_add=(now["xadd"] - 1) if n[0] >= 2 else None, rows_free=rows_free,
                       x2=now["x2_st"])
        for j in range(2):
            prev, held = None, None
            for t in range(T):
                w(next_chunk(lay, wo0 + j), t)
                if j == 0 and t == 0:
                    ppw[0] = small_w("ple_w", "headW", lay=lay, j=0)
                if j == 0 and t == 2:
                    ppw[1] = small_w("ple_w", "kpe", lay=lay, j=1)
                x = xin(t, j)
                slot = n[0] % 2
                n[0] += 1
                s = proj(lay, wo0 + j, t, ["xadd"], {"xadd": 1}, slot=slot, xin=x.after["xin%d" % slot], j=j)
                if j == 1:
                    if prev:
                        norm_b(prev[0], 0, prev[1])
                    a = norm_a(t, 0, ("xadd", s.after["xadd"]), g1)
                    prev = (t, a.after["xn"])
        norm_b(prev[0], 0, prev[1])
        read_by["G"] = ("xn", now["xn"])
        g2 = gain(last_gain).after["gain"]
        gj = wo0 + 2
        n = 0
        read_by["pst0"], read_by["pst1"] = pa_reader, pa_reader
        for j in range(2):
            prev = None
            for t in range(T):
                if next_chunk(lay, gj + j):
                    w(next_chunk(lay, gj + j), t)
                pslot = n % 2
                pt = add("p_split", {"p_ld%d" % pslot: 1, "b_full": 1, "hi": 1, "lo": 1}, ring="B", jobs=1,
                         freed=["lo"], lay=lay, t=t, slot=pslot, reader=read_by["pst%d" % pslot])
                read_by["pst%d" % pslot] = ("b_full", pt.after["b_full"])
                s = proj(lay, gj + j, t, ["sg"], {"sg": 1}, slot=n % 2, j=j,
                         wait_add=now["xadd"] - 1)
                q = add("pp", {"b_full": 1, "pp": 1, "xadd": 1}, ring="B", jobs=1, freed=["pp"],
                        t=t, j=j, slot=n % 2, ready=max(pt.after["lo"], 0), w_ready=ppw[j], sg=s.after["sg"])
                read_by["headW" if j == 0 else "kpe"] = ("b_full", q.after["b_full"])
                n += 1
                if j == 1 and lay == 0:
                    if prev:
                        norm_b(prev[0], 0, prev[1])
                    add("save_x", {"x2_st": 1}, t=t, ready=q.after["xadd"])
                    a = norm_a(t, 0, ("xadd", q.after["xadd"]), g2)
                    prev = (t, a.after["xn"])
                if j == 1 and lay == 1:
                    add("final", {"sq": 1, "rstd": 1, "fin": 1, "out_st": 1}, t=t,
                        ready=q.after["xadd"], gain=g2)
            if j == 1 and lay == 0:
                norm_b(prev[0], 0, prev[1])
        read_by["G"] = ("xn", now["xn"])

    cs = add("cs_load", {"cs_ld": 1}, pn=now["b_full"])
    tail(0, 4, "in1", ("lo", now["lo"]))

    kp = []
    for job in range(2):
        for d in range(4):
            w(next_chunk(1, 0), 4 * job + d)
        kp.append(rope_job(1, 0, job, job, extra_inc={"widx": 1}, freed=("rot_in", "widx"), cs=cs.after["cs_ld"],
                           wait_add=now["xadd"]))
    for job in range(2):
        s = split4("p1", job, ("rot", kp[job].after["rot"]), dest="kpeT", j=job)
        lo_at["kiT"] = s.after["lo"]

    def idx_scores(t, q_ready):
        keys = (t + 1) * P
        for h in range(IDX_HEADS):
            for c in range((keys + CW - 1) // CW):
                n = min(CW, keys - c * CW)
                s = add("idx", {"b_full": 1, "relu": 1, "sc": 1}, ring="B", jobs=1, freed=["relu"],
                        t=t, h=h, c=c, n=n, q_ready=max(q_ready, lo_at["kiT"]), k=idx_n[0], x2=now["x2_st"],
                        gfree=read_by["G"])
                idx_n[0] += 1
        add("idx_mask", None, t=t)
    idx_n = [0]
    prev = None
    for t in range(T):
        w(next_chunk(1, 1), t)
        if t < FULL:
            continue
        s = rope_job(1, 1, t, t % 2)
        if prev:
            x = split4("p1", prev[0] % 2, ("rot", prev[1]), dest="qiT", slot2=prev[0] % 2)
            idx_scores(prev[0], x.after["lo"])
        prev = (t, s.after["rot"])
    x = split4("p1", prev[0] % 2, ("rot", prev[1]), dest="qiT", slot2=prev[0] % 2)
    idx_scores(prev[0], x.after["lo"])
    read_by["G"] = ("sc", now["sc"])

    bits = [31 - i for i in range(32)]

    def search():
        if bits:
            add("bit", None, bit=bits.pop(0))

    n = 0
    for i, name in ((2, "kv"), (3, "q"), (4, "q")):
        for t in range(T):
            w(next_chunk(1, i), t)
            slot = n % 2
            inc = {"st%d" % slot: 1}
            if name == "kv":
                inc["vcopy"] = 1
            rope_job(1, i, t, slot, extra_inc=inc, freed=("rot_in", "vcopy") if name == "kv" else ("rot_in",),
                     base=(i - 3) * CW, st_before=now["st%d" % slot])
            n += 1
            if n % 4:
                search()
    q_stored = (now["st0"], now["st1"])

    def t2_load(what, i, reader):
        return add("t2_load", {"t2_ld": 1}, what=what, i=i, reader=reader, stored=q_stored).after["t2_ld"]

    def q_prep(h, ld):
        s = None
        for j in range(2):
            s = split4("t2", 0, ("t2_ld", ld), dest="qT", slot2=h % 2, j=j)
        return s.after["lo"], ("b_full", s.after["b_full"])

    sel_done = []

    def z_extra(k):
        for _ in range(2):
            search()
        if not bits and len(sel_done) < SPREAD + 1 and k >= 8:
            if not sel_done:
                add("above", None)
                sel_done.append(-1)
            else:
                for _ in range(1):
                    if len(sel_done) <= SPREAD:
                        add("sel", {"found": 1}, t=FULL + len(sel_done) - 1)
                        sel_done.append(0)
    ld = t2_load("q", 0, ("b_full", now["b_full"]))
    k0 = add("k0_load", {"k0_ld": 1}, stored=q_stored)
    q_ready, rd = q_prep(0, ld)
    v0_ld = t2_load("v", 0, rd)
    wz = add("z_wait", {}, rot=now["rot"])
    z_chunk(1, 5, 0, 2, extra=z_extra)
    z_chunk(1, 6, CW, 2, prefetch=False, extra=z_extra)
    while len(sel_done) <= SPREAD:
        z_extra(99)
    read_by["G"] = ("found", now["found"])
    act_free = now["a_full"]
    k_ready, v_ready = {}, {}
    for j in range(2):
        k_ready[0] = split4("p1", 0, ("k0_ld", k0.after["k0_ld"]), dest="kT", g=0, j=j, whole=True).after["lo"]

    def v_prep(g, ld, act_free):
        s = add("v_split", {"hi": 1, "lo": 1}, g=g, ld=ld, act_free=act_free)
        v_ready[g] = s.after["lo"]
        return ("lo", s.after["lo"])
    rd = v_prep(0, v0_ld, act_free)

    waiting = []

    def finish(limit):
        while len(waiting) > limit:
            hh, qq, pn, ps = waiting.pop(0)
            lo = t_step(1, hh, qq, pn, ps)
            if qq % 4 == 3:
                pv_step(1, hh, qq // 4, lo, v_ready[hh // GROUP], zl[hh])
                if qq == 7 and hh + 1 < HEADS:
                    zl[hh + 1] = z_load(1, hh + 1)
    zl = {0: z_load(1, 0)}
    q_at = {0: q_ready}
    last_mask = None
    for h in range(HEADS):
        if h + 1 < HEADS:
            ld = t2_load("q", h + 1, rd)
        for qb in range(T):
            if h == 0:
                for t in ([0, 1, 2] if qb == 0 else [qb + 2] if qb + 2 < T else []):
                    add("mask", None, t=t, a_full=act_free)
            ps = att["n"] % 3
            pn = s_step(1, h, qb, max(q_at[h], k_ready[h // GROUP]))
            waiting.append((h, qb, pn, ps))
            finish(2)
            if qb == 3 and h + 1 < HEADS:
                q_at[h + 1], rd = q_prep(h + 1, ld)
                if h in (0, 1):
                    ld2 = t2_load("kv"[h], 1, rd)
            if qb == 6 and h == 0:
                for j in range(2):
                    s = split4("t2", 0, ("t2_ld", ld2), dest="kT", g=1, j=j)
                k_ready[1] = s.after["lo"]
                rd = ("b_full", s.after["b_full"])
            if qb == 6 and h == 1:
                rd = v_prep(1, ld2, act_free)
        w(chunk_of(1, 7), h)
    read_by["ring1"] = ("nb", now["nb"])
    read_by["headW"] = read_by["kpe"] = ("a_full", now["a_full"])
    finish(0)
    tail(1, 7, "final", ("lo", now["lo"]))
    return steps, now


def build(nc, x, p, positions, norm_in, w_in0, q_norm, kv_norm, w_uq, w_uk, w_uv, w_out0, w_in1, w_out1,
          ple_proj, ple_norm, ple_gate, final_norm, freqs, out):
    steps, total = plan()
    weights = {"mla_in": w_in0, "dsa_in": w_in1, "out0": w_out0, "out1": w_out1,
               "gate0": ple_gate[0], "gate1": ple_gate[1]}
    gains = {"in0": norm_in[0:1, :], "in1": norm_in[1:2, :], "ple0": ple_norm[0:1, :], "ple1": ple_norm[1:2, :],
             "final": final_norm}

    with ExitStack() as ctx:
        def sb(name, cols, dt=F32):
            return ctx.enter_context(nc.sbuf_tensor(name, [P, cols], dt))

        act = [sb("act_hi", KD * S, F32R), sb("act_lo", KD * S, F32R)]
        ring = [sb("ring_hi", 2 * KD * CW, F32R), sb("ring_lo", 2 * KD * CW, F32R)]
        kpe = [sb("kpe_hi", S, F32R), sb("kpe_lo", S, F32R)]
        head_w = [sb("head_w_hi", 1024, F32R), sb("head_w_lo", 1024, F32R)]
        p_t = [sb("p_t_hi", PLE, F32R), sb("p_t_lo", PLE, F32R)]
        ident_r = sb("ident_r", P, F32R)
        tri_r = sb("tri_r", P, F32R)
        xr = sb("xr", T * D)
        raw = sb("raw", RAW_SLOTS * CW)
        p0 = sb("p0", 1024)
        p1 = sb("p1", 1024)
        cs = sb("cs", 1024)
        t2 = sb("t2", 1024)
        gz = sb("gz", 1024)
        ident = sb("ident", P)
        tri = sb("tri", P)
        small = sb("small", 128)
        pos_i = sb("pos_i", T, I32)
        frq = sb("frq", NFREQ)
        wis = sb("wis", T * IDX_HEADS)
        bits_u = sb("bits_u", 4 * SPREAD, U32)
        psum = ctx.enter_context(nc.psum_tensor("psum", [P, 8 * CW], F32))

        sem = {n: ctx.enter_context(nc.semaphore(n)) for n in DMA_SEMS + PLAIN_SEMS}
        z_dram = [nc.dram_tensor("z_scratch%d" % l, [D, S], F32, kind="Internal").ap() for l in range(2)]
        x2_dram = nc.dram_tensor("x2_scratch", [S, D], F32, kind="Internal").ap()
        q_dram = nc.dram_tensor("q_scratch", [S, D], F32, kind="Internal").ap()
        kv_dram = nc.dram_tensor("kv_scratch", [S, CW], F32, kind="Internal").ap()
        cs_dram = nc.dram_tensor("cs_scratch", [P, 1024], F32, kind="Internal").ap()

        ms = small[:, 0:8]
        mean = small[:, 8:16]
        rs = small[:, 16:24]
        lat_ms, lat_mean, lat_rs = small[:, 24:28], small[:, 28:32], small[:, 32:36]
        minus_half = small[:, 36:38]
        posf = small[:, 40:48]
        mx, nb, sm, ri = small[:, 48:51], small[:, 51:54], small[:, 54:57], small[:, 57:60]
        cnt = small[:, 64:64 + SPREAD]
        need = small[:, 72:72 + SPREAD]
        junk1 = small[:, 80:88]
        u_bits, u_mask, u_cand, u_inc = (bits_u[:, k * SPREAD:(k + 1) * SPREAD] for k in range(4))
        rows = [p0, p1, cs]

        def bank(b, n=CW):
            return psum[:, b * CW:b * CW + n]

        def act_tile(part, t):
            return act[part][:].rearrange("p (d s) -> p d s", s=S)[:, :, t * P:(t + 1) * P]

        def act_at(part, d, c0, n):
            return act[part][:, d * S + c0:d * S + c0 + n]

        def w_at(part, buf, d, c0, n):
            at = (buf * KD + d) * CW + c0
            return ring[part][:, at:at + n]

        PT0, V0, Q0, K0, PE0 = 0, 4096, 5120, 6144, 7168
        def pt_at(part, kt, c0, n):
            return act[part][:, PT0 + kt * CW + c0:PT0 + kt * CW + c0 + n]
        def region(part, at, c0, n):
            return act[part][:, at + c0:at + c0 + n]
        def kT1(part, g, c0, n):
            return act[part][:, 4096 + g * 1024 + c0:4096 + g * 1024 + c0 + n]
        def v1(part, g, c0, n):
            return act[part][:, 6144 + g * 1024 + c0:6144 + g * 1024 + c0 + n]
        def qT1(part, slot, c0, n):
            return (kpe, head_w)[slot][part][:, c0:c0 + n]
        def mask_at(t):
            if t < T - 1:
                return ring[0][:, KD * CW + SCORE_AT[t]:KD * CW + SCORE_AT[t + 1]]
            return ring[1][:, KD * CW:KD * CW + S]
        def score_at(t, c0=0, n=None):
            n = (t + 1) * P - c0 if n is None else n
            return xr[:, SCORE_AT[t] + c0:SCORE_AT[t] + c0 + n]

        def small_dest(s, part):
            k = s.n["piece"]
            w = head_w[part]
            if s.kind == "ple_w":
                return [((head_w if s.n["res"] == "headW" else kpe)[part][:, k * CW:(k + 1) * CW], 0, CW)]
            if k == 0:
                pairs = []
                for r in range(2):
                    pairs += [(w[:, r * 256:r * 256 + 192], r * 192, 192),
                              (w[:, r * 256 + 192:r * 256 + 224], r * 192 + 160, 32),
                              (w[:, r * 256 + 224:r * 256 + 256], r * 192 + 128, 32)]
                return pairs
            return [(w[:, 512:1024], 0, 512)]

        def split_dest(s, part):
            dest = s.n["dest"]
            if dest == "kpeT":
                ap = kpe[part][:, s.n["j"] * CW:(s.n["j"] + 1) * CW]
            elif dest == "cT":
                t = s.n["t"]
                return ring[part][:, 0:4 * S].rearrange("p (f s) -> p f s", s=S)[:, :, t * P:(t + 1) * P]
            elif dest == "qiT":
                ap = head_w[part][:, s.n["slot2"] * CW:(s.n["slot2"] + 1) * CW]
            elif dest == "qT":
                ap = qT1(part, s.n["slot2"], s.n["j"] * CW, CW)
            else:
                ap = kT1(part, s.n["g"], s.n["j"] * CW, CW)
            return ap.rearrange("p (a b) -> p a b", b=P)

        def in4(ap):
            return ap.rearrange("p (a b) -> p a b", b=P)

        block = ctx.enter_context(nc.Block())

        @block.sync
        def _(sp):
            for s in steps:
                k, n = s.kind, s.n
                if k == "start":
                    sp.dma_start(frq[:], freqs.partition_broadcast(P)).then_inc(sem["const_ld"], 16)
                    sp.dma_start(pos_i[:], positions.rearrange("b (t p) -> p (b t)", p=P),
                                 allow_slow_non_contiguous=True).then_inc(sem["const_ld"], 16)
                    sp.dma_start(gz[:], gains["in0"].partition_broadcast(P)).then_inc(sem["gain"], 16)
                elif k == "load_x":
                    t = n["t"]
                    sp.dma_start(xr[:, t * D:(t + 1) * D], x[t * P:(t + 1) * P, :]).then_inc(sem["x_ld%d" % t], 16)
                elif k in ("w", "head_w", "ple_w"):
                    slot = n["g"] % RAW_SLOTS
                    if n["g"] >= RAW_SLOTS:
                        sp.wait_ge(sem["w"], n["g"] - RAW_SLOTS + 1)
                    dst = raw[:, slot * CW:(slot + 1) * CW]
                    ld = sem["raw_ld%d" % slot]
                    if k == "w":
                        d = n["d"]
                        sp.dma_start(dst[:, 0:n["cols"]],
                                     weights[n["src"]][d * P:(d + 1) * P, n["c0"]:n["c0"] + n["cols"]]).then_inc(ld, 16)
                    elif k == "ple_w":
                        r, j = n["piece"], n["j"]
                        sp.dma_start(dst, ple_proj[n["lay"], r * P:(r + 1) * P, j * CW:(j + 1) * CW]).then_inc(ld, 16)
                    elif n["piece"] == 0:
                        h = n["h"]
                        sp.dma_start(dst[:, 0:384].rearrange("p (r c) -> p r c", r=2),
                                     w_uq.rearrange("(r p) c -> p r c", p=P)[:, :, h * 192:(h + 1) * 192]).then_inc(ld, 16)
                    else:
                        h = n["h"]
                        sp.dma_start(dst.rearrange("p (q r c) -> p q r c", q=2, r=2)[:, 0],
                                     w_uk.rearrange("(r p) c -> p r c", p=P)[:, :, h * P:(h + 1) * P]).then_inc(ld, 16)
                        sp.dma_start(dst.rearrange("p (q r c) -> p q r c", q=2, r=2)[:, 1],
                                     w_uv.rearrange("(r p) c -> p r c", p=P)[:, :, h * P:(h + 1) * P]).then_inc(ld, 16)
                elif k == "gain":
                    sp.wait_ge(sem[n["reader"][0]], n["reader"][1])
                    if n["which"] == "latent":
                        sp.dma_start(gz[:, 0:RANK], q_norm.partition_broadcast(P)).then_inc(sem["gain"], 16)
                        sp.dma_start(gz[:, RANK:2 * RANK], kv_norm.partition_broadcast(P)).then_inc(sem["gain"], 16)
                    else:
                        sp.dma_start(gz[:], gains[n["which"]].partition_broadcast(P)).then_inc(sem["gain"], 16)
                elif k == "tables":
                    sp.wait_ge(sem["trig"], s.after["trig"])
                    sp.dma_start(cs_dram, cs[:]).then_inc(sem["cs_st"], 16)
                elif k == "cs_load":
                    sp.wait_ge(sem["b_full"], n["pn"])
                    sp.wait_ge(sem["cs_st"], 16)
                    sp.dma_start(cs[:], cs_dram).then_inc(sem["cs_ld"], 16)
                elif k == "proj" and n["name"] == "z":
                    sp.wait_ge(sem["zs"], s.after["zs"])
                    f = n["base"] + (n["job"] % 4) * P
                    half = n["job"] // 4
                    sp.dma_start(z_dram[n["lay"]][f:f + P, half * CW:(half + 1) * CW],
                                 p0[:, n["slot"] * CW:(n["slot"] + 1) * CW]).then_inc(sem["z_st%d" % n["slot"]], 16)
                elif k == "proj" and n["name"] in ("q", "kv"):
                    sp.wait_ge(sem["rot"], s.after["rot"])
                    if n["name"] == "kv":
                        sp.wait_ge(sem["vcopy"], s.after["vcopy"])
                    t = n["job"]
                    dst = (kv_dram[t * P:(t + 1) * P, :] if n["name"] == "kv"
                           else q_dram[t * P:(t + 1) * P, n["base"]:n["base"] + CW])
                    sp.dma_start(dst, p1[:, n["slot"] * CW:(n["slot"] + 1) * CW]).then_inc(sem["st%d" % n["slot"]], 16)
                elif k == "z_load":
                    sp.wait_ge(sem[n["reader"][0]], n["reader"][1])
                    sp.wait_ge(sem["z_st0"], n["stored"][0])
                    sp.wait_ge(sem["z_st1"], n["stored"][1])
                    h = n["h"]
                    sp.dma_start(gz[:], z_dram[n["lay"]][h * P:(h + 1) * P, :]).then_inc(sem["z_ld"], 16)
                elif k == "xin":
                    sp.wait_ge(sem["b_full"], n["rows_free"])
                    if n["wait_add"] is not None:
                        sp.wait_ge(sem["xadd"], n["wait_add"])
                    if n["lay"] == 1:
                        sp.wait_ge(sem["x2_st"], n["x2"])
                    t, j = n["t"], n["j"]
                    src = x if n["lay"] == 0 else x2_dram
                    sp.dma_start(p1[:, n["slot"] * CW:(n["slot"] + 1) * CW],
                                 src[t * P:(t + 1) * P, j * CW:(j + 1) * CW]).then_inc(sem["xin%d" % n["slot"]], 16)
                elif k == "p_split":
                    sp.wait_ge(sem[n["reader"][0]], n["reader"][1])
                    t = n["t"]
                    sp.dma_start(t2[:, n["slot"] * PLE:(n["slot"] + 1) * PLE],
                                 p[n["lay"], t * P:(t + 1) * P, :]).then_inc(sem["p_ld%d" % n["slot"]], 16)
                elif k == "save_x":
                    sp.wait_ge(sem["xadd"], n["ready"])
                    t = n["t"]
                    sp.dma_start(x2_dram[t * P:(t + 1) * P, :], xr[:, t * D:(t + 1) * D]).then_inc(sem["x2_st"], 16)
                elif k == "t2_load":
                    sp.wait_ge(sem[n["reader"][0]], n["reader"][1])
                    sp.wait_ge(sem["st0"], n["stored"][0])
                    sp.wait_ge(sem["st1"], n["stored"][1])
                    i = n["i"]
                    src = {"q": q_dram[:, i * P:(i + 1) * P] if n["what"] == "q" else None,
                           "k": kv_dram[:, (i % 2) * P:(i % 2) * P + P],
                           "v": kv_dram[:, 256 + (i % 2) * P:256 + (i % 2) * P + P]}[n["what"]]
                    sp.dma_start(t2[:].rearrange("p (t c) -> p t c", c=P),
                                 src.rearrange("(t p) c -> p t c", p=P)).then_inc(sem["t2_ld"], 16)
                elif k == "k0_load":
                    sp.wait_ge(sem["st0"], n["stored"][0])
                    sp.wait_ge(sem["st1"], n["stored"][1])
                    sp.dma_start(p1[:].rearrange("p (t c) -> p t c", c=P),
                                 kv_dram[:, 0:P].rearrange("(t p) c -> p t c", p=P)).then_inc(sem["k0_ld"], 16)
                elif k == "final":
                    sp.wait_ge(sem["fin"], s.after["fin"])
                    t = n["t"]
                    sp.dma_start(out[t * P:(t + 1) * P, :], xr[:, t * D:(t + 1) * D]).then_inc(sem["out_st"], 16)
            sp.wait_ge(sem["out_st"], total["out_st"])

        @block.gpsimd
        def _(pool):
            chain = [0]

            def linked(ins):
                chain[0] += 1
                ins.then_inc(sem["pool_chain"], 1)
                pool.wait_ge(sem["pool_chain"], chain[0])

            for s in steps:
                k, n = s.kind, s.n
                if k == "start":
                    linked(nc.gpsimd.memset(ident[:], 0.0))
                    linked(nc.gpsimd.affine_select(out=ident[:], in_=ident[:], compare_op=ALU.not_equal, fill=1.0,
                                                   base=0, pattern=[[-1, P]], channel_multiplier=1))
                    linked(nc.gpsimd.memset(tri[:], 0.0))
                    linked(nc.gpsimd.affine_select(out=tri[:], in_=tri[:], compare_op=ALU.is_ge, fill=NEG,
                                                   base=0, pattern=[[-1, P]], channel_multiplier=1))
                    linked(nc.gpsimd.tensor_copy(ident_r[:], ident[:]))
                    linked(nc.gpsimd.tensor_copy(tri_r[:], tri[:]))
                    nc.gpsimd.memset(minus_half, -0.5).then_inc(sem["consts"], 1)
                    pool.wait_ge(sem["consts"], 1)
                elif k in ("w", "head_w", "ple_w"):
                    slot = n["g"] % RAW_SLOTS
                    pool.wait_ge(sem["raw_ld%d" % slot], s.after["raw_ld%d" % slot])
                    if n["reader"]:
                        pool.wait_ge(sem[n["reader"][0]], n["reader"][1])
                    src = raw[:, slot * CW:(slot + 1) * CW]
                    if k == "w":
                        pairs = [[(w_at(part, n["buf"], n["d"], 0, n["cols"]), 0, n["cols"])] for part in range(2)]
                    else:
                        pairs = [small_dest(s, part) for part in range(2)]
                    for dst, c0, cols in pairs[0]:
                        last = nc.gpsimd.tensor_copy(dst, src[:, c0:c0 + cols])
                    linked(last)
                    for (dst, c0, cols), (hi, _, _) in zip(pairs[1], pairs[0]):
                        last = nc.gpsimd.tensor_tensor(dst, src[:, c0:c0 + cols], hi.bitcast(F32), ALU.subtract)
                    last.then_inc(sem["w"], 1)
                elif k in ("norm_a", "final"):
                    t = n["t"]
                    pool.wait_ge(sem["sq"], s.after["sq"])
                    linked(nc.gpsimd.tensor_scalar(mean[:, t:t + 1], ms[:, t:t + 1], 1.0 / D, EPS, ALU.mult, ALU.add))
                    nc.gpsimd.tensor_tensor(rs[:, t:t + 1], mean[:, t:t + 1], minus_half[:, 0:1],
                                            ALU.pow).then_inc(sem["rstd"], 1)
                elif k == "proj" and n["name"] == "c":
                    c = 2 * n["slot"]
                    pool.wait_ge(sem["sq"], s.after["sq"])
                    linked(nc.gpsimd.tensor_scalar(lat_mean[:, c:c + 2], lat_ms[:, c:c + 2], 1.0 / RANK, EPS,
                                                   ALU.mult, ALU.add))
                    nc.gpsimd.tensor_tensor(lat_rs[:, c:c + 2], lat_mean[:, c:c + 2], minus_half,
                                            ALU.pow).then_inc(sem["rstd"], 1)

        @block.scalar
        def _(act_e):
            def split_hi(s, j, dst, src):
                act_e.wait_ge(sem["b_full"], s.before["b_full"] + j + 1)
                nc.scalar.activation(dst, src, ACT.Copy).then_inc(sem["hi"], 1)

            for s in steps:
                k, n = s.kind, s.n
                if k in ("norm_a", "final"):
                    t = n["t"]
                    act_e.wait_ge(sem[n["ready"][0]] if k == "norm_a" else sem["xadd"],
                                  n["ready"][1] if k == "norm_a" else n["ready"])
                    dst = rows[n["slot"] if k == "norm_a" else 0]
                    nc.scalar.activation(dst[:], xr[:, t * D:(t + 1) * D], ACT.Square,
                                         accum_out=ms[:, t:t + 1]).then_inc(sem["sq"], 1)
                elif k == "norm_b":
                    t = n["t"]
                    for j in range(2):
                        split_hi(s, j, act_tile(0, t)[:, 4 * j:4 * j + 4, :], in4(bank(s.banks[j])))
                elif k == "split4":
                    split_hi(s, 0, split_dest(s, 0), in4(bank(s.banks[0])))
                elif k == "tables":
                    for i in range(2):
                        act_e.wait_ge(sem["stage"], s.before["stage"] + i + 1)
                        nc.scalar.activation(cs[:, (1 - i) * CW:(2 - i) * CW], p1[:, i * CW:(i + 1) * CW],
                                             ACT.Sin).then_inc(sem["trig"], 1)
                    for j in range(2):
                        act_e.wait_ge(sem["b_full"], s.before["b_full"] + j + 1)
                        nc.scalar.activation(t2[:, j * CW:(j + 1) * CW], bank(s.banks[j]), ACT.Copy).then_inc(sem["csq"], 1)
                elif k == "z_wait":
                    act_e.wait_ge(sem["rot"], n["rot"])
                elif k == "proj":
                    name, b = n["name"], s.banks[0]
                    if name == "z":
                        slot = n["slot"]
                        act_e.wait_ge(sem["a_full"], s.after["a_full"])
                        if s.before["z_st%d" % slot]:
                            act_e.wait_ge(sem["z_st%d" % slot], s.before["z_st%d" % slot])
                        nc.scalar.activation(p0[:, slot * CW:(slot + 1) * CW], bank(b), ACT.Silu).then_inc(sem["zs"], 1)
                    elif name == "c":
                        act_e.wait_ge(sem["a_full"], s.after["a_full"])
                        for r in range(2):
                            c = n["slot"] * CW + r * RANK
                            nc.scalar.activation(p1[:, c:c + RANK], bank(b)[:, r * RANK:(r + 1) * RANK], ACT.Square,
                                                 accum_out=lat_ms[:, 2 * n["slot"] + r:2 * n["slot"] + r + 1]).then_inc(sem["sq"], 1)
                    elif name == "gate":
                        act_e.wait_ge(sem["a_full"], s.after["a_full"])
                        act_e.wait_ge(sem["xadd"], n["wait_add"])
                        nc.scalar.activation(p1[:, n["slot"] * CW:(n["slot"] + 1) * CW], bank(b),
                                             ACT.Sigmoid).then_inc(sem["sg"], 1)
                    elif name == "kv":
                        act_e.wait_ge(sem["a_full"], s.after["a_full"])
                        if n["st_before"]:
                            act_e.wait_ge(sem["st%d" % n["slot"]], n["st_before"])
                        c = n["slot"] * CW + 256
                        nc.scalar.activation(p1[:, c:c + 256], bank(b)[:, 256:512], ACT.Copy).then_inc(sem["vcopy"], 1)
                elif k == "p_split":
                    split_hi(s, 0, p_t[0][:], bank(s.banks[0], PLE))
                elif k == "hproj":
                    b, j, name = s.banks[0], n["j"], n["name"]
                    if name == "pe":
                        act_e.wait_ge(sem["stage"], s.after["stage"])
                    at = {"q": Q0, "pe": PE0, "k": K0, "v": V0}[name]
                    split_hi(s, 0, region(0, at, j * CW, CW), bank(b))
                elif k == "idx":
                    slot = n["k"] % 2
                    act_e.wait_ge(sem["b_full"], s.after["b_full"])
                    if n["k"] >= 2:
                        act_e.wait_ge(sem["sc"], s.before["sc"] - 1)
                    else:
                        act_e.wait_ge(sem[n["gfree"][0]], n["gfree"][1])
                    nc.scalar.activation(gz[:, slot * CW:slot * CW + n["n"]], bank(s.banks[0], n["n"]), ACT.Relu,
                                         scale=IDX_SCALE).then_inc(sem["relu"], 1)
                elif k == "S":
                    ps, keys = n["ps"], (n["qb"] + 1) * P
                    src = bank(s.banks[0], keys) if n["lay"] == 0 else rows[ps][:, 0:keys]
                    act_e.wait_ge(sem["nb"], s.after["nb"])
                    if n["lay"] == 0 and ps == 2:
                        act_e.wait_ge(sem["cs_st"], 16)
                    nc.scalar.activation(rows[ps][:, 0:keys], src, ACT.Exp, bias=nb[:, ps:ps + 1],
                                         scale=MLA_SCALE if n["lay"] == 0 else DSA_SCALE,
                                         accum_out=sm[:, ps:ps + 1]).then_inc(sem["ex"], 1)
                elif k == "R":
                    ps, keys = n["ps"], (n["qb"] + 1) * P
                    act_e.wait_ge(sem["ri"], s.after["ri"])
                    nc.scalar.activation(rows[ps][:, 0:keys], rows[ps][:, 0:keys], ACT.Copy,
                                         scale=ri[:, ps:ps + 1]).then_inc(sem["pn"], 1)
                elif k == "T":
                    for j, b in enumerate(s.banks):
                        kts = min(4, n["qb"] + 1 - 4 * j)
                        dst = act[0][:, 0:8 * CW].rearrange("p (k c) -> p k c", c=CW)[
                            :, 4 * j:4 * j + kts, (n["qb"] % 4) * P:(n["qb"] % 4 + 1) * P]
                        split_hi(s, j, dst, in4(bank(b, kts * P)))
                elif k == "og_split":
                    t = n["t"]
                    act_e.wait_ge(sem["og"], s.after["og"])
                    act_e.wait_ge(sem["b_full"], n["act_free"])
                    nc.scalar.activation(act_tile(0, t), in4(xr[:, t * D:(t + 1) * D]), ACT.Copy).then_inc(sem["hi"], 1)
                elif k == "v_split":
                    act_e.wait_ge(sem["t2_ld"], n["ld"])
                    act_e.wait_ge(sem["a_full"], n["act_free"])
                    nc.scalar.activation(v1(0, n["g"], 0, S), t2[:], ACT.Copy).then_inc(sem["hi"], 1)

        @block.vector
        def _(dve):
            chain = [0]

            def linked(ins):
                chain[0] += 1
                ins.then_inc(sem["dve_chain"], 1)
                dve.wait_ge(sem["dve_chain"], chain[0])

            def split_lo(s, j, dst, src, hi):
                dve.wait_ge(sem["hi"], s.before["hi"] + j + 1)
                nc.vector.tensor_tensor(dst, src, hi.bitcast(F32), ALU.subtract).then_inc(sem["lo"], 1)

            def rotate(s, src, groups, half, c_ap, s_ap, dsts):
                pa = p0[:, 0:2 * groups * half].rearrange("p (g u e) -> p g u e", u=2, e=half)
                pb = p0[:, CW:CW + 2 * groups * half].rearrange("p (g u e) -> p g u e", u=2, e=half)
                if s.before["rot"]:
                    dve.wait_ge(sem["rot"], s.before["rot"])
                nc.vector.tensor_tensor(pa, src, c_ap, ALU.mult)
                nc.vector.tensor_tensor(pb, src, s_ap, ALU.mult).then_inc(sem["rot_in"], 1)
                dve.wait_ge(sem["rot_in"], s.after["rot_in"])
                for dst in dsts:
                    nc.vector.tensor_tensor(dst[:, :, 0, :], pa[:, :, 0, :], pb[:, :, 1, :], ALU.subtract)
                    last = nc.vector.tensor_tensor(dst[:, :, 1, :], pa[:, :, 1, :], pb[:, :, 0, :], ALU.add)
                last.then_inc(sem["rot"], 1)

            cos_all = cs[:, 0:CW].rearrange("p (t e) -> p t e", e=HALF)
            sin_all = cs[:, CW:2 * CW].rearrange("p (t e) -> p t e", e=HALF)

            def trig_tile(tab, t, step, groups):
                v = tab[:, t, 0::step]
                return v.unsqueeze(1).unsqueeze(1).to_broadcast([P, groups, 2, HALF // step])

            def trig_tiles(tab, t0):
                v = tab[:, t0:t0 + 4, 0::2]
                return v.unsqueeze(2).to_broadcast([P, 4, 2, HALF // 2])

            for s in steps:
                k, n = s.kind, s.n
                if k == "norm_a":
                    t, slot = n["t"], n["slot"]
                    dve.wait_ge(sem["rstd"], s.after["rstd"])
                    dve.wait_ge(sem["gain"], n["gain"])
                    nc.vector.scalar_tensor_tensor(rows[slot][:], xr[:, t * D:(t + 1) * D], rs[:, t:t + 1], gz[:],
                                                   ALU.mult, ALU.mult).then_inc(sem["xn"], 1)
                elif k == "final":
                    t = n["t"]
                    dve.wait_ge(sem["rstd"], s.after["rstd"])
                    dve.wait_ge(sem["gain"], n["gain"])
                    rw = xr[:, t * D:(t + 1) * D]
                    nc.vector.scalar_tensor_tensor(rw, rw, rs[:, t:t + 1], gz[:], ALU.mult, ALU.mult).then_inc(sem["fin"], 1)
                elif k == "norm_b":
                    t = n["t"]
                    for j in range(2):
                        split_lo(s, j, act_tile(1, t)[:, 4 * j:4 * j + 4, :], in4(bank(s.banks[j])),
                                 act_tile(0, t)[:, 4 * j:4 * j + 4, :])
                elif k == "split4":
                    split_lo(s, 0, split_dest(s, 1), in4(bank(s.banks[0])), split_dest(s, 0))
                elif k == "tables":
                    c1, c2, c3 = two_pi_parts()
                    ang, turns, back = p1[:, 0:CW], p1[:, CW:2 * CW], t2[:, 0:CW]
                    dve.wait_ge(sem["const_ld"], 32)
                    dve.wait_ge(sem["hi"], s.before["hi"])
                    linked(nc.vector.tensor_copy(posf, pos_i[:]))
                    ang = t2[:, CW:2 * CW]
                    for t in range(T):
                        last = nc.vector.tensor_scalar(ang[:, t * NFREQ:(t + 1) * NFREQ], frq[:], posf[:, t:t + 1],
                                                       None, ALU.mult)
                    linked(last)
                    for i in range(2):
                        turns = p1[:, i * CW:(i + 1) * CW]
                        linked(nc.vector.tensor_scalar(turns, ang, 1.0 / TWO_PI, 0.25 * i, ALU.mult, ALU.add))
                        linked(nc.vector.tensor_scalar(turns, turns, 12582912.0, -12582912.0, ALU.add, ALU.add))
                        linked(nc.vector.scalar_tensor_tensor(back, turns, -c1, ang, ALU.mult, ALU.add))
                        linked(nc.vector.scalar_tensor_tensor(back, turns, -c2, back, ALU.mult, ALU.add))
                        linked(nc.vector.scalar_tensor_tensor(back, turns, -c3, back, ALU.mult, ALU.add))
                        nc.vector.tensor_scalar(turns, back, 0.25 * i * TWO_PI, None, ALU.add).then_inc(sem["stage"], 1)
                    dve.wait_ge(sem["trig"], s.after["trig"])
                    for j in range(2):
                        st = p1[:, j * CW:(j + 1) * CW].rearrange("p (t u e) -> p t u e", t=4, u=4)
                        co, si = cos_all[:, 4 * j:4 * j + 4, 0::2], sin_all[:, 4 * j:4 * j + 4, 0::2]
                        nc.vector.tensor_copy(st[:, :, 0, :], co)
                        nc.vector.tensor_copy(st[:, :, 1, :], co)
                        nc.vector.tensor_scalar(st[:, :, 2, :], si, -1.0, None, ALU.mult)
                        nc.vector.tensor_copy(st[:, :, 3, :], si).then_inc(sem["stage"], 1)
                elif k == "proj":
                    name, b = n["name"], s.banks[0]
                    if name in ("kpe", "kiwi", "qi", "kv", "q"):
                        dve.wait_ge(sem["a_full"], s.after["a_full"])
                        slot, job = n["slot"], n["job"]
                        st = p1[:, slot * CW:(slot + 1) * CW]
                        if name == "kpe":
                            dve.wait_ge(sem["csq"], s.before["csq"])
                            dve.wait_ge(sem["z_st0"], s.before["z_st0"])
                            dve.wait_ge(sem["z_st1"], s.before["z_st1"])
                            dve.wait_ge(sem["hi"], s.before["hi"])
                        if name == "kiwi":
                            dve.wait_ge(sem["cs_ld"], n["cs"])
                            dve.wait_ge(sem["hi"], s.before["hi"])
                        if name in ("kpe", "kiwi"):
                            cols = n["cols"]
                            v = bank(b, 4 * cols).rearrange("p (t c) -> p t c", c=cols)
                            if name == "kiwi":
                                nc.vector.tensor_scalar(
                                    wis[:].rearrange("p (t h) -> p t h", h=IDX_HEADS)[:, 4 * job:4 * job + 4, :],
                                    v[:, :, IDX_DIM:IDX_DIM + IDX_HEADS], W_IDX_SCALE, None, ALU.mult).then_inc(sem["widx"], 1)
                            dup = st.rearrange("p (t r u e) -> p t r u e", t=4, r=2, u=2)
                            rotate(s, v[:, :, 0:64].rearrange("p t (u e) -> p t u e", u=2), 4, 32,
                                   trig_tiles(cos_all, 4 * job), trig_tiles(sin_all, 4 * job),
                                   [dup[:, :, r] for r in range(2)])
                        elif name == "qi":
                            rotate(s, bank(b).rearrange("p (g u e) -> p g u e", u=2, e=32), 8, 32,
                                   trig_tile(cos_all, job, 2, 8), trig_tile(sin_all, job, 2, 8),
                                   [st.rearrange("p (g u e) -> p g u e", u=2, e=32)])
                        else:
                            g = 4 if name == "q" else 2
                            if name == "kv":
                                dve.wait_ge(sem["vcopy"], s.after["vcopy"])
                            if n["st_before"]:
                                dve.wait_ge(sem["st%d" % slot], n["st_before"])
                            rotate(s, bank(b, g * HD).rearrange("p (g u e) -> p g u e", u=2, e=HALF), g, HALF,
                                   trig_tile(cos_all, job, 1, g), trig_tile(sin_all, job, 1, g),
                                   [st[:, 0:g * HD].rearrange("p (g u e) -> p g u e", u=2, e=HALF)])
                    elif name == "c":
                        dve.wait_ge(sem["rstd"], s.after["rstd"])
                        dve.wait_ge(sem["gain"], n["gain"])
                        for r in range(2):
                            c = n["slot"] * CW + r * RANK
                            last = nc.vector.scalar_tensor_tensor(
                                p1[:, c:c + RANK], bank(b)[:, r * RANK:(r + 1) * RANK],
                                lat_rs[:, 2 * n["slot"] + r:2 * n["slot"] + r + 1], gz[:, r * RANK:(r + 1) * RANK],
                                ALU.mult, ALU.mult)
                        last.then_inc(sem["xn"], 1)
                    elif name == "wo":
                        dve.wait_ge(sem["a_full"], s.after["a_full"])
                        dve.wait_ge(sem["xin%d" % n["slot"]], n["xin"])
                        c = n["job"] * D + n["j"] * CW
                        nc.vector.tensor_tensor(xr[:, c:c + CW], bank(b), p1[:, n["slot"] * CW:(n["slot"] + 1) * CW],
                                                ALU.add).then_inc(sem["xadd"], 1)
                elif k == "pp":
                    dve.wait_ge(sem["sg"], n["sg"])
                    dve.wait_ge(sem["b_full"], s.after["b_full"])
                    st = p1[:, n["slot"] * CW:(n["slot"] + 1) * CW]
                    nc.vector.tensor_tensor(st, bank(s.banks[0]), st, ALU.mult).then_inc(sem["pp"], 1)
                    dve.wait_ge(sem["pp"], s.after["pp"])
                    c = n["t"] * D + n["j"] * CW
                    nc.vector.tensor_tensor(xr[:, c:c + CW], xr[:, c:c + CW], st, ALU.add).then_inc(sem["xadd"], 1)
                elif k == "p_split":
                    split_lo(s, 0, p_t[1][:], bank(s.banks[0], PLE), p_t[0][:])
                elif k == "hproj":
                    b, j, name = s.banks[0], n["j"], n["name"]
                    if name == "pe":
                        dve.wait_ge(sem["b_full"], s.after["b_full"])
                        dve.wait_ge(sem["csq"], n["csq"])
                        nc.vector.tensor_tensor(bank(b), bank(b), t2[:, j * CW:(j + 1) * CW],
                                                ALU.mult).then_inc(sem["stage"], 1)
                    at = {"q": Q0, "pe": PE0, "k": K0, "v": V0}[name]
                    split_lo(s, 0, region(1, at, j * CW, CW), bank(b), region(0, at, j * CW, CW))
                elif k == "idx":
                    t, h, slot = n["t"], n["h"], n["k"] % 2
                    dve.wait_ge(sem["relu"], s.after["relu"])
                    if n["k"] == 0:
                        dve.wait_ge(sem["x2_st"], n["x2"])
                    else:
                        dve.wait_ge(sem["sc"], s.before["sc"])
                    dst = score_at(t, n["c"] * CW, n["n"])
                    src = gz[:, slot * CW:slot * CW + n["n"]]
                    wcol = wis[:, t * IDX_HEADS + h:t * IDX_HEADS + h + 1]
                    if h == 0:
                        nc.vector.tensor_scalar(dst, src, wcol, None, ALU.mult).then_inc(sem["sc"], 1)
                    else:
                        nc.vector.scalar_tensor_tensor(dst, src, wcol, dst, ALU.mult, ALU.add).then_inc(sem["sc"], 1)
                elif k == "idx_mask":
                    dve.wait_ge(sem["sc"], s.after["sc"])
                    dst = score_at(n["t"], n["t"] * P, P)
                    linked(nc.vector.tensor_tensor(dst, dst, tri[:], ALU.add))
                elif k == "bit":
                    bit = n["bit"]
                    cand = u_cand.bitcast(F32)
                    if bit == 31:
                        linked(nc.vector.memset(cand, 0.0))
                    else:
                        linked(nc.vector.scalar_tensor_tensor(u_cand, u_bits, 1 << bit, u_mask,
                                                              ALU.bitwise_or, ALU.bitwise_xor))
                    for i in range(SPREAD):
                        t = FULL + i
                        linked(nc.vector.tensor_scalar(gz[:, 0:(t + 1) * P], score_at(t), cand[:, i:i + 1], 0.0,
                                                        ALU.is_ge, ALU.add, accum_out=cnt[:, i:i + 1]))
                    if bit == 31:
                        linked(nc.vector.tensor_scalar(u_bits, cnt, TOPK - 0.5, float(1 << 31), ALU.is_gt, ALU.mult))
                        um = u_mask.bitcast(I32)
                        linked(nc.vector.tensor_scalar(um, u_bits.bitcast(I32), -(1 << 31), 31,
                                                       ALU.bitwise_xor, ALU.arith_shift_right))
                        linked(nc.vector.tensor_scalar(um, um, -(1 << 31), None, ALU.bitwise_or))
                    else:
                        linked(nc.vector.tensor_scalar(u_inc, cnt, TOPK - 0.5, float(1 << bit), ALU.is_gt, ALU.mult))
                        linked(nc.vector.tensor_tensor(u_bits, u_bits, u_inc, ALU.bitwise_or))
                elif k == "above":
                    linked(nc.vector.tensor_tensor(u_cand, u_bits, u_mask, ALU.bitwise_xor))
                    thr = u_cand.bitcast(F32)
                    for i in range(SPREAD):
                        t = FULL + i
                        linked(nc.vector.tensor_scalar(gz[:, 0:(t + 1) * P], score_at(t), thr[:, i:i + 1], 0.0,
                                                        ALU.is_gt, ALU.add, accum_out=cnt[:, i:i + 1]))
                    linked(nc.vector.tensor_scalar(need, cnt, -1.0, float(TOPK), ALU.mult, ALU.add))
                elif k == "sel":
                    t = n["t"]
                    i, keys = t - FULL, (t + 1) * P
                    thr = u_cand.bitcast(F32)[:, i:i + 1]
                    eq, order = gz[:, 0:keys], cs[:, 0:keys]
                    if i:
                        dve.wait_ge(sem["found"], s.before["found"])
                    linked(nc.vector.tensor_scalar(eq, score_at(t), thr, None, ALU.is_equal))
                    linked(nc.vector.tensor_tensor_scan(order, eq, eq, 0.0, ALU.add, ALU.max))
                    linked(nc.vector.scalar_tensor_tensor(eq, order, need[:, i:i + 1], eq, ALU.is_le, ALU.mult))
                    nc.vector.scalar_tensor_tensor(score_at(t), score_at(t), thr, eq, ALU.is_gt,
                                                   ALU.add).then_inc(sem["found"], 1)
                elif k == "mask":
                    t = n["t"]
                    if t == 0:
                        dve.wait_ge(sem["a_full"], n["a_full"])
                        dve.wait_ge(sem["found"], s.before["found"])
                        dve.wait_ge(sem["z_st0"], s.before["z_st0"])
                        dve.wait_ge(sem["z_st1"], s.before["z_st1"])
                    if t < FULL:
                        if t:
                            nc.vector.memset(mask_at(t)[:, 0:t * P].bitcast(F32), 0.0)
                        linked(nc.vector.tensor_copy(mask_at(t)[:, t * P:(t + 1) * P], tri[:]))
                    else:
                        linked(nc.vector.tensor_scalar(mask_at(t), score_at(t), -1.0, -NEG, ALU.add, ALU.mult))
                elif k == "S":
                    ps, keys = n["ps"], (n["qb"] + 1) * P
                    dve.wait_ge(sem["a_full"], s.after["a_full"])
                    src = bank(s.banks[0], keys)
                    if n["lay"] == 0:
                        linked(nc.vector.tensor_reduce(mx[:, ps:ps + 1], src, AX_X, ALU.max))
                    else:
                        linked(nc.vector.tensor_tensor_reduce(rows[ps][:, 0:keys], src, mask_at(n["qb"]).bitcast(F32),
                                                              1.0, -3.4e38, ALU.add, ALU.max, mx[:, ps:ps + 1]))
                    nc.vector.tensor_scalar(nb[:, ps:ps + 1], mx[:, ps:ps + 1],
                                            -MLA_SCALE if n["lay"] == 0 else -DSA_SCALE, None,
                                            ALU.mult).then_inc(sem["nb"], 1)
                elif k == "R":
                    ps = n["ps"]
                    dve.wait_ge(sem["ex"], n["ex"])
                    nc.vector.reciprocal(ri[:, ps:ps + 1], sm[:, ps:ps + 1]).then_inc(sem["ri"], 1)
                elif k == "T":
                    for j, b in enumerate(s.banks):
                        kts = min(4, n["qb"] + 1 - 4 * j)
                        parts = [act[part][:, 0:8 * CW].rearrange("p (k c) -> p k c", c=CW)[
                            :, 4 * j:4 * j + kts, (n["qb"] % 4) * P:(n["qb"] % 4 + 1) * P] for part in range(2)]
                        split_lo(s, j, parts[1], in4(bank(b, kts * P)), parts[0])
                elif k == "PV":
                    h, g = n["h"], n["g"]
                    dve.wait_ge(sem["b_full"], s.after["b_full"])
                    dve.wait_ge(sem["z_ld"], n["z_ld"])
                    dst = xr[:].rearrange("p (t c) -> p t c", c=D)[:, 4 * g:4 * g + 4, h * P:(h + 1) * P]
                    nc.vector.tensor_tensor(dst, in4(bank(s.banks[0])), in4(gz[:, g * CW:(g + 1) * CW]),
                                            ALU.mult).then_inc(sem["og"], 1)
                elif k == "og_split":
                    t = n["t"]
                    dve.wait_ge(sem["hi"], s.after["hi"])
                    nc.vector.tensor_tensor(act_tile(1, t), in4(xr[:, t * D:(t + 1) * D]), act_tile(0, t).bitcast(F32),
                                            ALU.subtract).then_inc(sem["lo"], 1)
                elif k == "v_split":
                    dve.wait_ge(sem["hi"], s.after["hi"])
                    nc.vector.tensor_tensor(v1(1, n["g"], 0, S), t2[:], v1(0, n["g"], 0, S).bitcast(F32),
                                            ALU.subtract).then_inc(sem["lo"], 1)

        @block.tensor
        def _(pe):
            def product(dst, lhs, rhs, start, stop):
                nc.tensor.matmul(dst, lhs(1), rhs(0), start=start, stop=False)
                nc.tensor.matmul(dst, lhs(0), rhs(1), start=False, stop=False)
                return nc.tensor.matmul(dst, lhs(0), rhs(0), start=False, stop=stop)

            def bank_free(s, j=0):
                for name, v in s.free[j]:
                    pe.wait_ge(sem[name], v)

            for s in steps:
                k, n = s.kind, s.n
                if k == "norm_b":
                    pe.wait_ge(sem["xn"], n["xn"])
                    pe.wait_ge(sem["consts"], 1)
                    for j in range(2):
                        bank_free(s, j)
                        for i in range(4):
                            c = (4 * j + i) * P
                            last = nc.tensor.transpose(bank(s.banks[j])[:, i * P:(i + 1) * P],
                                                       rows[n["slot"]][:, c:c + P], ident[:])
                        last.then_inc(sem["b_full"], 1)
                elif k == "split4":
                    pe.wait_ge(sem[n["ready"][0]], n["ready"][1])
                    bank_free(s)
                    if n["src"] == "t2" or n.get("whole"):
                        src = (t2 if n["src"] == "t2" else p1)[:, n["j"] * CW:(n["j"] + 1) * CW]
                    else:
                        src = p1[:, n["slot"] * CW:(n["slot"] + 1) * CW]
                    for i in range(4):
                        last = nc.tensor.transpose(bank(s.banks[0])[:, i * P:(i + 1) * P], src[:, i * P:(i + 1) * P],
                                                   ident[:])
                    last.then_inc(sem["b_full"], 1)
                elif k == "tables":
                    for j in range(2):
                        pe.wait_ge(sem["stage"], s.before["stage"] + 3 + j)
                        bank_free(s, j)
                        for i in range(4):
                            c = j * CW + i * P
                            last = nc.tensor.transpose(bank(s.banks[j])[:, i * P:(i + 1) * P], p1[:, c:c + P], ident[:])
                        last.then_inc(sem["b_full"], 1)
                elif k == "proj":
                    name, b, buf = n["name"], s.banks[0], n["buf"]
                    bank_free(s)
                    pe.wait_ge(sem["lo"], n["act"])
                    first = s.before["a_full"]
                    if name in ("kpe", "kiwi"):
                        cols = n["cols"]
                        pe.wait_ge(sem["w"], n["w_ready"][KD - 1])
                        for i, t in enumerate(n["tiles"]):
                            for d in range(KD):
                                last = product(bank(b)[:, i * cols:(i + 1) * cols],
                                               lambda part: act_at(part, d, t * P, P),
                                               lambda part: w_at(part, buf, d, 0, cols), d == 0, d == KD - 1)
                    elif name == "z":
                        half, m = n["job"] // 4, n["job"] % 4
                        for d in range(KD):
                            pe.wait_ge(sem["w"], n["w_ready"][d])
                            last = product(bank(b), lambda part: w_at(part, buf, d, m * P, P),
                                           lambda part: act_at(part, d, half * CW, CW), d == 0, d == KD - 1)
                    else:
                        t = n["job"]
                        for d in range(KD):
                            pe.wait_ge(sem["w"], n["w_ready"][d])
                            last = product(bank(b), lambda part: act_at(part, d, t * P, P),
                                           lambda part: w_at(part, buf, d, 0, CW), d == 0, d == KD - 1)
                    last.then_inc(sem["a_full"], 1)
                elif k == "p_split":
                    pe.wait_ge(sem["p_ld%d" % n["slot"]], s.after["p_ld%d" % n["slot"]])
                    bank_free(s)
                    for i in range(2):
                        c = n["slot"] * PLE + i * P
                        last = nc.tensor.transpose(bank(s.banks[0])[:, i * P:(i + 1) * P], t2[:, c:c + P], ident[:])
                    last.then_inc(sem["b_full"], 1)
                elif k == "pp":
                    pe.wait_ge(sem["lo"], n["ready"])
                    pe.wait_ge(sem["w"], n["w_ready"])
                    bank_free(s)
                    wp = head_w if n["j"] == 0 else kpe
                    for r in range(2):
                        last = product(bank(s.banks[0]), lambda part: p_t[part][:, r * P:(r + 1) * P],
                                       lambda part: wp[part][:, r * CW:(r + 1) * CW], r == 0, r == 1)
                    last.then_inc(sem["b_full"], 1)
                elif k == "hproj":
                    b, j, name = s.banks[0], n["j"], n["name"]
                    pe.wait_ge(sem["w"], n["w_ready"])
                    pe.wait_ge(sem["lo"], n["c_ready"])
                    bank_free(s)
                    if name in ("q", "pe", "k"):
                        off, step, lat = {"q": (0, 256, 0), "pe": (128, 256, 0), "k": (512, 128, 2)}[name]
                        for r in range(2):
                            last = product(bank(b), lambda part: head_w[part][:, off + r * step:off + r * step + P],
                                           lambda part: ring[part][:, (lat + r) * S + j * CW:(lat + r) * S + (j + 1) * CW],
                                           r == 0, r == 1)
                    else:
                        for i in range(4):
                            kt = 4 * j + i
                            for r in range(2):
                                last = product(bank(b)[:, i * P:(i + 1) * P],
                                               lambda part: ring[part][:, (2 + r) * S + kt * P:(2 + r) * S + (kt + 1) * P],
                                               lambda part: head_w[part][:, 768 + r * P:768 + (r + 1) * P], r == 0, r == 1)
                    last.then_inc(sem["b_full"], 1)
                elif k == "idx":
                    h, t = n["h"], n["t"]
                    pe.wait_ge(sem["lo"], n["q_ready"])
                    bank_free(s)
                    r0, c0 = 64 * (h % 2), (t % 2) * CW + (h // 2) * P
                    product(bank(s.banks[0], n["n"]), lambda part: head_w[part][r0:r0 + 64, c0:c0 + P],
                            lambda part: kpe[part][r0:r0 + 64, n["c"] * CW:n["c"] * CW + n["n"]],
                            True, True).then_inc(sem["b_full"], 1)
                elif k == "S":
                    lay, qb = n["lay"], n["qb"]
                    pe.wait_ge(sem["lo"], n["q_ready"])
                    bank_free(s)
                    keys = (qb + 1) * P
                    for c0 in range(0, keys, CW):
                        cn = min(CW, keys - c0)
                        dst = psum[:, s.banks[0] * CW + c0:s.banks[0] * CW + c0 + cn]
                        if lay == 0:
                            diag = c0 + cn == keys
                            product(dst, lambda part: region(part, Q0, qb * P, P),
                                    lambda part: region(part, K0, c0, cn), True, False)
                            last = product(dst, lambda part: region(part, PE0, qb * P, P),
                                           lambda part: kpe[part][:, c0:c0 + cn], False, not diag)
                            if diag:
                                last = nc.tensor.matmul(dst[:, cn - P:cn], ident_r[:], tri_r[:], start=False, stop=True)
                        else:
                            g = n["h"] // GROUP
                            last = product(dst, lambda part: qT1(part, n["h"] % 2, qb * P, P),
                                           lambda part: kT1(part, g, c0, cn), True, True)
                    last.then_inc(sem["a_full"], 1)
                elif k == "T":
                    pe.wait_ge(sem["pn"], n["pn"])
                    for j, b in enumerate(s.banks):
                        bank_free(s, j)
                        for i in range(min(4, n["qb"] + 1 - 4 * j)):
                            c = (4 * j + i) * P
                            last = nc.tensor.transpose(bank(b)[:, i * P:(i + 1) * P], rows[n["ps"]][:, c:c + P], ident[:])
                        last.then_inc(sem["b_full"], 1)
                elif k == "PV":
                    g, lay = n["g"], n["lay"]
                    pe.wait_ge(sem["lo"], n["ready"])
                    bank_free(s)
                    kts = 4 * g + 4
                    for kt in range(kts):
                        c0 = max(0, kt - 4 * g) * P
                        vals = ((lambda part: region(part, V0, kt * P, P)) if lay == 0
                                else (lambda part: v1(part, n["h"] // GROUP, kt * P, P)))
                        last = product(bank(s.banks[0])[:, c0:CW], vals,
                                       lambda part: pt_at(part, kt, c0, CW - c0), kt == 0, kt == kts - 1)
                    last.then_inc(sem["b_full"], 1)


NAMES = ["x", "p", "positions", "norm_in", "mla_w_in", "mla_q_norm", "mla_kv_norm", "mla_w_uq", "mla_w_uk",
         "mla_w_uv", "mla_w_out", "dsa_w_in", "dsa_w_out", "ple_w_proj", "ple_norm", "ple_w_gate", "final_norm"]


def kernel(**inputs):
    import concourse.bacc as bacc
    from concourse.bass_utils import run_bass_kernel_spmd as run

    nc = bacc.Bacc("TRN2", target_bir_lowering=False, num_devices=1)
    arrays = {n: np.ascontiguousarray(inputs[n]) for n in NAMES}
    half = np.float32(NFREQ)
    arrays["freqs"] = (1.0 / (np.float32(10000.0) ** (np.arange(NFREQ, dtype=np.float32) / half))).astype(np.float32)
    h = {n: nc.dram_tensor("in_" + n, a.shape, mybir.dt.from_np(a.dtype), kind="ExternalInput").ap()
         for n, a in arrays.items()}
    out = nc.dram_tensor("out", (1, S, D), F32, kind="ExternalOutput").ap()
    build(nc, h["x"][0], h["p"].rearrange("l b s c -> (l b) s c"), h["positions"], h["norm_in"],
          h["mla_w_in"][0], h["mla_q_norm"][0], h["mla_kv_norm"][0], h["mla_w_uq"][0],
          h["mla_w_uk"][0].rearrange("c h n -> c (h n)"), h["mla_w_uv"][0].rearrange("c h n -> c (h n)"),
          h["mla_w_out"][0], h["dsa_w_in"][0], h["dsa_w_out"][0], h["ple_w_proj"], h["ple_norm"], h["ple_w_gate"],
          h["final_norm"], h["freqs"], out[0])
    r = run(nc, [{"in_" + n: a for n, a in arrays.items()}], core_ids=[0])
    return r.results[0]["out"]
```

```python
from contextlib import ExitStack

import numpy as np
import concourse.bass as bass
from concourse import mybir

ALU = mybir.AluOpType
ACT = mybir.ActivationFunctionType
F32 = mybir.dt.float32
F32R = mybir.dt.float32r
U32 = mybir.dt.uint32
I32 = mybir.dt.int32
AX_X = mybir.AxisListType.X

P = 128
S = 1024
D = 1024
T = S // P
KD = D // P
CW = 512
HEADS = 8
RANK = 256
NOPE, ROPE_D, VDIM = 128, 64, 128
MLA_SCALE = float(np.float32((NOPE + ROPE_D) ** -0.5))
HD = 128
DSA_SCALE = float(np.float32(HD ** -0.5))
KV_HEADS = 2
GROUP = HEADS // KV_HEADS
IDX_HEADS, IDX_DIM = 8, 64
IDX_SCALE = float(IDX_DIM ** -0.5)
W_IDX_SCALE = float(np.float32(IDX_HEADS ** -0.5))
TOPK = 256
FULL = TOPK // P
PLE = 256
EPS = 1e-6
NEG = -3.0e38
HALF = HD // 2
NFREQ = HALF
SCORE_AT = [P * t * (t + 1) // 2 for t in range(T + 1)]
SPREAD = T - FULL
SEARCH = [2, 4, 5, 3, 6, 7]
ACT_TILES = [3, 6, 7]
TWO_PI = 2 * np.pi
RAW_SLOTS = 3


def two_pi_parts():
    c1 = 6.28125
    bits = np.frombuffer(np.float32(TWO_PI - c1).tobytes(), np.uint32)[0] & 0xFFFFF000
    c2 = float(np.frombuffer(np.uint32(bits).tobytes(), np.float32)[0])
    return c1, c2, TWO_PI - c1 - c2


SMALL = 2
SEQ = {
    0: [("c", "mla_in", 0, CW, 0), ("kpe", "mla_in", 512, P, SMALL),
        ("z", "mla_in", 576, CW, 1), ("z", "mla_in", 1088, CW, 0),
        ("wo", "out0", 0, CW, 0), ("wo", "out0", CW, CW, 1),
        ("gate", "gate0", 0, CW, 0), ("gate", "gate0", CW, CW, 1)],
    1: [("kiwi", "dsa_in", 2048, P, SMALL), ("qi", "dsa_in", 1536, CW, 0), ("kv", "dsa_in", 1024, CW, 1),
        ("q", "dsa_in", 0, CW, 0), ("q", "dsa_in", CW, CW, 1),
        ("z", "dsa_in", 2120, CW, 0), ("z", "dsa_in", 2632, CW, 1),
        ("wo", "out1", 0, CW, 0), ("wo", "out1", CW, CW, 1),
        ("gate", "gate1", 0, CW, 0), ("gate", "gate1", CW, CW, 1)],
}
RES = ["ring0", "ring1", "headW"]
CHUNKS = [(lay, i) + c for lay in (0, 1) for i, c in enumerate(SEQ[lay])]
DMA_SEMS = (["raw_ld%d" % i for i in range(RAW_SLOTS)] + ["x_ld%d" % t for t in range(T)] +
            ["const_ld", "gain", "z_st0", "z_st1", "z_ld", "xin0", "xin1", "p_ld0", "p_ld1",
             "x2_st", "st0", "st1", "cs_st", "cs_ld", "t2_ld", "k0_ld", "lat_ld", "out_st"])
PLAIN_SEMS = ["a_full", "b_full", "hi", "lo", "sq", "rstd", "xn", "w", "zs", "rot_in", "rot",
              "xadd", "sg", "pp", "relu", "sc", "nb", "ex", "ri", "pn", "og", "stage", "trig",
              "csq", "consts", "vcopy", "found", "widx", "w_hi", "w0", "fk", "tally", "cand", "pool_chain", "dve_chain", "act_chain", "fin", "pe_in"]


class Step:
    pass


def plan():
    steps, now = [], {n: 0 for n in DMA_SEMS + PLAIN_SEMS}
    bank_free = {b: [] for b in range(8)}
    ring_at = {"A": 0, "B": 0}
    read_by = {}
    granules = [0]

    def add(kind, incs=None, ring=None, jobs=0, freed=None, wide=False, **kw):
        s = Step()
        s.kind, s.before = kind, dict(now)
        for n, k in (incs or {}).items():
            now[n] += k * (16 if n in DMA_SEMS else 1)
        s.after = dict(now)
        s.n = dict(kw)
        s.banks, s.free = [], []
        for j in range(jobs):
            if wide:
                first = (ring_at["A"] + 1) // 2 * 2 % 4
                banks = [first, first + 1]
                ring_at["A"] = first + 2
            else:
                banks = [ring_at[ring] % 4 + (4 if ring == "B" else 0)]
                ring_at[ring] += 1
            need = {}
            for b in banks:
                for n, v in bank_free[b]:
                    need[n] = max(need.get(n, 0), v)
            s.banks.append(banks[0])
            s.free.append(sorted(need.items()))
            for b in banks:
                bank_free[b] = [(n, s.before[n] + j + 1) for n in freed]
        steps.append(s)
        return s

    def w(chunk, d):
        lay, i, name, src, c0, n, buf = chunk
        res = RES[buf]
        g = granules[0]
        granules[0] += 1
        first = (lay, i) == (0, 0)
        done = "w0" if first else "w"
        incs = {done: 1, "raw_ld%d" % (g % RAW_SLOTS): 1}
        if first:
            incs["w_hi"] = 1
        s = add("w_first" if first else "w", incs, src=src, d=d, c0=c0, cols=n, raw_free=raw_free(g),
                buf=buf, g=g, reader=read_by.get(res) if d == 0 else None)
        split_at.append((done, s.after[done]))
        w_after[(lay, i, d)] = split_at[g]

    w_after = {}
    split_at = []

    def raw_free(g):
        return split_at[g - RAW_SLOTS] if g >= RAW_SLOTS else None

    def small_w(kind, res, **kw):
        pieces = 2
        for k in range(pieces):
            g = granules[0]
            granules[0] += 1
            loads = 2 if kind == "head_w" and k == 1 else 1
            s = add(kind, {"w": 1, "raw_ld%d" % (g % RAW_SLOTS): loads}, piece=k, g=g, res=res,
                    raw_free=raw_free(g),
                    reader=read_by.get(res) if k == 0 else None, **kw)
            split_at.append(("w", s.after["w"]))
        return s.after["w"]

    lo_at = {}

    def norm_a(t, slot, ready, gain):
        return add("norm_a", {"sq": 1, "rstd": 1, "xn": 1}, t=t, slot=slot, ready=ready, gain=gain)

    def norm_b(t, slot, xn):
        s = add("norm_b", {"b_full": 2, "hi": 2, "lo": 2}, ring="B", jobs=2, freed=["lo"],
                t=t, slot=slot, xn=xn)
        lo_at[("act", t)] = s.after["lo"]

    def gain(which):
        return add("gain", {"gain": 1}, which=which, reader=read_by.get("G"))

    def split4(src, slot, ready, cols=CW, **kw):
        return add("split4", {"b_full": 1, "hi": 1, "lo": 1}, ring="B", jobs=1, freed=["lo"],
                   src=src, slot=slot, ready=ready, cols=cols, **kw)

    def chunk_of(lay, i):
        return next(c for c in CHUNKS if c[:2] == (lay, i))

    def next_chunk(lay, i):
        at = [c[:2] for c in CHUNKS].index((lay, i)) + 1
        return CHUNKS[at] if at < len(CHUNKS) else None

    def proj(lay, i, job, freed, incs, jobs_note=None, **kw):
        c = chunk_of(lay, i)
        half = {"z": job // 4, "kpe": job, "kiwi": job}.get(c[2])
        tiles = [job] if half is None else range(4 * half, 4 * half + 4)
        allinc = {"a_full": 1}
        allinc.update(incs)
        s = add("proj", allinc, ring="A", jobs=1, freed=freed, lay=lay, chunk=i, name=c[2], cols=c[5],
                buf=c[6], job=job, half=half, w_ready=[w_after[(lay, i, d)] for d in range(KD)],
                act=max(lo_at[("act", t)] for t in tiles), **kw)
        read_by[RES[c[6]]] = ("a_full", s.after["a_full"])
        return s

    store_at = {"st0": 0, "st1": 0}

    add("start", {"const_ld": 2, "gain": 1, "lat_ld": 2, "consts": 1})
    for t in range(T):
        if t < 2:
            add("load_x", {"x_ld%d" % t: 1}, t=t)
        w(chunk_of(0, 0), t)
        if 2 <= t:
            add("load_x", {"x_ld%d" % t: 1}, t=t)

    def z_chunk(lay, i, base, slots, prefetch=True, extra=None):
        for job in range(8):
            if prefetch:
                w(next_chunk(lay, i), job)
            slot = job % 2
            proj(lay, i, job, ["zs"], {"zs": 1, "z_st%d" % slot: 1}, slot=slot, base=base)
            if extra:
                extra(8 * (base // CW) + job)

    def rope_job(lay, i, job, slot, extra_inc=None, **kw):
        inc = {"rot_in": 1, "rot": 1}
        inc.update(extra_inc or {})
        return proj(lay, i, job, ["rot_in"], inc, slot=slot, **kw)

    def key_job(lay, i, job):
        return proj(lay, i, job, ["fk"], {"fk": 1}, slot=job)

    def key_back(lay, job, fk, **kw):
        incs = {"b_full": 1, "rot_in": 1, "rot": 1}
        if lay == 1:
            incs["widx"] = 1
        return add("key_back", incs, ring="B", jobs=1, freed=["rot_in"], lay=lay, job=job, fk=fk, **kw)

    def key_split(lay, job, rot):
        return split4("p1" if lay == 0 else "t2", job, ("rot", rot), dest="kpeT", j=job).after["lo"]

    prev = norm_a(0, 0, ("x_ld0", 16), now["gain"])
    for t in range(T):
        nxt = norm_a(t + 1, (t + 1) % 2, ("x_ld%d" % (t + 1), 16), now["gain"]) if t + 1 < T else None
        norm_b(t, t % 2, prev.after["xn"])
        prev = nxt
        w(next_chunk(0, 0), t)
        w(next_chunk(0, 1), t)
        proj(0, 0, t, ["xn"], {"sq": 2, "rstd": 1, "xn": 1}, slot=t % 2)
    latent_rows = now["xn"]
    read_by["G"] = ("xn", now["xn"])
    tb = add("tables", {"stage": 2, "trig": 2, "cs_st": 1})
    fk = [key_job(0, 1, job).after["fk"] for job in range(2)]
    rots, marks = [], {}

    def z0_extra(k):
        if k in (0, 1):
            rots.append(key_back(0, k, fk[k], trig=tb.after["trig"]).after["rot"])
        elif k in (2, 3):
            lo_at["kpeT"] = key_split(0, k - 2, rots[k - 2])
        elif k == 5:
            marks["csq"] = add("table_t", {"stage": 2, "b_full": 2, "csq": 2}, ring="B", jobs=2,
                               freed=["csq"]).after["csq"]
        elif k >= 8:
            lo_at["cT"] = split4("xr", 0, ("xn", latent_rows), dest="cT", t=k - 8).after["lo"]
    z_chunk(0, 2, 0, 2, extra=z0_extra)
    head_w = {0: small_w("head_w", "headW", h=0)}
    z_chunk(0, 3, CW, 2, prefetch=False, extra=z0_extra)

    att = {"n": 0}
    order = [6, 7, 0, 1, 4, 5, 2, 3]

    def s_step(lay, h, qb, q_ready):
        n = att["n"]
        att["n"] += 1
        incs = {"a_full": 1, "nb": 1, "ex": 1}
        s = add("S", incs, ring="A", jobs=1, freed=["ex" if lay == 0 else "nb"], wide=True,
                lay=lay, h=h, qb=qb, ps=n % 3, q_ready=q_ready)
        r = add("R", {"ri": 1, "pn": 1}, lay=lay, ps=n % 3, qb=qb, ex=s.after["ex"])
        return r.after["pn"]

    def t_step(lay, h, qb, pn, ps):
        jobs = qb // 4 + 1
        s = add("T", {"b_full": jobs, "hi": jobs, "lo": jobs}, ring="B", jobs=jobs, freed=["lo"],
                lay=lay, qb=qb, pn=pn, ps=ps, pbuf=order.index(qb) // 2 % 2)
        return s.after["lo"]

    def pv_step(lay, h, g, pt_ready, v_ready, z_ld):
        s = add("PV", {"b_full": 1, "og": 1}, ring="B", jobs=1, freed=["og"], lay=lay, h=h, g=g,
                pbuf=order.index(2 * g) // 2 % 2, ready=max(pt_ready, v_ready), z_ld=z_ld)
        read_by["G"] = ("og", s.after["og"])
        return s

    def hproj(h, names):
        for j, name in enumerate(names):
            incs = {"b_full": 1, "hi": 1, "lo": 1}
            if name == "pe":
                incs["stage"] = 1
            s = add("hproj", incs, ring="B", jobs=1, freed=["lo"], h=h, name=name, j=j % 2,
                    w_ready=head_w[h], c_ready=lo_at["cT"], csq=marks["csq"])
        read_by["headW"] = ("b_full", s.after["b_full"])
        read_by["ring1"] = ("b_full", s.after["b_full"])
        return s.after["lo"]

    def z_load(lay, h):
        s = add("z_load", {"z_ld": 1}, lay=lay, h=h, reader=read_by.get("G"),
                stored=(now["z_st0"], now["z_st1"]))
        return s.after["z_ld"]

    qk_ready = hproj(0, ["q", "q", "pe", "pe", "k", "k"])
    v_ready = hproj(0, ["v", "v"])
    for h in range(HEADS):
        zl = z_load(0, h)
        more = h + 1 < HEADS
        if more:
            head_w[h + 1] = small_w("head_w", "headW", h=h + 1)
        pn, lo = {}, {}
        for i, qb in enumerate(order):
            ps = att["n"] % 3
            pn[i] = (s_step(0, h, qb, max(qk_ready, lo_at["kpeT"])), ps)
            if i in (5, 7):
                pv_step(0, h, order[i - 5] // 2, lo[i - 4], v_ready, zl)
            if i >= 2:
                lo[i - 2] = t_step(0, h, order[i - 2], *pn[i - 2])
        read_by["kpe"] = ("a_full", now["a_full"])
        if h:
            w(chunk_of(0, 4), h)
        if h == 1:
            w(chunk_of(0, 4), 0)
        if more:
            hproj(h + 1, ["q", "q"])
        t_step(0, h, order[6], *pn[6])
        if more:
            hproj(h + 1, ["pe", "pe"])
        lo[7] = t_step(0, h, order[7], *pn[7])
        pv_step(0, h, order[4] // 2, lo[5], v_ready, zl)
        if more:
            qk_ready = hproj(h + 1, ["k", "k"])
        pv_step(0, h, order[6] // 2, lo[7], v_ready, zl)
        if more:
            v_ready = hproj(h + 1, ["v", "v"])

    def tail(lay, wo0, last_gain, pa_reader):
        g1 = gain("ple%d" % lay).after["gain"]
        rows_free = now["b_full"]
        ppw = {}
        for t in range(T):
            s = add("og_split", {"hi": 1, "lo": 1}, t=t, act_free=now["b_full"])
            lo_at[("act", t)] = s.after["lo"]
        read_by["pst0"], read_by["pst1"] = pa_reader, pa_reader
        n = [0]

        def xin(t, j):
            return add("xin", {"xin%d" % (n[0] % 2): 1}, lay=lay, t=t, j=j, slot=n[0] % 2,
                       wait_add=(now["xadd"] - 1) if n[0] >= 2 else None, rows_free=rows_free,
                       x2=now["x2_st"])
        for j in range(2):
            prev, held = None, None
            for t in range(T):
                w(next_chunk(lay, wo0 + j), t)
                if j == 0 and t == 0:
                    ppw[0] = small_w("ple_w", "headW", lay=lay, j=0)
                if j == 0 and t == 2:
                    ppw[1] = small_w("ple_w", "kpe", lay=lay, j=1)
                x = xin(t, j)
                slot = n[0] % 2
                n[0] += 1
                s = proj(lay, wo0 + j, t, ["xadd"], {"xadd": 1}, slot=slot, xin=x.after["xin%d" % slot], j=j)
                if j == 1:
                    if prev:
                        norm_b(prev[0], 0, prev[1])
                    a = norm_a(t, 0, ("xadd", s.after["xadd"]), g1)
                    prev = (t, a.after["xn"])
        norm_b(prev[0], 0, prev[1])
        read_by["G"] = ("xn", now["xn"])
        g2 = gain(last_gain).after["gain"]
        gj = wo0 + 2
        n = 0
        p_at = {}

        def p_load(k):
            if k < 2 * T:
                slot = k % 2
                p_at[k] = add("p_load", {"p_ld%d" % slot: 1}, lay=lay, t=k % T, slot=slot,
                              reader=read_by["pst%d" % slot]).after["p_ld%d" % slot]
        p_load(0)
        for j in range(2):
            prev = None
            for t in range(T):
                p_load(n + 1)
                if next_chunk(lay, gj + j):
                    w(next_chunk(lay, gj + j), t)
                pslot = n % 2
                pt = add("p_split", {"b_full": 1, "hi": 1, "lo": 1}, ring="B", jobs=1,
                         freed=["lo"], lay=lay, t=t, slot=pslot, p_ld=p_at[n])
                read_by["pst%d" % pslot] = ("b_full", pt.after["b_full"])
                s = proj(lay, gj + j, t, ["sg"], {"sg": 1}, slot=n % 2, j=j,
                         wait_add=now["xadd"] - 1)
                q = add("pp", {"b_full": 1, "pp": 1, "xadd": 1}, ring="B", jobs=1, freed=["pp"],
                        t=t, j=j, slot=n % 2, ready=max(pt.after["lo"], 0), w_ready=ppw[j], sg=s.after["sg"])
                read_by["headW" if j == 0 else "kpe"] = ("b_full", q.after["b_full"])
                n += 1
                if j == 1 and lay == 0:
                    if prev:
                        norm_b(prev[0], 0, prev[1])
                    add("save_x", {"x2_st": 1}, t=t, ready=q.after["xadd"])
                    a = norm_a(t, 0, ("xadd", q.after["xadd"]), g2)
                    prev = (t, a.after["xn"])
                if j == 1 and lay == 1:
                    add("final", {"sq": 1, "rstd": 1, "fin": 1, "out_st": 1}, t=t,
                        ready=q.after["xadd"], gain=g2)
            if j == 1 and lay == 0:
                norm_b(prev[0], 0, prev[1])
        read_by["G"] = ("xn", now["xn"])

    cs = add("cs_load", {"cs_ld": 1}, pn=now["b_full"])
    tail(0, 4, "in1", ("lo", now["lo"]))

    def idx_scores(t, q_ready):
        keys = (t + 1) * P
        for h in range(0, IDX_HEADS, 2):
            for c in range((keys + CW - 1) // CW):
                n = min(CW, keys - c * CW)
                s = add("idx", {"b_full": 2, "relu": 2, "sc": 2}, ring="B", jobs=2, freed=["relu"],
                        t=t, h=h, c=c, n=n, q_ready=max(q_ready, lo_at["kiT"]), k=idx_n[0], x2=now["x2_st"],
                        gfree=read_by["G"])
                idx_n[0] += 2
        add("idx_mask", None, t=t)
    idx_n = [0]
    fk = [key_job(1, 0, job).after["fk"] for job in range(2)]
    for t in range(T):
        w(next_chunk(1, 0), t)

    def qi_job(t):
        w(next_chunk(1, 1), t)
        return rope_job(1, 1, t, t % 2, cs=cs.after["cs_ld"]).after["rot"]

    def qi_split(t, rot):
        return split4("p1", t % 2, ("rot", rot), dest="qiT", slot2=t % 2).after["lo"]
    w(next_chunk(1, 1), 0)
    w(next_chunk(1, 1), 1)
    rot = {FULL: qi_job(FULL)}
    rots = [key_back(1, job, fk[job]).after["rot"] for job in range(2)]
    for t in range(FULL, T):
        if t + 1 < T:
            rot[t + 1] = qi_job(t + 1)
        if t == FULL:
            for job in range(2):
                lo_at["kiT"] = key_split(1, job, rots[job])
        idx_scores(t, qi_split(t, rot[t]))
    read_by["G"] = ("sc", now["sc"])

    bits = [31 - i for i in range(32)]

    def search():
        if bits:
            st = add("bit", {"cand": 1, "tally": len(ACT_TILES)}, bit=bits.pop(0))
            for b in (6, 7):
                bank_free[b] = bank_free[b] + [("tally", st.after["tally"])]

    n = 0
    for i, name in ((2, "kv"), (3, "q"), (4, "q")):
        for t in range(T):
            w(next_chunk(1, i), t)
            slot = n % 2
            inc = {"st%d" % slot: 1}
            if name == "kv":
                inc["vcopy"] = 1
            rope_job(1, i, t, slot, extra_inc=inc, base=(i - 3) * CW, st_before=now["st%d" % slot])
            n += 1
            search()
    q_stored = (now["st0"], now["st1"])

    def t2_load(what, i, reader):
        return add("t2_load", {"t2_ld": 1}, what=what, i=i, reader=reader, stored=q_stored).after["t2_ld"]

    def q_prep(h, ld):
        s = None
        for j in range(2):
            s = split4("t2", 0, ("t2_ld", ld), dest="qT", slot2=h % 2, j=j)
        return s.after["lo"], ("b_full", s.after["b_full"])

    sel_done = []

    def z_extra(k):
        search()
        if not bits and len(sel_done) < SPREAD + 1 and k >= 8:
            if not sel_done:
                add("last_step", None)
                add("above", None)
                sel_done.append(-1)
            else:
                for _ in range(1):
                    if len(sel_done) <= SPREAD:
                        add("sel", {"found": 1}, t=FULL + len(sel_done) - 1)
                        sel_done.append(0)
    ld = t2_load("q", 0, ("b_full", now["b_full"]))
    k0 = add("k0_load", {"k0_ld": 1}, stored=q_stored)
    q_ready, rd = q_prep(0, ld)
    v0_ld = t2_load("v", 0, rd)
    wz = add("z_wait", {}, rot=now["rot"])
    z_chunk(1, 5, 0, 2, extra=z_extra)
    z_chunk(1, 6, CW, 2, prefetch=False, extra=z_extra)
    while len(sel_done) <= SPREAD:
        z_extra(99)
    read_by["G"] = ("found", now["found"])
    act_free = now["a_full"]
    k_ready, v_ready = {}, {}
    for j in range(2):
        k_ready[0] = split4("p1", 0, ("k0_ld", k0.after["k0_ld"]), dest="kT", g=0, j=j, whole=True).after["lo"]

    def v_prep(g, ld, act_free):
        s = add("v_split", {"hi": 1, "lo": 1}, g=g, ld=ld, act_free=act_free)
        v_ready[g] = s.after["lo"]
        return ("lo", s.after["lo"])
    rd = v_prep(0, v0_ld, act_free)

    waiting = []

    ready_pv = []

    def outputs():
        hh, g, lo = ready_pv.pop(0)
        pv_step(1, hh, g, lo, v_ready[hh // GROUP], zl[hh])
        if g == order[-1] // 2 and hh + 1 < HEADS:
            zl[hh + 1] = z_load(1, hh + 1)

    def transposes():
        hh, qq, pn, ps = waiting.pop(0)
        lo = t_step(1, hh, qq, pn, ps)
        if qq % 2:
            ready_pv.append((hh, qq // 2, lo))
    zl = {0: z_load(1, 0)}
    q_at = {0: q_ready}
    last_mask = None
    for h in range(HEADS):
        if h + 1 < HEADS:
            ld = t2_load("q", h + 1, rd)
        for i, qb in enumerate(order):
            if h == 0:
                for t in (order[0:3] if i == 0 else order[i + 2:i + 3]):
                    add("mask", None, t=t, a_full=act_free, first=t == order[0])
            ps = att["n"] % 3
            pn = s_step(1, h, qb, max(q_at[h], k_ready[h // GROUP]))
            waiting.append((h, qb, pn, ps))
            if ready_pv and i % 2:
                outputs()
            if len(waiting) > 2:
                transposes()
            if i == 3 and h + 1 < HEADS:
                q_at[h + 1], rd = q_prep(h + 1, ld)
                if h in (0, 1):
                    ld2 = t2_load("kv"[h], 1, rd)
            if i == 6 and h == 0:
                for j in range(2):
                    s = split4("t2", 0, ("t2_ld", ld2), dest="kT", g=1, j=j)
                k_ready[1] = s.after["lo"]
                rd = ("b_full", s.after["b_full"])
            if i == 6 and h == 1:
                rd = v_prep(1, ld2, act_free)
        w(chunk_of(1, 7), h)
    read_by["ring1"] = ("nb", now["nb"])
    read_by["headW"] = read_by["kpe"] = ("a_full", now["a_full"])
    outputs()
    transposes()
    transposes()
    outputs()
    tail(1, 7, "final", ("lo", now["lo"]))
    return steps, now


def build(nc, x, p, positions, norm_in, w_in0, q_norm, kv_norm, w_uq, w_uk, w_uv, w_out0, w_in1, w_out1,
          ple_proj, ple_norm, ple_gate, final_norm, freqs, out):
    steps, total = plan()
    weights = {"mla_in": w_in0, "dsa_in": w_in1, "out0": w_out0, "out1": w_out1,
               "gate0": ple_gate[0], "gate1": ple_gate[1]}
    gains = {"in0": norm_in[0:1, :], "in1": norm_in[1:2, :], "ple0": ple_norm[0:1, :], "ple1": ple_norm[1:2, :],
             "final": final_norm}

    with ExitStack() as ctx:
        def sb(name, cols, dt=F32):
            return ctx.enter_context(nc.sbuf_tensor(name, [P, cols], dt))

        act = [sb("act_hi", KD * S, F32R), sb("act_lo", KD * S, F32R)]
        ring = [sb("ring_hi", 2 * KD * CW, F32R), sb("ring_lo", 2 * KD * CW, F32R)]
        kpe = [sb("kpe_hi", S, F32R), sb("kpe_lo", S, F32R)]
        head_w = [sb("head_w_hi", 1024, F32R), sb("head_w_lo", 1024, F32R)]
        p_t = [sb("p_t_hi", PLE, F32R), sb("p_t_lo", PLE, F32R)]
        ident_r = sb("ident_r", P, F32R)
        tri_r = sb("tri_r", P, F32R)
        xr = sb("xr", T * D)
        raw = sb("raw", RAW_SLOTS * CW)
        p0 = sb("p0", 1024)
        p1 = sb("p1", 1024)
        cs = sb("cs", 1024)
        t2 = sb("t2", 1024)
        gz = sb("gz", 1024)
        ident = sb("ident", P)
        tri = sb("tri", P)
        small = sb("small", 128)
        pos_i = sb("pos_i", T, I32)
        frq = sb("frq", NFREQ)
        wis = sb("wis", T * IDX_HEADS)
        bits_u = sb("bits_u", 6 * SPREAD, U32)
        psum = ctx.enter_context(nc.psum_tensor("psum", [P, 8 * CW], F32))

        sem = {n: ctx.enter_context(nc.semaphore(n)) for n in DMA_SEMS + PLAIN_SEMS}
        z_dram = [nc.dram_tensor("z_scratch%d" % l, [D, S], F32, kind="Internal").ap() for l in range(2)]
        x2_dram = nc.dram_tensor("x2_scratch", [S, D], F32, kind="Internal").ap()
        q_dram = nc.dram_tensor("q_scratch", [S, D], F32, kind="Internal").ap()
        kv_dram = nc.dram_tensor("kv_scratch", [S, CW], F32, kind="Internal").ap()
        cs_dram = nc.dram_tensor("cs_scratch", [P, 1024], F32, kind="Internal").ap()

        ms = small[:, 0:8]
        mean = small[:, 8:16]
        rs = small[:, 16:24]
        lat_ms, lat_mean, lat_rs = small[:, 24:28], small[:, 28:32], small[:, 32:36]
        minus_half = small[:, 36:38]
        posf = small[:, 40:48]
        mx, nb, sm, ri = small[:, 48:51], small[:, 51:54], small[:, 54:57], small[:, 57:60]
        cnt = small[:, 64:64 + SPREAD]
        need = small[:, 72:72 + SPREAD]
        reach = small[:, 88:88 + SPREAD]
        u_bits, u_mask, u_cand, u_inc, u_minus, u_mask2 = (bits_u[:, k * SPREAD:(k + 1) * SPREAD] for k in range(6))
        rows = [p0, p1, cs]

        def bank(b, n=CW):
            return psum[:, b * CW:b * CW + n]

        def act_tile(part, t):
            return act[part][:].rearrange("p (d s) -> p d s", s=S)[:, :, t * P:(t + 1) * P]

        def act_at(part, d, c0, n):
            return act[part][:, d * S + c0:d * S + c0 + n]

        def w_at(part, buf, d, c0, n):
            if buf == SMALL:
                return head_w[part][:, d * P + c0:d * P + c0 + n]
            at = (buf * KD + d) * CW + c0
            return ring[part][:, at:at + n]

        CT0 = KD * CW
        PT0, V0, Q0, K0, PE0 = 0, 4096, 5120, 6144, 7168
        def pt_at(part, buf, kt, c0, n):
            at = PT0 + buf * 2048 + kt * 256 + c0
            return act[part][:, at:at + n]
        def pt_tiles(part, buf, qb, kt, kts):
            at = PT0 + buf * 2048 + kt * 256
            return act[part][:, at:at + kts * 256].rearrange("p (k c) -> p k c", c=256)[
                :, :, (qb % 2) * P:(qb % 2 + 1) * P]
        def region(part, at, c0, n):
            return act[part][:, at + c0:at + c0 + n]
        def kT1(part, g, c0, n):
            return act[part][:, 4096 + g * 1024 + c0:4096 + g * 1024 + c0 + n]
        def v1(part, g, c0, n):
            return act[part][:, 6144 + g * 1024 + c0:6144 + g * 1024 + c0 + n]
        def qT1(part, slot, c0, n):
            return (kpe, head_w)[slot][part][:, c0:c0 + n]
        def mask_at(t):
            if t < T - 1:
                return ring[0][:, KD * CW + SCORE_AT[t]:KD * CW + SCORE_AT[t + 1]]
            return ring[1][:, KD * CW:KD * CW + S]
        def score_at(t, c0=0, n=None):
            n = (t + 1) * P - c0 if n is None else n
            return xr[:, SCORE_AT[t] + c0:SCORE_AT[t] + c0 + n]

        def small_dest(s, part):
            k = s.n["piece"]
            w = head_w[part]
            if s.kind == "ple_w":
                return [((head_w if s.n["res"] == "headW" else kpe)[part][:, k * CW:(k + 1) * CW], 0, CW)]
            if k == 0:
                pairs = []
                for r in range(2):
                    pairs += [(w[:, r * 256:r * 256 + 192], r * 192, 192),
                              (w[:, r * 256 + 192:r * 256 + 224], r * 192 + 160, 32),
                              (w[:, r * 256 + 224:r * 256 + 256], r * 192 + 128, 32)]
                return pairs
            return [(w[:, 512:1024], 0, 512)]

        def split_dest(s, part):
            dest = s.n["dest"]
            if dest == "kpeT":
                ap = kpe[part][:, s.n["j"] * CW:(s.n["j"] + 1) * CW]
            elif dest == "cT":
                t = s.n["t"]
                return ring[part][:, CT0:CT0 + 4 * S].rearrange("p (f s) -> p f s", s=S)[:, :, t * P:(t + 1) * P]
            elif dest == "qiT":
                ap = head_w[part][:, s.n["slot2"] * CW:(s.n["slot2"] + 1) * CW]
            elif dest == "qT":
                ap = qT1(part, s.n["slot2"], s.n["j"] * CW, CW)
            else:
                ap = kT1(part, s.n["g"], s.n["j"] * CW, CW)
            return ap.rearrange("p (a b) -> p a b", b=P)

        def in4(ap):
            return ap.rearrange("p (a b) -> p a b", b=P)

        block = ctx.enter_context(nc.Block())

        @block.sync
        def _(sp):
            for s in steps:
                k, n = s.kind, s.n
                if k == "start":
                    sp.dma_start(frq[:], freqs.partition_broadcast(P)).then_inc(sem["const_ld"], 16)
                    sp.dma_start(pos_i[:], positions.rearrange("b (t p) -> p (b t)", p=P),
                                 allow_slow_non_contiguous=True).then_inc(sem["const_ld"], 16)
                    sp.dma_start(gz[:], gains["in0"].partition_broadcast(P)).then_inc(sem["gain"], 16)
                    sp.dma_start(t2[:, 0:RANK], q_norm.partition_broadcast(P)).then_inc(sem["lat_ld"], 16)
                    sp.dma_start(t2[:, RANK:2 * RANK], kv_norm.partition_broadcast(P)).then_inc(sem["lat_ld"], 16)
                elif k == "load_x":
                    t = n["t"]
                    sp.dma_start(xr[:, t * D:(t + 1) * D], x[t * P:(t + 1) * P, :]).then_inc(sem["x_ld%d" % t], 16)
                elif k in ("w", "w_first", "head_w", "ple_w"):
                    slot = n["g"] % RAW_SLOTS
                    if n["raw_free"]:
                        sp.wait_ge(sem[n["raw_free"][0]], n["raw_free"][1])
                    dst = raw[:, slot * CW:(slot + 1) * CW]
                    ld = sem["raw_ld%d" % slot]
                    if k in ("w", "w_first"):
                        d = n["d"]
                        sp.dma_start(dst[:, 0:n["cols"]],
                                     weights[n["src"]][d * P:(d + 1) * P, n["c0"]:n["c0"] + n["cols"]]).then_inc(ld, 16)
                    elif k == "ple_w":
                        r, j = n["piece"], n["j"]
                        sp.dma_start(dst, ple_proj[n["lay"], r * P:(r + 1) * P, j * CW:(j + 1) * CW]).then_inc(ld, 16)
                    elif n["piece"] == 0:
                        h = n["h"]
                        sp.dma_start(dst[:, 0:384].rearrange("p (r c) -> p r c", r=2),
                                     w_uq.rearrange("(r p) c -> p r c", p=P)[:, :, h * 192:(h + 1) * 192]).then_inc(ld, 16)
                    else:
                        h = n["h"]
                        sp.dma_start(dst.rearrange("p (q r c) -> p q r c", q=2, r=2)[:, 0],
                                     w_uk.rearrange("(r p) c -> p r c", p=P)[:, :, h * P:(h + 1) * P]).then_inc(ld, 16)
                        sp.dma_start(dst.rearrange("p (q r c) -> p q r c", q=2, r=2)[:, 1],
                                     w_uv.rearrange("(r p) c -> p r c", p=P)[:, :, h * P:(h + 1) * P]).then_inc(ld, 16)
                elif k == "gain":
                    sp.wait_ge(sem[n["reader"][0]], n["reader"][1])
                    sp.dma_start(gz[:], gains[n["which"]].partition_broadcast(P)).then_inc(sem["gain"], 16)
                elif k == "tables":
                    sp.wait_ge(sem["trig"], s.after["trig"])
                    sp.dma_start(cs_dram, cs[:]).then_inc(sem["cs_st"], 16)
                elif k == "cs_load":
                    sp.wait_ge(sem["b_full"], n["pn"])
                    sp.wait_ge(sem["cs_st"], 16)
                    sp.dma_start(cs[:], cs_dram).then_inc(sem["cs_ld"], 16)
                elif k == "proj" and n["name"] == "z":
                    sp.wait_ge(sem["zs"], s.after["zs"])
                    f = n["base"] + (n["job"] % 4) * P
                    half = n["job"] // 4
                    sp.dma_start(z_dram[n["lay"]][f:f + P, half * CW:(half + 1) * CW],
                                 (gz, p0)[n["lay"]][:, n["slot"] * CW:(n["slot"] + 1) * CW]).then_inc(sem["z_st%d" % n["slot"]], 16)
                elif k == "proj" and n["name"] in ("q", "kv"):
                    sp.wait_ge(sem["rot"], s.after["rot"])
                    if n["name"] == "kv":
                        sp.wait_ge(sem["vcopy"], s.after["vcopy"])
                    t = n["job"]
                    dst = (kv_dram[t * P:(t + 1) * P, :] if n["name"] == "kv"
                           else q_dram[t * P:(t + 1) * P, n["base"]:n["base"] + CW])
                    sp.dma_start(dst, p1[:, n["slot"] * CW:(n["slot"] + 1) * CW]).then_inc(sem["st%d" % n["slot"]], 16)
                elif k == "z_load":
                    sp.wait_ge(sem[n["reader"][0]], n["reader"][1])
                    sp.wait_ge(sem["z_st0"], n["stored"][0])
                    sp.wait_ge(sem["z_st1"], n["stored"][1])
                    h = n["h"]
                    sp.dma_start(gz[:], z_dram[n["lay"]][h * P:(h + 1) * P, :]).then_inc(sem["z_ld"], 16)
                elif k == "xin":
                    sp.wait_ge(sem["b_full"], n["rows_free"])
                    if n["wait_add"] is not None:
                        sp.wait_ge(sem["xadd"], n["wait_add"])
                    if n["lay"] == 1:
                        sp.wait_ge(sem["x2_st"], n["x2"])
                    t, j = n["t"], n["j"]
                    src = x if n["lay"] == 0 else x2_dram
                    sp.dma_start(p1[:, n["slot"] * CW:(n["slot"] + 1) * CW],
                                 src[t * P:(t + 1) * P, j * CW:(j + 1) * CW]).then_inc(sem["xin%d" % n["slot"]], 16)
                elif k == "p_load":
                    sp.wait_ge(sem[n["reader"][0]], n["reader"][1])
                    t = n["t"]
                    sp.dma_start(t2[:, n["slot"] * PLE:(n["slot"] + 1) * PLE],
                                 p[n["lay"], t * P:(t + 1) * P, :]).then_inc(sem["p_ld%d" % n["slot"]], 16)
                elif k == "save_x":
                    sp.wait_ge(sem["xadd"], n["ready"])
                    t = n["t"]
                    sp.dma_start(x2_dram[t * P:(t + 1) * P, :], xr[:, t * D:(t + 1) * D]).then_inc(sem["x2_st"], 16)
                elif k == "t2_load":
                    sp.wait_ge(sem[n["reader"][0]], n["reader"][1])
                    sp.wait_ge(sem["st0"], n["stored"][0])
                    sp.wait_ge(sem["st1"], n["stored"][1])
                    i = n["i"]
                    src = {"q": q_dram[:, i * P:(i + 1) * P] if n["what"] == "q" else None,
                           "k": kv_dram[:, (i % 2) * P:(i % 2) * P + P],
                           "v": kv_dram[:, 256 + (i % 2) * P:256 + (i % 2) * P + P]}[n["what"]]
                    sp.dma_start(t2[:].rearrange("p (t c) -> p t c", c=P),
                                 src.rearrange("(t p) c -> p t c", p=P)).then_inc(sem["t2_ld"], 16)
                elif k == "k0_load":
                    sp.wait_ge(sem["st0"], n["stored"][0])
                    sp.wait_ge(sem["st1"], n["stored"][1])
                    sp.dma_start(p1[:].rearrange("p (t c) -> p t c", c=P),
                                 kv_dram[:, 0:P].rearrange("(t p) c -> p t c", p=P)).then_inc(sem["k0_ld"], 16)
                elif k == "final":
                    sp.wait_ge(sem["fin"], s.after["fin"])
                    t = n["t"]
                    sp.dma_start(out[t * P:(t + 1) * P, :], xr[:, t * D:(t + 1) * D]).then_inc(sem["out_st"], 16)
            sp.wait_ge(sem["out_st"], total["out_st"])

        @block.gpsimd
        def _(pool):
            chain = [0]

            def linked(ins):
                chain[0] += 1
                ins.then_inc(sem["pool_chain"], 1)
                pool.wait_ge(sem["pool_chain"], chain[0])

            for s in steps:
                k, n = s.kind, s.n
                if k == "start":
                    linked(nc.gpsimd.memset(ident[:], 0.0))
                    linked(nc.gpsimd.affine_select(out=ident[:], in_=ident[:], compare_op=ALU.not_equal, fill=1.0,
                                                   base=0, pattern=[[-1, P]], channel_multiplier=1))
                    linked(nc.gpsimd.memset(tri[:], 0.0))
                    linked(nc.gpsimd.affine_select(out=tri[:], in_=tri[:], compare_op=ALU.is_ge, fill=NEG,
                                                   base=0, pattern=[[-1, P]], channel_multiplier=1))
                    linked(nc.gpsimd.tensor_copy(ident_r[:], ident[:]))
                    linked(nc.gpsimd.tensor_copy(tri_r[:], tri[:]))
                    nc.gpsimd.memset(minus_half, -0.5).then_inc(sem["consts"], 1)
                    pool.wait_ge(sem["consts"], 1)
                elif k in ("w", "head_w", "ple_w"):
                    slot = n["g"] % RAW_SLOTS
                    pool.wait_ge(sem["raw_ld%d" % slot], s.after["raw_ld%d" % slot])
                    if n["reader"]:
                        pool.wait_ge(sem[n["reader"][0]], n["reader"][1])
                    src = raw[:, slot * CW:(slot + 1) * CW]
                    if k == "w":
                        pairs = [[(w_at(part, n["buf"], n["d"], 0, n["cols"]), 0, n["cols"])] for part in range(2)]
                    else:
                        pairs = [small_dest(s, part) for part in range(2)]
                    for dst, c0, cols in pairs[0]:
                        last = nc.gpsimd.tensor_copy(dst, src[:, c0:c0 + cols])
                    linked(last)
                    for (dst, c0, cols), (hi, _, _) in zip(pairs[1], pairs[0]):
                        last = nc.gpsimd.tensor_tensor(dst, src[:, c0:c0 + cols], hi.bitcast(F32), ALU.subtract)
                    last.then_inc(sem["w"], 1)
                elif k == "R" and n["lay"] == 1:
                    row = rows[n["ps"]][:, 0:(n["qb"] + 1) * P]
                    pool.wait_ge(sem["ri"], s.after["ri"])
                    nc.gpsimd.tensor_scalar(row, row, ri[:, n["ps"]:n["ps"] + 1], 1.0, ALU.mult,
                                            ALU.mult).then_inc(sem["pn"], 1)
                elif k in ("norm_a", "final"):
                    t = n["t"]
                    pool.wait_ge(sem["sq"], s.after["sq"])
                    linked(nc.gpsimd.tensor_scalar(mean[:, t:t + 1], ms[:, t:t + 1], 1.0 / D, EPS, ALU.mult, ALU.add))
                    nc.gpsimd.tensor_tensor(rs[:, t:t + 1], mean[:, t:t + 1], minus_half[:, 0:1],
                                            ALU.pow).then_inc(sem["rstd"], 1)
                elif k == "proj" and n["name"] == "c":
                    c = 2 * n["slot"]
                    pool.wait_ge(sem["sq"], s.after["sq"])
                    linked(nc.gpsimd.tensor_scalar(lat_mean[:, c:c + 2], lat_ms[:, c:c + 2], 1.0 / RANK, EPS,
                                                   ALU.mult, ALU.add))
                    nc.gpsimd.tensor_tensor(lat_rs[:, c:c + 2], lat_mean[:, c:c + 2], minus_half,
                                            ALU.pow).then_inc(sem["rstd"], 1)

        @block.scalar
        def _(act_e):
            def split_hi(s, j, dst, src):
                act_e.wait_ge(sem["b_full"], s.before["b_full"] + j + 1)
                nc.scalar.activation(dst, src, ACT.Copy).then_inc(sem["hi"], 1)

            for s in steps:
                k, n = s.kind, s.n
                if k in ("norm_a", "final"):
                    t = n["t"]
                    act_e.wait_ge(sem[n["ready"][0]] if k == "norm_a" else sem["xadd"],
                                  n["ready"][1] if k == "norm_a" else n["ready"])
                    dst = rows[n["slot"] if k == "norm_a" else 0]
                    nc.scalar.activation(dst[:], xr[:, t * D:(t + 1) * D], ACT.Square,
                                         accum_out=ms[:, t:t + 1]).then_inc(sem["sq"], 1)
                elif k == "w_first":
                    slot = n["g"] % RAW_SLOTS
                    act_e.wait_ge(sem["raw_ld%d" % slot], s.after["raw_ld%d" % slot])
                    nc.scalar.activation(w_at(0, n["buf"], n["d"], 0, CW), raw[:, slot * CW:(slot + 1) * CW],
                                         ACT.Copy).then_inc(sem["w_hi"], 1)
                elif k == "norm_b":
                    t = n["t"]
                    for j in range(2):
                        split_hi(s, j, act_tile(0, t)[:, 4 * j:4 * j + 4, :], in4(bank(s.banks[j])))
                elif k == "split4":
                    split_hi(s, 0, split_dest(s, 0), in4(bank(s.banks[0])))
                elif k == "tables":
                    for i in range(2):
                        act_e.wait_ge(sem["stage"], s.before["stage"] + i + 1)
                        nc.scalar.activation(cs[:, (1 - i) * CW:(2 - i) * CW], p1[:, i * CW:(i + 1) * CW],
                                             ACT.Sin).then_inc(sem["trig"], 1)
                elif k == "table_t":
                    for j in range(2):
                        act_e.wait_ge(sem["b_full"], s.before["b_full"] + j + 1)
                        nc.scalar.activation(t2[:, j * CW:(j + 1) * CW], bank(s.banks[j]), ACT.Copy,
                                             scale=MLA_SCALE).then_inc(sem["csq"], 1)
                elif k == "bit":
                    act_e.wait_ge(sem["cand"], s.after["cand"])
                    act_e.wait_ge(sem["lo"], s.before["lo"])
                    for t in ACT_TILES:
                        i = SEARCH.index(t)
                        if s.before["tally"] or t != ACT_TILES[0]:
                            act_e.wait_ge(sem["tally"], s.before["tally"] + ACT_TILES.index(t))
                        nc.scalar.activation(bank(6, (t + 1) * P), score_at(t), ACT.Sign,
                                             bias=u_minus.bitcast(F32)[:, i:i + 1],
                                             accum_out=cnt[:, i:i + 1]).then_inc(sem["tally"], 1)
                elif k == "z_wait":
                    act_e.wait_ge(sem["rot"], n["rot"])
                elif k == "proj":
                    name, b = n["name"], s.banks[0]
                    if name == "z":
                        slot = n["slot"]
                        act_e.wait_ge(sem["a_full"], s.after["a_full"])
                        if s.before["z_st%d" % slot]:
                            act_e.wait_ge(sem["z_st%d" % slot], s.before["z_st%d" % slot])
                        nc.scalar.activation((gz, p0)[n["lay"]][:, slot * CW:(slot + 1) * CW], bank(b),
                                             ACT.Silu).then_inc(sem["zs"], 1)
                    elif name in ("kpe", "kiwi"):
                        act_e.wait_ge(sem["a_full"], s.after["a_full"])
                        if name == "kpe":
                            act_e.wait_ge(sem["trig"], s.before["trig"])
                        else:
                            act_e.wait_ge(sem["xn"], s.before["xn"])
                        nc.scalar.activation((p1, gz)[n["lay"]][:, n["slot"] * CW:(n["slot"] + 1) * CW], bank(b),
                                             ACT.Copy).then_inc(sem["fk"], 1)
                    elif name == "c":
                        act_e.wait_ge(sem["a_full"], s.after["a_full"])
                        for r in range(2):
                            c = n["job"] * D + CW + r * RANK
                            nc.scalar.activation(xr[:, c:c + RANK], bank(b)[:, r * RANK:(r + 1) * RANK], ACT.Square,
                                                 accum_out=lat_ms[:, 2 * n["slot"] + r:2 * n["slot"] + r + 1]).then_inc(sem["sq"], 1)
                    elif name == "gate":
                        act_e.wait_ge(sem["a_full"], s.after["a_full"])
                        act_e.wait_ge(sem["xadd"], n["wait_add"])
                        nc.scalar.activation(p1[:, n["slot"] * CW:(n["slot"] + 1) * CW], bank(b),
                                             ACT.Sigmoid).then_inc(sem["sg"], 1)
                    elif name == "kv":
                        act_e.wait_ge(sem["a_full"], s.after["a_full"])
                        if n["st_before"]:
                            act_e.wait_ge(sem["st%d" % n["slot"]], n["st_before"])
                        c = n["slot"] * CW + 256
                        nc.scalar.activation(p1[:, c:c + 256], bank(b)[:, 256:512], ACT.Copy).then_inc(sem["vcopy"], 1)
                elif k == "p_split":
                    split_hi(s, 0, p_t[0][:], bank(s.banks[0], PLE))
                elif k == "hproj":
                    b, j, name = s.banks[0], n["j"], n["name"]
                    if name == "pe":
                        act_e.wait_ge(sem["stage"], s.after["stage"])
                    at = {"q": Q0, "pe": PE0, "k": K0, "v": V0}[name]
                    act_e.wait_ge(sem["b_full"], s.after["b_full"])
                    nc.scalar.activation(region(0, at, j * CW, CW), bank(b), ACT.Copy,
                                         scale=MLA_SCALE if name == "q" else 1.0).then_inc(sem["hi"], 1)
                elif k == "idx":
                    for j in range(2):
                        act_e.wait_ge(sem["b_full"], s.before["b_full"] + j + 1)
                        if n["k"]:
                            act_e.wait_ge(sem["sc"], s.before["sc"] + j - 1)
                        elif j == 0:
                            act_e.wait_ge(sem[n["gfree"][0]], n["gfree"][1])
                        nc.scalar.activation(gz[:, j * CW:j * CW + n["n"]], bank(s.banks[j], n["n"]), ACT.Relu,
                                             scale=IDX_SCALE).then_inc(sem["relu"], 1)
                elif k == "S":
                    ps, keys = n["ps"], (n["qb"] + 1) * P
                    src = bank(s.banks[0], keys) if n["lay"] == 0 else rows[ps][:, 0:keys]
                    act_e.wait_ge(sem["nb"], s.after["nb"])
                    if n["lay"] == 0 and ps == 2:
                        act_e.wait_ge(sem["cs_st"], 16)
                    nc.scalar.activation(rows[ps][:, 0:keys], src, ACT.Exp, bias=nb[:, ps:ps + 1],
                                         scale=1.0 if n["lay"] == 0 else -1.0,
                                         accum_out=sm[:, ps:ps + 1]).then_inc(sem["ex"], 1)
                elif k == "R" and n["lay"] == 0:
                    ps, keys = n["ps"], (n["qb"] + 1) * P
                    act_e.wait_ge(sem["ri"], s.after["ri"])
                    nc.scalar.activation(rows[ps][:, 0:keys], rows[ps][:, 0:keys], ACT.Copy,
                                         scale=ri[:, ps:ps + 1]).then_inc(sem["pn"], 1)
                elif k == "T":
                    for j, b in enumerate(s.banks):
                        kts = min(4, n["qb"] + 1 - 4 * j)
                        split_hi(s, j, pt_tiles(0, n["pbuf"], n["qb"], 4 * j, kts), in4(bank(b, kts * P)))
                elif k == "og_split":
                    t = n["t"]
                    act_e.wait_ge(sem["og"], s.after["og"])
                    act_e.wait_ge(sem["b_full"], n["act_free"])
                    nc.scalar.activation(act_tile(0, t), in4(xr[:, t * D:(t + 1) * D]), ACT.Copy).then_inc(sem["hi"], 1)
                elif k == "v_split":
                    act_e.wait_ge(sem["t2_ld"], n["ld"])
                    act_e.wait_ge(sem["a_full"], n["act_free"])
                    nc.scalar.activation(v1(0, n["g"], 0, S), t2[:], ACT.Copy).then_inc(sem["hi"], 1)

        @block.vector
        def _(dve):
            chain = [0]

            def linked(ins):
                chain[0] += 1
                ins.then_inc(sem["dve_chain"], 1)
                dve.wait_ge(sem["dve_chain"], chain[0])

            def split_lo(s, j, dst, src, hi):
                dve.wait_ge(sem["hi"], s.before["hi"] + j + 1)
                nc.vector.tensor_tensor(dst, src, hi.bitcast(F32), ALU.subtract).then_inc(sem["lo"], 1)

            def rotate(s, src, groups, half, c_ap, s_ap, dsts):
                pa = p0[:, 0:2 * groups * half].rearrange("p (g u e) -> p g u e", u=2, e=half)
                pb = p0[:, CW:CW + 2 * groups * half].rearrange("p (g u e) -> p g u e", u=2, e=half)
                if s.before["rot"]:
                    dve.wait_ge(sem["rot"], s.before["rot"])
                nc.vector.tensor_tensor(pa, src, c_ap, ALU.mult)
                nc.vector.tensor_tensor(pb, src, s_ap, ALU.mult).then_inc(sem["rot_in"], 1)
                dve.wait_ge(sem["rot_in"], s.after["rot_in"])
                for dst in dsts:
                    nc.vector.tensor_tensor(dst[:, :, 0, :], pa[:, :, 0, :], pb[:, :, 1, :], ALU.subtract)
                    last = nc.vector.tensor_tensor(dst[:, :, 1, :], pa[:, :, 1, :], pb[:, :, 0, :], ALU.add)
                last.then_inc(sem["rot"], 1)

            cos_all = cs[:, 0:CW].rearrange("p (t e) -> p t e", e=HALF)
            sin_all = cs[:, CW:2 * CW].rearrange("p (t e) -> p t e", e=HALF)

            def trig_tile(tab, t, step, groups):
                v = tab[:, t, 0::step]
                return v.unsqueeze(1).unsqueeze(1).to_broadcast([P, groups, 2, HALF // step])

            def trig_tiles(tab, t0):
                v = tab[:, t0:t0 + 4, 0::2]
                return v.unsqueeze(2).to_broadcast([P, 4, 2, HALF // 2])

            for s in steps:
                k, n = s.kind, s.n
                if k == "norm_a":
                    t, slot = n["t"], n["slot"]
                    dve.wait_ge(sem["rstd"], s.after["rstd"])
                    dve.wait_ge(sem["gain"], n["gain"])
                    nc.vector.scalar_tensor_tensor(rows[slot][:], xr[:, t * D:(t + 1) * D], rs[:, t:t + 1], gz[:],
                                                   ALU.mult, ALU.mult).then_inc(sem["xn"], 1)
                elif k == "w_first":
                    slot = n["g"] % RAW_SLOTS
                    dve.wait_ge(sem["w_hi"], s.after["w_hi"])
                    nc.vector.tensor_tensor(w_at(1, n["buf"], n["d"], 0, CW), raw[:, slot * CW:(slot + 1) * CW],
                                            w_at(0, n["buf"], n["d"], 0, CW).bitcast(F32),
                                            ALU.subtract).then_inc(sem["w0"], 1)
                elif k == "final":
                    t = n["t"]
                    dve.wait_ge(sem["rstd"], s.after["rstd"])
                    dve.wait_ge(sem["gain"], n["gain"])
                    rw = xr[:, t * D:(t + 1) * D]
                    nc.vector.scalar_tensor_tensor(rw, rw, rs[:, t:t + 1], gz[:], ALU.mult, ALU.mult).then_inc(sem["fin"], 1)
                elif k == "norm_b":
                    t = n["t"]
                    for j in range(2):
                        split_lo(s, j, act_tile(1, t)[:, 4 * j:4 * j + 4, :], in4(bank(s.banks[j])),
                                 act_tile(0, t)[:, 4 * j:4 * j + 4, :])
                elif k == "split4":
                    split_lo(s, 0, split_dest(s, 1), in4(bank(s.banks[0])), split_dest(s, 0))
                elif k == "tables":
                    c1, c2, c3 = two_pi_parts()
                    ang, turns, back = p1[:, 0:CW], p1[:, CW:2 * CW], t2[:, 0:CW]
                    dve.wait_ge(sem["const_ld"], 32)
                    dve.wait_ge(sem["hi"], s.before["hi"])
                    dve.wait_ge(sem["xn"], s.before["xn"])
                    linked(nc.vector.tensor_copy(posf, pos_i[:]))
                    ang = t2[:, CW:2 * CW]
                    for t in range(T):
                        last = nc.vector.tensor_scalar(ang[:, t * NFREQ:(t + 1) * NFREQ], frq[:], posf[:, t:t + 1],
                                                       None, ALU.mult)
                    linked(last)
                    for i in range(2):
                        turns = p1[:, i * CW:(i + 1) * CW]
                        linked(nc.vector.tensor_scalar(turns, ang, 1.0 / TWO_PI, 0.25 * i, ALU.mult, ALU.add))
                        linked(nc.vector.tensor_scalar(turns, turns, 12582912.0, -12582912.0, ALU.add, ALU.add))
                        linked(nc.vector.scalar_tensor_tensor(back, turns, -c1, ang, ALU.mult, ALU.add))
                        linked(nc.vector.scalar_tensor_tensor(back, turns, -c2, back, ALU.mult, ALU.add))
                        linked(nc.vector.scalar_tensor_tensor(back, turns, -c3, back, ALU.mult, ALU.add))
                        nc.vector.tensor_scalar(turns, back, 0.25 * i * TWO_PI, None, ALU.add).then_inc(sem["stage"], 1)
                elif k == "table_t":
                    dve.wait_ge(sem["hi"], s.before["hi"])
                    for j in range(2):
                        st = p1[:, j * CW:(j + 1) * CW].rearrange("p (t u e) -> p t u e", t=4, u=4)
                        co, si = cos_all[:, 4 * j:4 * j + 4, 0::2], sin_all[:, 4 * j:4 * j + 4, 0::2]
                        nc.vector.tensor_copy(st[:, :, 0, :], co)
                        nc.vector.tensor_copy(st[:, :, 1, :], co)
                        nc.vector.tensor_scalar(st[:, :, 2, :], si, -1.0, None, ALU.mult)
                        nc.vector.tensor_copy(st[:, :, 3, :], si).then_inc(sem["stage"], 1)
                elif k == "proj":
                    name, b = n["name"], s.banks[0]
                    if name in ("qi", "kv", "q"):
                        dve.wait_ge(sem["a_full"], s.after["a_full"])
                        slot, job = n["slot"], n["job"]
                        st = p1[:, slot * CW:(slot + 1) * CW]
                        if name == "qi":
                            dve.wait_ge(sem["cs_ld"], n["cs"])
                            dve.wait_ge(sem["hi"], s.before["hi"])
                            rotate(s, bank(b).rearrange("p (g u e) -> p g u e", u=2, e=32), 8, 32,
                                   trig_tile(cos_all, job, 2, 8), trig_tile(sin_all, job, 2, 8),
                                   [st.rearrange("p (g u e) -> p g u e", u=2, e=32)])
                        else:
                            g = 4 if name == "q" else 2
                            if name == "kv":
                                dve.wait_ge(sem["vcopy"], s.after["vcopy"])
                            if n["st_before"]:
                                dve.wait_ge(sem["st%d" % slot], n["st_before"])
                            rotate(s, bank(b, g * HD).rearrange("p (g u e) -> p g u e", u=2, e=HALF), g, HALF,
                                   trig_tile(cos_all, job, 1, g), trig_tile(sin_all, job, 1, g),
                                   [st[:, 0:g * HD].rearrange("p (g u e) -> p g u e", u=2, e=HALF)])
                    elif name == "c":
                        dve.wait_ge(sem["rstd"], s.after["rstd"])
                        dve.wait_ge(sem["lat_ld"], 32)
                        for r in range(2):
                            c = n["job"] * D + r * RANK
                            last = nc.vector.scalar_tensor_tensor(
                                xr[:, c:c + RANK], bank(b)[:, r * RANK:(r + 1) * RANK],
                                lat_rs[:, 2 * n["slot"] + r:2 * n["slot"] + r + 1], t2[:, r * RANK:(r + 1) * RANK],
                                ALU.mult, ALU.mult)
                        last.then_inc(sem["xn"], 1)
                    elif name == "wo":
                        dve.wait_ge(sem["a_full"], s.after["a_full"])
                        dve.wait_ge(sem["xin%d" % n["slot"]], n["xin"])
                        c = n["job"] * D + n["j"] * CW
                        nc.vector.tensor_tensor(xr[:, c:c + CW], bank(b), p1[:, n["slot"] * CW:(n["slot"] + 1) * CW],
                                                ALU.add).then_inc(sem["xadd"], 1)
                elif k == "key_back":
                    b, job = s.banks[0], n["job"]
                    dve.wait_ge(sem["b_full"], s.after["b_full"])
                    if n["lay"] == 0:
                        dve.wait_ge(sem["trig"], n["trig"])
                    v = in4(bank(b))
                    if n["lay"] == 1:
                        nc.vector.tensor_scalar(
                            wis[:].rearrange("p (t h) -> p t h", h=IDX_HEADS)[:, 4 * job:4 * job + 4, :],
                            v[:, :, IDX_DIM:IDX_DIM + IDX_HEADS], W_IDX_SCALE, None, ALU.mult).then_inc(sem["widx"], 1)
                    dup = (p1, t2)[n["lay"]][:, job * CW:(job + 1) * CW].rearrange(
                        "p (t r u e) -> p t r u e", t=4, r=2, u=2)
                    rotate(s, v[:, :, 0:64].rearrange("p t (u e) -> p t u e", u=2), 4, 32,
                           trig_tiles(cos_all, 4 * job), trig_tiles(sin_all, 4 * job),
                           [dup[:, :, r] for r in range(2)])
                elif k == "pp":
                    dve.wait_ge(sem["sg"], n["sg"])
                    dve.wait_ge(sem["b_full"], s.after["b_full"])
                    st = p1[:, n["slot"] * CW:(n["slot"] + 1) * CW]
                    nc.vector.tensor_tensor(st, bank(s.banks[0]), st, ALU.mult).then_inc(sem["pp"], 1)
                    dve.wait_ge(sem["pp"], s.after["pp"])
                    c = n["t"] * D + n["j"] * CW
                    nc.vector.tensor_tensor(xr[:, c:c + CW], xr[:, c:c + CW], st, ALU.add).then_inc(sem["xadd"], 1)
                elif k == "p_split":
                    split_lo(s, 0, p_t[1][:], bank(s.banks[0], PLE), p_t[0][:])
                elif k == "hproj":
                    b, j, name = s.banks[0], n["j"], n["name"]
                    if name == "pe":
                        dve.wait_ge(sem["b_full"], s.after["b_full"])
                        dve.wait_ge(sem["csq"], n["csq"])
                        nc.vector.tensor_tensor(bank(b), bank(b), t2[:, j * CW:(j + 1) * CW],
                                                ALU.mult).then_inc(sem["stage"], 1)
                    at = {"q": Q0, "pe": PE0, "k": K0, "v": V0}[name]
                    if name == "q":
                        dve.wait_ge(sem["hi"], s.after["hi"])
                        nc.vector.scalar_tensor_tensor(region(1, at, j * CW, CW), bank(b), MLA_SCALE,
                                                       region(0, at, j * CW, CW).bitcast(F32),
                                                       ALU.mult, ALU.subtract).then_inc(sem["lo"], 1)
                    else:
                        split_lo(s, 0, region(1, at, j * CW, CW), bank(b), region(0, at, j * CW, CW))
                elif k == "idx":
                    t = n["t"]
                    dst = score_at(t, n["c"] * CW, n["n"])
                    for j in range(2):
                        h = n["h"] + j
                        dve.wait_ge(sem["relu"], s.before["relu"] + j + 1)
                        if n["k"] + j == 0:
                            dve.wait_ge(sem["x2_st"], n["x2"])
                        else:
                            dve.wait_ge(sem["sc"], s.before["sc"] + j)
                        src = gz[:, j * CW:j * CW + n["n"]]
                        wcol = wis[:, t * IDX_HEADS + h:t * IDX_HEADS + h + 1]
                        if h == 0:
                            nc.vector.tensor_scalar(dst, src, wcol, None, ALU.mult).then_inc(sem["sc"], 1)
                        else:
                            nc.vector.scalar_tensor_tensor(dst, src, wcol, dst, ALU.mult, ALU.add).then_inc(sem["sc"], 1)
                elif k == "idx_mask":
                    dve.wait_ge(sem["sc"], s.after["sc"])
                    dst = score_at(n["t"], n["t"] * P, P)
                    linked(nc.vector.tensor_tensor(dst, dst, tri[:], ALU.add))
                elif k == "bit":
                    bit = n["bit"]
                    cand = u_cand.bitcast(F32)
                    if bit == 31:
                        linked(nc.vector.memset(cand, 0.0))
                        for i, t in enumerate(SEARCH):
                            linked(nc.vector.memset(reach[:, i:i + 1],
                                                    2.0 * TOPK - (t + 1) * P if t in ACT_TILES else float(TOPK)))
                        nc.vector.memset(u_minus.bitcast(F32), 0.0).then_inc(sem["cand"], 1)
                    else:
                        linked(nc.vector.scalar_tensor_tensor(u_cand, u_bits, 1 << bit, u_mask,
                                                              ALU.bitwise_or, ALU.bitwise_xor))
                        nc.vector.scalar_tensor_tensor(u_minus, u_bits, 1 << bit, u_mask2,
                                                       ALU.bitwise_or, ALU.bitwise_xor).then_inc(sem["cand"], 1)
                    for i, t in enumerate(SEARCH):
                        if t not in ACT_TILES:
                            linked(nc.vector.tensor_scalar(gz[:, 0:(t + 1) * P], score_at(t), cand[:, i:i + 1], 0.0,
                                                           ALU.is_ge, ALU.add, accum_out=cnt[:, i:i + 1]))
                    dve.wait_ge(sem["tally"], s.after["tally"])
                    linked(nc.vector.tensor_tensor(u_inc, cnt, reach, ALU.is_ge))
                    if bit == 31:
                        linked(nc.vector.tensor_scalar(u_bits, u_inc, 31, None, ALU.logical_shift_left))
                        um, um2 = u_mask.bitcast(I32), u_mask2.bitcast(I32)
                        linked(nc.vector.tensor_scalar(um2, u_bits.bitcast(I32), -(1 << 31), 31,
                                                       ALU.bitwise_xor, ALU.arith_shift_right))
                        linked(nc.vector.tensor_scalar(um, um2, -(1 << 31), None, ALU.bitwise_or))
                        linked(nc.vector.tensor_scalar(um2, um, -(1 << 31), None, ALU.bitwise_xor))
                    else:
                        linked(nc.vector.scalar_tensor_tensor(u_bits, u_inc, bit, u_bits,
                                                              ALU.logical_shift_left, ALU.bitwise_or))
                elif k == "last_step":
                    linked(nc.vector.tensor_scalar(u_inc, u_bits, 0xFFFF, None, ALU.bitwise_and))
                    linked(nc.vector.tensor_scalar(u_cand, u_bits, 16, None, ALU.logical_shift_right))
                    linked(nc.vector.tensor_scalar(u_inc, u_inc, 1.0, None, ALU.add))
                    linked(nc.vector.tensor_scalar(u_minus, u_inc, 16, None, ALU.logical_shift_right))
                    linked(nc.vector.tensor_tensor(u_cand, u_cand, u_minus, ALU.add))
                    linked(nc.vector.tensor_scalar(u_inc, u_inc, 0xFFFF, None, ALU.bitwise_and))
                    linked(nc.vector.scalar_tensor_tensor(u_minus, u_cand, 16, u_inc,
                                                          ALU.logical_shift_left, ALU.bitwise_or))
                    linked(nc.vector.tensor_tensor(u_cand, u_minus, u_mask, ALU.bitwise_xor))
                    for i, t in enumerate(SEARCH):
                        linked(nc.vector.tensor_scalar(gz[:, 0:(t + 1) * P], score_at(t),
                                                       u_cand.bitcast(F32)[:, i:i + 1], 0.0,
                                                       ALU.is_ge, ALU.add, accum_out=cnt[:, i:i + 1]))
                    linked(nc.vector.tensor_scalar(u_inc, cnt, TOPK - 0.5, None, ALU.is_gt))
                    linked(nc.vector.tensor_scalar(u_inc.bitcast(I32), u_inc.bitcast(I32), 31, 31,
                                                   ALU.logical_shift_left, ALU.arith_shift_right))
                    linked(nc.vector.tensor_tensor(u_minus, u_minus, u_bits, ALU.bitwise_xor))
                    linked(nc.vector.tensor_tensor(u_minus, u_minus, u_inc, ALU.bitwise_and))
                    linked(nc.vector.tensor_tensor(u_bits, u_bits, u_minus, ALU.bitwise_xor))
                elif k == "above":
                    linked(nc.vector.tensor_tensor(u_cand, u_bits, u_mask, ALU.bitwise_xor))
                    thr = u_cand.bitcast(F32)
                    for i, t in enumerate(SEARCH):
                        linked(nc.vector.tensor_scalar(gz[:, 0:(t + 1) * P], score_at(t), thr[:, i:i + 1], 0.0,
                                                        ALU.is_gt, ALU.add, accum_out=cnt[:, i:i + 1]))
                    linked(nc.vector.tensor_scalar(need, cnt, -1.0, float(TOPK), ALU.mult, ALU.add))
                elif k == "sel":
                    t = n["t"]
                    i, keys = SEARCH.index(t), (t + 1) * P
                    thr = u_cand.bitcast(F32)[:, i:i + 1]
                    eq, order = gz[:, 0:keys], cs[:, 0:keys]
                    if t > FULL:
                        dve.wait_ge(sem["found"], s.before["found"])
                    linked(nc.vector.tensor_scalar(eq, score_at(t), thr, None, ALU.is_equal))
                    linked(nc.vector.tensor_tensor_scan(order, eq, eq, 0.0, ALU.add, ALU.max))
                    linked(nc.vector.scalar_tensor_tensor(eq, order, need[:, i:i + 1], eq, ALU.is_le, ALU.mult))
                    nc.vector.scalar_tensor_tensor(score_at(t), score_at(t), thr, eq, ALU.is_gt,
                                                   ALU.add).then_inc(sem["found"], 1)
                elif k == "mask":
                    t = n["t"]
                    if n["first"]:
                        dve.wait_ge(sem["a_full"], n["a_full"])
                        dve.wait_ge(sem["found"], s.before["found"])
                        dve.wait_ge(sem["z_st0"], s.before["z_st0"])
                        dve.wait_ge(sem["z_st1"], s.before["z_st1"])
                    if t < FULL:
                        if t:
                            nc.vector.memset(mask_at(t)[:, 0:t * P].bitcast(F32), 0.0)
                        linked(nc.vector.tensor_copy(mask_at(t)[:, t * P:(t + 1) * P], tri[:]))
                    else:
                        linked(nc.vector.tensor_scalar(mask_at(t), score_at(t), -1.0, -NEG, ALU.add, ALU.mult))
                elif k == "S":
                    ps, keys = n["ps"], (n["qb"] + 1) * P
                    dve.wait_ge(sem["a_full"], s.after["a_full"])
                    src = bank(s.banks[0], keys)
                    if n["lay"] == 0:
                        nc.vector.tensor_reduce(nb[:, ps:ps + 1], src, AX_X, ALU.max, negate=True).then_inc(sem["nb"], 1)
                    else:
                        nc.vector.tensor_tensor_reduce(rows[ps][:, 0:keys], src, mask_at(n["qb"]).bitcast(F32),
                                                       -DSA_SCALE, 3.4e38, ALU.add, ALU.min,
                                                       nb[:, ps:ps + 1]).then_inc(sem["nb"], 1)
                elif k == "R":
                    ps = n["ps"]
                    dve.wait_ge(sem["ex"], n["ex"])
                    nc.vector.reciprocal(ri[:, ps:ps + 1], sm[:, ps:ps + 1]).then_inc(sem["ri"], 1)
                elif k == "T":
                    for j, b in enumerate(s.banks):
                        kts = min(4, n["qb"] + 1 - 4 * j)
                        parts = [pt_tiles(part, n["pbuf"], n["qb"], 4 * j, kts) for part in range(2)]
                        split_lo(s, j, parts[1], in4(bank(b, kts * P)), parts[0])
                elif k == "PV":
                    h, g = n["h"], n["g"]
                    dve.wait_ge(sem["b_full"], s.after["b_full"])
                    dve.wait_ge(sem["z_ld"], n["z_ld"])
                    dst = xr[:].rearrange("p (t c) -> p t c", c=D)[:, 2 * g:2 * g + 2, h * P:(h + 1) * P]
                    nc.vector.tensor_tensor(dst, in4(bank(s.banks[0], 256)), in4(gz[:, g * 256:(g + 1) * 256]),
                                            ALU.mult).then_inc(sem["og"], 1)
                elif k == "og_split":
                    t = n["t"]
                    dve.wait_ge(sem["hi"], s.after["hi"])
                    nc.vector.tensor_tensor(act_tile(1, t), in4(xr[:, t * D:(t + 1) * D]), act_tile(0, t).bitcast(F32),
                                            ALU.subtract).then_inc(sem["lo"], 1)
                elif k == "v_split":
                    dve.wait_ge(sem["hi"], s.after["hi"])
                    nc.vector.tensor_tensor(v1(1, n["g"], 0, S), t2[:], v1(0, n["g"], 0, S).bitcast(F32),
                                            ALU.subtract).then_inc(sem["lo"], 1)

        @block.tensor
        def _(pe):
            def product(dst, lhs, rhs, start, stop):
                nc.tensor.matmul(dst, lhs(1), rhs(0), start=start, stop=False)
                nc.tensor.matmul(dst, lhs(0), rhs(1), start=False, stop=False)
                return nc.tensor.matmul(dst, lhs(0), rhs(0), start=False, stop=stop)

            def bank_free(s, j=0):
                for name, v in s.free[j]:
                    pe.wait_ge(sem[name], v)

            for s in steps:
                k, n = s.kind, s.n
                if k == "norm_b":
                    pe.wait_ge(sem["xn"], n["xn"])
                    pe.wait_ge(sem["consts"], 1)
                    for j in range(2):
                        bank_free(s, j)
                        for i in range(4):
                            c = (4 * j + i) * P
                            last = nc.tensor.transpose(bank(s.banks[j])[:, i * P:(i + 1) * P],
                                                       rows[n["slot"]][:, c:c + P], ident[:])
                        last.then_inc(sem["b_full"], 1)
                elif k == "split4":
                    pe.wait_ge(sem[n["ready"][0]], n["ready"][1])
                    bank_free(s)
                    if n["src"] == "xr":
                        src = xr[:, n["t"] * D:n["t"] * D + CW]
                    elif n["src"] == "t2" or n.get("whole"):
                        src = (t2 if n["src"] == "t2" else p1)[:, n["j"] * CW:(n["j"] + 1) * CW]
                    else:
                        src = p1[:, n["slot"] * CW:(n["slot"] + 1) * CW]
                    for i in range(4):
                        last = nc.tensor.transpose(bank(s.banks[0])[:, i * P:(i + 1) * P], src[:, i * P:(i + 1) * P],
                                                   ident[:])
                    last.then_inc(sem["b_full"], 1)
                elif k == "key_back":
                    pe.wait_ge(sem["fk"], n["fk"])
                    bank_free(s)
                    for i in range(4):
                        c = n["job"] * CW + i * P
                        last = nc.tensor.transpose(bank(s.banks[0])[:, i * P:(i + 1) * P],
                                                   (p1, gz)[n["lay"]][:, c:c + P], ident[:])
                    last.then_inc(sem["b_full"], 1)
                elif k == "table_t":
                    for j in range(2):
                        pe.wait_ge(sem["stage"], s.before["stage"] + 1 + j)
                        bank_free(s, j)
                        for i in range(4):
                            c = j * CW + i * P
                            last = nc.tensor.transpose(bank(s.banks[j])[:, i * P:(i + 1) * P], p1[:, c:c + P], ident[:])
                        last.then_inc(sem["b_full"], 1)
                elif k == "proj":
                    name, b, buf = n["name"], s.banks[0], n["buf"]
                    bank_free(s)
                    pe.wait_ge(sem["lo"], n["act"])
                    if n["half"] is not None:
                        half, m = n["half"], n["job"] % 4 if name == "z" else 0
                        for d in range(KD):
                            pe.wait_ge(sem[n["w_ready"][d][0]], n["w_ready"][d][1])
                            last = product(bank(b), lambda part: w_at(part, buf, d, m * P, P),
                                           lambda part: act_at(part, d, half * CW, CW), d == 0, d == KD - 1)
                    else:
                        t = n["job"]
                        for d in range(KD):
                            pe.wait_ge(sem[n["w_ready"][d][0]], n["w_ready"][d][1])
                            last = product(bank(b), lambda part: act_at(part, d, t * P, P),
                                           lambda part: w_at(part, buf, d, 0, CW), d == 0, d == KD - 1)
                    last.then_inc(sem["a_full"], 1)
                elif k == "p_split":
                    pe.wait_ge(sem["p_ld%d" % n["slot"]], n["p_ld"])
                    bank_free(s)
                    for i in range(2):
                        c = n["slot"] * PLE + i * P
                        last = nc.tensor.transpose(bank(s.banks[0])[:, i * P:(i + 1) * P], t2[:, c:c + P], ident[:])
                    last.then_inc(sem["b_full"], 1)
                elif k == "pp":
                    pe.wait_ge(sem["lo"], n["ready"])
                    pe.wait_ge(sem["w"], n["w_ready"])
                    bank_free(s)
                    wp = head_w if n["j"] == 0 else kpe
                    for r in range(2):
                        last = product(bank(s.banks[0]), lambda part: p_t[part][:, r * P:(r + 1) * P],
                                       lambda part: wp[part][:, r * CW:(r + 1) * CW], r == 0, r == 1)
                    last.then_inc(sem["b_full"], 1)
                elif k == "hproj":
                    b, j, name = s.banks[0], n["j"], n["name"]
                    pe.wait_ge(sem["w"], n["w_ready"])
                    pe.wait_ge(sem["lo"], n["c_ready"])
                    bank_free(s)
                    if name in ("q", "pe", "k"):
                        off, step, lat = {"q": (0, 256, 0), "pe": (128, 256, 0), "k": (512, 128, 2)}[name]
                        for r in range(2):
                            last = product(bank(b), lambda part: head_w[part][:, off + r * step:off + r * step + P],
                                           lambda part: ring[part][:, CT0 + (lat + r) * S + j * CW:CT0 + (lat + r) * S + (j + 1) * CW],
                                           r == 0, r == 1)
                    else:
                        for i in range(4):
                            kt = 4 * j + i
                            for r in range(2):
                                last = product(bank(b)[:, i * P:(i + 1) * P],
                                               lambda part: ring[part][:, CT0 + (2 + r) * S + kt * P:CT0 + (2 + r) * S + (kt + 1) * P],
                                               lambda part: head_w[part][:, 768 + r * P:768 + (r + 1) * P], r == 0, r == 1)
                    last.then_inc(sem["b_full"], 1)
                elif k == "idx":
                    t = n["t"]
                    pe.wait_ge(sem["lo"], n["q_ready"])
                    bank_free(s, 0)
                    bank_free(s, 1)
                    c0 = (t % 2) * CW + (n["h"] // 2) * P
                    keys = slice(n["c"] * CW, n["c"] * CW + n["n"])
                    for i, (qp, kp) in enumerate(((1, 0), (0, 1), (0, 0))):
                        for j in range(2):
                            half = slice(64 * j, 64 * j + 64)
                            last = nc.tensor.matmul(bank(s.banks[j], n["n"]), head_w[qp][half, c0:c0 + P],
                                                    kpe[kp][half, keys], start=i == 0, stop=i == 2)
                            if i == 2:
                                last.then_inc(sem["b_full"], 1)
                elif k == "S":
                    lay, qb = n["lay"], n["qb"]
                    pe.wait_ge(sem["lo"], n["q_ready"])
                    bank_free(s)
                    keys = (qb + 1) * P
                    for c0 in range(0, keys, CW):
                        cn = min(CW, keys - c0)
                        dst = psum[:, s.banks[0] * CW + c0:s.banks[0] * CW + c0 + cn]
                        if lay == 0:
                            diag = c0 + cn == keys
                            product(dst, lambda part: region(part, Q0, qb * P, P),
                                    lambda part: region(part, K0, c0, cn), True, False)
                            last = product(dst, lambda part: region(part, PE0, qb * P, P),
                                           lambda part: kpe[part][:, c0:c0 + cn], False, not diag)
                            if diag:
                                last = nc.tensor.matmul(dst[:, cn - P:cn], ident_r[:], tri_r[:], start=False, stop=True)
                        else:
                            g = n["h"] // GROUP
                            last = product(dst, lambda part: qT1(part, n["h"] % 2, qb * P, P),
                                           lambda part: kT1(part, g, c0, cn), True, True)
                    last.then_inc(sem["a_full"], 1)
                elif k == "T":
                    pe.wait_ge(sem["pn"], n["pn"])
                    for j, b in enumerate(s.banks):
                        bank_free(s, j)
                        for i in range(min(4, n["qb"] + 1 - 4 * j)):
                            c = (4 * j + i) * P
                            last = nc.tensor.transpose(bank(b)[:, i * P:(i + 1) * P], rows[n["ps"]][:, c:c + P], ident[:])
                        last.then_inc(sem["b_full"], 1)
                elif k == "PV":
                    g, lay = n["g"], n["lay"]
                    pe.wait_ge(sem["lo"], n["ready"])
                    bank_free(s)
                    kts = 2 * g + 2
                    for kt in range(kts):
                        c0 = max(0, kt - 2 * g) * P
                        vals = ((lambda part: region(part, V0, kt * P, P)) if lay == 0
                                else (lambda part: v1(part, n["h"] // GROUP, kt * P, P)))
                        last = product(bank(s.banks[0])[:, c0:256], vals,
                                       lambda part: pt_at(part, n["pbuf"], kt, c0, 256 - c0), kt == 0, kt == kts - 1)
                    last.then_inc(sem["b_full"], 1)


NAMES = ["x", "p", "positions", "norm_in", "mla_w_in", "mla_q_norm", "mla_kv_norm", "mla_w_uq", "mla_w_uk",
         "mla_w_uv", "mla_w_out", "dsa_w_in", "dsa_w_out", "ple_w_proj", "ple_norm", "ple_w_gate", "final_norm"]


def kernel(**inputs):
    import concourse.bacc as bacc
    from concourse.bass_utils import run_bass_kernel_spmd as run

    nc = bacc.Bacc("TRN2", target_bir_lowering=False, num_devices=1)
    arrays = {n: np.ascontiguousarray(inputs[n]) for n in NAMES}
    half = np.float32(NFREQ)
    arrays["freqs"] = (1.0 / (np.float32(10000.0) ** (np.arange(NFREQ, dtype=np.float32) / half))).astype(np.float32)
    h = {n: nc.dram_tensor("in_" + n, a.shape, mybir.dt.from_np(a.dtype), kind="ExternalInput").ap()
         for n, a in arrays.items()}
    out = nc.dram_tensor("out", (1, S, D), F32, kind="ExternalOutput").ap()
    build(nc, h["x"][0], h["p"].rearrange("l b s c -> (l b) s c"), h["positions"], h["norm_in"],
          h["mla_w_in"][0], h["mla_q_norm"][0], h["mla_kv_norm"][0], h["mla_w_uq"][0],
          h["mla_w_uk"][0].rearrange("c h n -> c (h n)"), h["mla_w_uv"][0].rearrange("c h n -> c (h n)"),
          h["mla_w_out"][0], h["dsa_w_in"][0], h["dsa_w_out"][0], h["ple_w_proj"], h["ple_norm"], h["ple_w_gate"],
          h["final_norm"], h["freqs"], out[0])
    r = run(nc, [{"in_" + n: a for n, a in arrays.items()}], core_ids=[0])
    return r.results[0]["out"]
```

```python
from contextlib import ExitStack

import numpy as np
import concourse.bass as bass
from concourse import mybir

ALU = mybir.AluOpType
ACT = mybir.ActivationFunctionType
F32 = mybir.dt.float32
F32R = mybir.dt.float32r
U32 = mybir.dt.uint32
I32 = mybir.dt.int32
AX_X = mybir.AxisListType.X

P = 128
S = 1024
D = 1024
T = S // P
KD = D // P
CW = 512
HEADS = 8
RANK = 256
NOPE, ROPE_D = 128, 64
MLA_SCALE = float(np.float32((NOPE + ROPE_D) ** -0.5))
HD = 128
DSA_SCALE = float(np.float32(HD ** -0.5))
KV_HEADS = 2
GROUP = HEADS // KV_HEADS
IDX_HEADS, IDX_DIM = 8, 64
IDX_SCALE = float(IDX_DIM ** -0.5)
W_IDX_SCALE = float(np.float32(IDX_HEADS ** -0.5))
TOPK = 256
FULL = TOPK // P
PLE = 256
EPS = 1e-6
NEG = -3.0e38
HALF = HD // 2
NFREQ = HALF
SCORE_AT = [P * t * (t + 1) // 2 for t in range(T + 1)]
SPREAD = T - FULL
SEARCH = [2, 4, 5, 3, 6, 7]
ACT_TILES = [3, 6, 7]
TWO_PI = 2 * np.pi
RAW_SLOTS = 3


def two_pi_parts():
    c1 = 6.28125
    bits = np.frombuffer(np.float32(TWO_PI - c1).tobytes(), np.uint32)[0] & 0xFFFFF000
    c2 = float(np.frombuffer(np.uint32(bits).tobytes(), np.float32)[0])
    return c1, c2, TWO_PI - c1 - c2


SMALL = 2
SEQ = {
    0: [("c", "mla_in", 0, CW, 0), ("kpe", "mla_in", 512, P, SMALL),
        ("z", "mla_in", 576, CW, 1), ("z", "mla_in", 1088, CW, 0),
        ("wo", "out0", 0, CW, 0), ("wo", "out0", CW, CW, 1),
        ("gate", "gate0", 0, CW, 0), ("gate", "gate0", CW, CW, 1)],
    1: [("kiwi", "dsa_in", 2048, P, SMALL), ("qi", "dsa_in", 1536, CW, 0), ("kv", "dsa_in", 1024, CW, 1),
        ("q", "dsa_in", 0, CW, 0), ("q", "dsa_in", CW, CW, 1),
        ("z", "dsa_in", 2120, CW, 0), ("z", "dsa_in", 2632, CW, 1),
        ("wo", "out1", 0, CW, 0), ("wo", "out1", CW, CW, 1),
        ("gate", "gate1", 0, CW, 0), ("gate", "gate1", CW, CW, 1)],
}
RES = ["ring0", "ring1", "headW"]
CHUNKS = [(lay, i) + c for lay in (0, 1) for i, c in enumerate(SEQ[lay])]
DMA_SEMS = (["raw_ld%d" % i for i in range(RAW_SLOTS)] + ["x_ld%d" % t for t in range(T)] +
            ["const_ld", "gain", "z_st0", "z_st1", "z_ld", "xin0", "xin1", "p_ld0", "p_ld1",
             "x2_st", "st0", "st1", "cs_st", "cs_ld", "t2_ld", "k0_ld", "lat_ld", "out_st"])
PLAIN_SEMS = ["a_full", "b_full", "hi", "lo", "sq", "rstd", "xn", "w", "zs", "rot_in", "rot",
              "xadd", "sg", "pp", "relu", "sc", "nb", "ex", "pn", "og", "stage", "trig",
              "csq", "consts", "vcopy", "found", "widx", "w_hi", "w0", "fk", "tally", "cand", "pool_chain", "dve_chain", "fin"]


class Step:
    pass


def plan():
    steps, now = [], {n: 0 for n in DMA_SEMS + PLAIN_SEMS}
    bank_free = {b: [] for b in range(8)}
    ring_at = {"A": 0, "B": 0}
    read_by = {}
    granules = [0]

    def add(kind, incs=None, ring=None, jobs=0, freed=None, wide=False, **kw):
        s = Step()
        s.kind, s.before = kind, dict(now)
        for n, k in (incs or {}).items():
            now[n] += k * (16 if n in DMA_SEMS else 1)
        s.after = dict(now)
        s.n = dict(kw)
        s.banks, s.free = [], []
        for j in range(jobs):
            if wide:
                first = (ring_at[ring] + 1) // 2 * 2 % 4
                ring_at[ring] = first + 2
                first += 4 if ring == "B" else 0
                banks = [first, first + 1]
            else:
                banks = [ring_at[ring] % 4 + (4 if ring == "B" else 0)]
                ring_at[ring] += 1
            need = {}
            for b in banks:
                for n, v in bank_free[b]:
                    need[n] = max(need.get(n, 0), v)
            s.banks.append(banks[0])
            s.free.append(sorted(need.items()))
            for b in banks:
                bank_free[b] = [(n, s.before[n] + j + 1) for n in freed]
        steps.append(s)
        return s

    def w(chunk, d):
        lay, i, name, src, c0, n, buf = chunk
        res = RES[buf]
        g = granules[0]
        granules[0] += 1
        first = (lay, i) == (0, 0)
        done = "w0" if first else "w"
        incs = {done: 1, "raw_ld%d" % (g % RAW_SLOTS): 1}
        if first:
            incs["w_hi"] = 1
        s = add("w_first" if first else "w", incs, src=src, d=d, c0=c0, cols=n, raw_free=raw_free(g),
                buf=buf, g=g, reader=read_by.get(res) if d == 0 else None)
        split_at.append((done, s.after[done]))
        w_after[(lay, i, d)] = split_at[g]

    w_after = {}
    split_at = []

    def raw_free(g):
        return split_at[g - RAW_SLOTS] if g >= RAW_SLOTS else None

    def ahead(chunk, job):
        for d in ([0, 1] if job == 0 else [job + 1] if job + 1 < KD else []):
            w(chunk, d)

    def small_piece(kind, res, k, **kw):
        g = granules[0]
        granules[0] += 1
        s = add(kind, {"w": 1, "raw_ld%d" % (g % RAW_SLOTS): 1}, piece=k, g=g, res=res,
                raw_free=raw_free(g), reader=read_by.get(res) if k == 0 else None, **kw)
        split_at.append(("w", s.after["w"]))
        return s.after["w"]

    def small_w(kind, res, pieces=2, **kw):
        return [small_piece(kind, res, k, **kw) for k in range(pieces)]

    lo_at = {}

    def norm_a(t, slot, ready, gain):
        return add("norm_a", {"sq": 1, "rstd": 1, "xn": 1}, t=t, slot=slot, ready=ready, gain=gain)

    def norm_b(t, slot, xn):
        s = add("norm_b", {"b_full": 2, "hi": 2, "lo": 2}, ring="B", jobs=2, freed=["lo"],
                t=t, slot=slot, xn=xn)
        lo_at[("act", t)] = s.after["lo"]

    def gain(which):
        return add("gain", {"gain": 1}, which=which, reader=read_by.get("G"))

    def split4(src, slot, ready, cols=CW, **kw):
        return add("split4", {"b_full": 1, "hi": 1, "lo": 1}, ring="B", jobs=1, freed=["lo"],
                   src=src, slot=slot, ready=ready, cols=cols, **kw)

    def chunk_of(lay, i):
        return next(c for c in CHUNKS if c[:2] == (lay, i))

    def next_chunk(lay, i):
        at = [c[:2] for c in CHUNKS].index((lay, i)) + 1
        return CHUNKS[at] if at < len(CHUNKS) else None

    def proj(lay, i, job, freed, incs, **kw):
        c = chunk_of(lay, i)
        half = {"z": job // 4, "kpe": job, "kiwi": job}.get(c[2])
        tiles = [job] if half is None else range(4 * half, 4 * half + 4)
        s = add("proj", dict(incs, a_full=1), ring="A", jobs=1, freed=freed, lay=lay, chunk=i, name=c[2], cols=c[5],
                buf=c[6], job=job, half=half, w_ready=[w_after[(lay, i, d)] for d in range(KD)],
                act=max(lo_at[("act", t)] for t in tiles), **kw)
        read_by[RES[c[6]]] = ("a_full", s.after["a_full"])
        return s

    add("load_x", {"x_ld0": 1}, t=0)
    add("start", {"gain": 1, "consts": 1})
    def load_x(t):
        add("load_x", {"x_ld%d" % t: 1}, t=t)

    def z_chunk(lay, i, base, prefetch=True, extra=None):
        for job in range(8):
            if prefetch:
                ahead(next_chunk(lay, i), job)
            slot = job % 2
            proj(lay, i, job, ["zs"], {"zs": 1, "z_st%d" % slot: 1}, slot=slot, base=base)
            if extra:
                extra(8 * (base // CW) + job)

    def rope_job(lay, i, job, slot, extra_inc=None, **kw):
        inc = {"rot_in": 1, "rot": 1}
        inc.update(extra_inc or {})
        return proj(lay, i, job, ["rot_in"], inc, slot=slot, **kw)

    def key_job(lay, i, job):
        return proj(lay, i, job, ["fk"], {"fk": 1}, slot=job)

    def key_back(lay, job, fk, **kw):
        incs = {"b_full": 1, "rot_in": 1, "rot": 1}
        if lay == 1:
            incs["widx"] = 1
        return add("key_back", incs, ring="B", jobs=1, freed=["rot_in"], lay=lay, job=job, fk=fk, **kw)

    def key_split(lay, job, rot):
        return split4("p1" if lay == 0 else "t2", job, ("rot", rot), dest="kpeT", j=job).after["lo"]

    normed = {}

    def norm0(t):
        normed[t] = norm_a(t, t % 2, ("x_ld%d" % t, 16), now["gain"]).after["xn"]
    first = chunk_of(0, 0)
    norm0(0)
    for d in range(3):
        w(first, d)
    norm_b(0, 0, normed[0])
    load_x(1)
    w(first, 3)
    w(first, 4)
    w(first, 5)
    norm0(1)
    load_x(2)
    w(first, 6)
    w(first, 7)
    add("small_loads", {"const_ld": 2, "lat_ld": 2})
    norm_b(1, 1, normed[1])
    load_x(3)
    for t in range(T):
        if t + 4 < T:
            load_x(t + 4)
        if t + 2 < T:
            norm0(t + 2)
        w(next_chunk(0, 0), t)
        w(next_chunk(0, 1), t)
        proj(0, 0, t, ["xn"], {"sq": 2, "rstd": 1, "xn": 1}, slot=t % 2)
        if t + 2 < T:
            norm_b(t + 2, t % 2, normed[t + 2])
    latent_rows = now["xn"]
    read_by["G"] = ("xn", now["xn"])
    tb = add("tables", {"stage": 2, "trig": 2, "cs_st": 1})
    fk = [key_job(0, 1, job).after["fk"] for job in range(2)]
    rots, marks = [], {}

    def z0_extra(k):
        if k in (0, 1):
            rots.append(key_back(0, k, fk[k], trig=tb.after["trig"]).after["rot"])
        elif k in (2, 3):
            lo_at["kpeT"] = key_split(0, k - 2, rots[k - 2])
        elif k == 5:
            marks["csq"] = add("table_t", {"stage": 2, "b_full": 2, "csq": 2}, ring="B", jobs=2,
                               freed=["csq"]).after["csq"]
        elif k >= 8:
            lo_at["cT"] = split4("xr", 0, ("xn", latent_rows), dest="cT", t=k - 8).after["lo"]
    z_chunk(0, 2, 0, extra=z0_extra)
    head_w = dict(enumerate(small_w("head_w", "headW", pieces=3, h=0)))
    z_chunk(0, 3, CW, prefetch=False, extra=z0_extra)

    att = {"n": 0}
    order = [6, 7, 0, 1, 4, 5, 2, 3]

    def s_step(lay, h, qb, q_ready):
        n = att["n"]
        att["n"] += 1
        s = add("S", {"a_full": 1, "nb": 1}, ring="A", jobs=1, freed=["ex" if lay == 0 else "nb"], wide=True,
                lay=lay, h=h, qb=qb, ps=n % 3, q_ready=q_ready)
        return dict(lay=lay, ps=n % 3, qb=qb, bank=s.banks[0], nb=s.after["nb"])

    def e_step(args):
        return add("E", {"ex": 1, "pn": 1}, **args).after["pn"]

    def t_step(lay, h, qb, pn, ps):
        jobs = qb // 4 + 1
        s = add("T", {"b_full": jobs, "hi": jobs, "lo": jobs}, ring="B", jobs=jobs, freed=["lo"],
                lay=lay, qb=qb, pn=pn, ps=ps, pbuf=order.index(qb) // 2 % 2)
        return s.after["lo"]

    def pv_step(lay, h, g, pt_ready, v_ready, z_ld):
        s = add("PV", {"b_full": 1, "og": 1}, ring="B", jobs=1, freed=["og"], lay=lay, h=h, g=g,
                pbuf=order.index(2 * g) // 2 % 2, ready=max(pt_ready, v_ready), z_ld=z_ld)
        read_by["G"] = ("og", s.after["og"])
        return s

    def hproj(h, names):
        for j, name in enumerate(names):
            incs = {"b_full": 1, "hi": 1, "lo": 1}
            if name == "pe":
                incs["stage"] = 1
            s = add("hproj", incs, ring="B", jobs=1, freed=["lo"], h=h, name=name, j=j if name == "v" else j % 2,
                    w_ready=head_w[{"q": 0, "pe": 0, "k": 1, "v": 2}[name]], c_ready=lo_at["cT"], csq=marks["csq"])
        read_by["headW"] = ("b_full", s.after["b_full"])
        read_by["ring1"] = ("b_full", s.after["b_full"])
        return s.after["lo"]

    def z_load(lay, h):
        s = add("z_load", {"z_ld": 1}, lay=lay, h=h, reader=read_by.get("G"),
                stored=(now["z_st0"], now["z_st1"]))
        return s.after["z_ld"]

    qk_ready = hproj(0, ["q", "q", "pe", "pe", "k", "k"])
    pn = {}

    def first_rows(h, i):
        ps = att["n"] % 3
        pn[i] = (e_step(s_step(0, h, order[i], max(qk_ready, lo_at["kpeT"]))), ps)

    first_rows(0, 0)
    first_rows(0, 1)
    v_ready = hproj(0, ["v"] * 4)
    for h in range(HEADS):
        zl = z_load(0, h)
        more = h + 1 < HEADS
        lo = {}
        for i, qb in enumerate(order):
            if i >= 2:
                ps = att["n"] % 3
                args = s_step(0, h, qb, max(qk_ready, lo_at["kpeT"]))
                lo[i - 2] = t_step(0, h, order[i - 2], *pn[i - 2])
                pn[i] = (e_step(args), ps)
            if more and (i in (3, 5) or (i == 6 and h % 2)):
                head_w[i // 2 - 1] = small_piece("head_w", "headW", i // 2 - 1, h=h + 1)
            if i in (5, 7):
                pv_step(0, h, order[i - 5] // 2, lo[i - 4], v_ready, zl)
        read_by["kpe"] = ("a_full", now["a_full"])
        if h:
            w(chunk_of(0, 4), h)
        if h == 1:
            w(chunk_of(0, 4), 0)
        if more:
            hproj(h + 1, ["q", "q"])
        t_step(0, h, order[6], *pn[6])
        if more:
            hproj(h + 1, ["pe", "pe"])
        lo[7] = t_step(0, h, order[7], *pn[7])
        if more:
            qk_ready = hproj(h + 1, ["k", "k"])
        pv_step(0, h, order[4] // 2, lo[5], v_ready, zl)
        if more:
            first_rows(h + 1, 0)
        pv_step(0, h, order[6] // 2, lo[7], v_ready, zl)
        if more:
            first_rows(h + 1, 1)
            if h % 2:
                v_ready = hproj(h + 1, ["v"] * 4)

    def tail(lay, wo0, last_gain, pa_reader):
        g1 = gain("ple%d" % lay).after["gain"]
        rows_free = now["b_full"]
        ppw = {}
        for t in range(T):
            s = add("og_split", {"hi": 1, "lo": 1}, t=t, act_free=now["b_full"])
            lo_at[("act", t)] = s.after["lo"]
        read_by["pst0"], read_by["pst1"] = pa_reader, pa_reader
        n = [0]

        def xin(t, j):
            return add("xin", {"xin%d" % (n[0] % 2): 1}, lay=lay, t=t, j=j, slot=n[0] % 2,
                       wait_add=(now["xadd"] - 1) if n[0] >= 2 else None, rows_free=rows_free,
                       x2=now["x2_st"])
        p_at = {}

        def p_load(k):
            if k < 2 * T:
                slot = k % 2
                p_at[k] = add("p_load", {"p_ld%d" % slot: 1}, lay=lay, t=k % T, slot=slot,
                              reader=read_by["pst%d" % slot]).after["p_ld%d" % slot]
        for j in range(2):
            prev = None
            for t in range(T):
                w(next_chunk(lay, wo0 + j), t)
                if j == 0 and t == 0:
                    ppw[0] = small_w("ple_w", "headW", lay=lay, j=0)[-1]
                if j == 0 and t == 2:
                    ppw[1] = small_w("ple_w", "kpe", lay=lay, j=1)[-1]
                x = xin(t, j)
                slot = n[0] % 2
                n[0] += 1
                if j == 1 and t == 0:
                    p_load(0)
                s = proj(lay, wo0 + j, t, ["xadd"], {"xadd": 1}, slot=slot, xin=x.after["xin%d" % slot], j=j)
                if j == 1:
                    if prev:
                        norm_b(prev[0], 0, prev[1])
                    a = norm_a(t, 0, ("xadd", s.after["xadd"]), g1)
                    prev = (t, a.after["xn"])
        last_rows = prev
        read_by["G"] = ("xn", now["xn"])
        g2 = gain(last_gain).after["gain"]
        gj = wo0 + 2
        n = 0
        for j in range(2):
            prev = None
            for t in range(T):
                p_load(n + 1)
                if next_chunk(lay, gj + j):
                    w(next_chunk(lay, gj + j), t)
                    if j == 1:
                        w(next_chunk(1, 0), t)
                pslot = n % 2
                pt = add("p_split", {"b_full": 1, "hi": 1, "lo": 1}, ring="B", jobs=1,
                         freed=["lo"], lay=lay, t=t, slot=pslot, p_ld=p_at[n])
                read_by["pst%d" % pslot] = ("b_full", pt.after["b_full"])
                s = proj(lay, gj + j, t, ["sg"], {"sg": 1}, slot=n % 2, j=j,
                         wait_add=now["xadd"] - 1)
                q = add("pp", {"b_full": 1, "pp": 1, "xadd": 1}, ring="B", jobs=1, freed=["pp"],
                        t=t, j=j, slot=n % 2, ready=pt.after["lo"], w_ready=ppw[j], sg=s.after["sg"])
                read_by["headW" if j == 0 else "kpe"] = ("b_full", q.after["b_full"])
                if n == 0:
                    norm_b(last_rows[0], 0, last_rows[1])
                n += 1
                if j == 1 and lay == 0:
                    if prev:
                        norm_b(prev[0], 0, prev[1])
                    add("save_x", {"x2_st": 1}, t=t, ready=q.after["xadd"])
                    a = norm_a(t, 0, ("xadd", q.after["xadd"]), g2)
                    prev = (t, a.after["xn"])
                if j == 1 and lay == 1:
                    if t:
                        add("store_out", {"out_st": 1}, t=t - 1, fin=fin)
                    fin = add("final", {"sq": 1, "rstd": 1, "fin": 1}, t=t, ready=q.after["xadd"],
                              gain=g2).after["fin"]
        if lay == 1:
            add("store_out", {"out_st": 1}, t=T - 1, fin=fin)
        read_by["G"] = ("xn", now["xn"])
        return prev

    cs = add("cs_load", {"cs_ld": 1}, pn=now["b_full"])
    last_rows = tail(0, 4, "in1", ("lo", now["lo"]))

    def idx_scores(t, q_ready):
        keys = (t + 1) * P
        for h in range(0, IDX_HEADS, 2):
            wide = keys > CW
            s = add("idx", {"b_full": 2, "relu": 2, "sc": 2}, ring="AB"[h // 2 % 2], jobs=2, freed=["relu"],
                    wide=wide, t=t, h=h, keys=keys, q_ready=max(q_ready, lo_at["kiT"]), k=idx_n[0],
                    x2=now["x2_st"], gfree=read_by["G"])
            idx_n[0] += 2
        add("idx_mask", None, t=t)
    idx_n = [0]
    fk = [key_job(1, 0, 0).after["fk"]]
    norm_b(last_rows[0], 0, last_rows[1])

    def qi_job(t):
        w(next_chunk(1, 1), t)
        return rope_job(1, 1, t, t % 2, cs=cs.after["cs_ld"]).after["rot"]

    def qi_split(t, rot):
        return add("qi_split", {"b_full": 2, "hi": 2, "lo": 2}, ring="B", jobs=2, freed=["lo"],
                   slot=t % 2, rot=rot).after["lo"]
    w(next_chunk(1, 1), 0)
    w(next_chunk(1, 1), 1)
    rot = {FULL: qi_job(FULL)}
    fk.append(key_job(1, 0, 1).after["fk"])
    rots = [key_back(1, job, fk[job]).after["rot"] for job in range(2)]
    qi_ready = {FULL: qi_split(FULL, rot[FULL])}
    rot[FULL + 1] = qi_job(FULL + 1)
    for job in range(2):
        lo_at["kiT"] = key_split(1, job, rots[job])
    for t in range(FULL, T):
        if t + 1 < T:
            qi_ready[t + 1] = qi_split(t + 1, rot[t + 1])
        if t + 2 < T:
            rot[t + 2] = qi_job(t + 2)
        idx_scores(t, qi_ready[t])
    read_by["G"] = ("sc", now["sc"])

    bits = [31 - i for i in range(32)]

    def search_begin():
        if bits:
            st = add("bit", {"cand": 1, "tally": len(ACT_TILES)}, bit=bits.pop(0))
            for b in (6, 7):
                bank_free[b] = bank_free[b] + [("tally", st.after["tally"])]
            return st

    def search_end(st):
        if st:
            add("bit_end", None, bit=st.n["bit"], tally=st.after["tally"])

    def search():
        search_end(search_begin())

    n = 0
    for i, name in ((2, "kv"), (3, "q"), (4, "q")):
        for t in range(T):
            ahead(next_chunk(1, i), t)
            slot = n % 2
            inc = {"st%d" % slot: 1}
            if name == "kv":
                inc["vcopy"] = 1
            st = search_begin() if name == "q" else None
            rope_job(1, i, t, slot, extra_inc=inc, base=(i - 3) * CW, st_before=now["st%d" % slot])
            n += 1
            if name == "q":
                search_end(st)
            else:
                search()
    q_stored = (now["st0"], now["st1"])

    def t2_load(what, i, reader):
        return add("t2_load", {"t2_ld": 1}, what=what, i=i, reader=reader, stored=q_stored).after["t2_ld"]

    def q_prep(h, ld):
        s = None
        for j in range(2):
            s = split4("t2", 0, ("t2_ld", ld), dest="qT", slot2=h % 2, j=j)
        return s.after["lo"], ("b_full", s.after["b_full"])

    first_q = {}
    after_bits = [("last_step", None, {}), ("above", None, {})]
    after_bits += [("sel", {"found": 1}, {"t": t}) for t in range(FULL, T)]

    def z_extra(k):
        search()
        if k == 3:
            first_q["ready"], rd = q_prep(0, ld)
            first_q["v_ld"] = t2_load("v", 0, rd)
        if not bits and k >= 8 and after_bits:
            kind, incs, kw = after_bits.pop(0)
            add(kind, incs, **kw)
    ld = t2_load("q", 0, ("b_full", now["b_full"]))
    k0 = add("k0_load", {"k0_ld": 1}, stored=q_stored)
    add("silu_room", {}, rot=now["rot"])
    z_chunk(1, 5, 0, extra=z_extra)
    z_chunk(1, 6, CW, prefetch=False, extra=z_extra)
    while after_bits:
        kind, incs, kw = after_bits.pop(0)
        add(kind, incs, **kw)
    read_by["G"] = ("found", now["found"])
    act_free = now["a_full"]
    k_ready, v_ready = {}, {}
    for j in range(2):
        k_ready[0] = split4("p1", 0, ("k0_ld", k0.after["k0_ld"]), dest="kT", g=0, j=j).after["lo"]

    def v_prep(g, ld, act_free):
        s = add("v_split", {"hi": 1, "lo": 1}, g=g, ld=ld, act_free=act_free)
        v_ready[g] = s.after["lo"]
        return ("lo", s.after["lo"])
    rd = v_prep(0, first_q["v_ld"], act_free)

    waiting = []

    ready_pv = []

    def outputs():
        hh, g, lo = ready_pv.pop(0)
        pv_step(1, hh, g, lo, v_ready[hh // GROUP], zl[hh])
        if g == order[-1] // 2 and hh + 1 < HEADS:
            zl[hh + 1] = z_load(1, hh + 1)

    def transposes():
        hh, qq, pn, ps = waiting.pop(0)
        lo = t_step(1, hh, qq, pn, ps)
        if qq % 2:
            ready_pv.append((hh, qq // 2, lo))
    zl = {0: z_load(1, 0)}
    q_at = {0: first_q["ready"]}
    for h in range(HEADS):
        if h + 1 < HEADS:
            ld = t2_load("q", h + 1, rd)
        for i, qb in enumerate(order):
            if h == 0:
                for t in (order[0:3] if i == 0 else order[i + 2:i + 3]):
                    add("mask", None, t=t, a_full=act_free, first=t == order[0])
            ps = att["n"] % 3
            args = s_step(1, h, qb, max(q_at[h], k_ready[h // GROUP]))
            pv = bool(ready_pv) and i % 2 == 1
            if len(waiting) > 1:
                transposes()
            waiting.append((h, qb, e_step(args), ps))
            if pv:
                outputs()
            if i == 2:
                w(chunk_of(1, 7), h)
            if i == 3 and h + 1 < HEADS:
                q_at[h + 1], rd = q_prep(h + 1, ld)
                if h in (0, 1):
                    ld2 = t2_load("kv"[h], 1, rd)
            if i == 6 and h == 0:
                for j in range(2):
                    s = split4("t2", 0, ("t2_ld", ld2), dest="kT", g=1, j=j)
                k_ready[1] = s.after["lo"]
                rd = ("b_full", s.after["b_full"])
            if i == 6 and h == 1:
                rd = v_prep(1, ld2, act_free)
    read_by["ring1"] = ("nb", now["nb"])
    read_by["headW"] = read_by["kpe"] = ("a_full", now["a_full"])
    outputs()
    transposes()
    transposes()
    outputs()
    tail(1, 7, "final", ("lo", now["lo"]))
    return steps, now


def build(nc, x, p, positions, norm_in, w_in0, q_norm, kv_norm, w_uq, w_uk, w_uv, w_out0, w_in1, w_out1,
          ple_proj, ple_norm, ple_gate, final_norm, freqs, out):
    steps, total = plan()
    weights = {"mla_in": w_in0, "dsa_in": w_in1, "out0": w_out0, "out1": w_out1,
               "gate0": ple_gate[0], "gate1": ple_gate[1]}
    gains = {"in0": norm_in[0:1, :], "in1": norm_in[1:2, :], "ple0": ple_norm[0:1, :], "ple1": ple_norm[1:2, :],
             "final": final_norm}

    with ExitStack() as ctx:
        def sb(name, cols, dt=F32):
            return ctx.enter_context(nc.sbuf_tensor(name, [P, cols], dt))

        act = [sb("act_hi", KD * S, F32R), sb("act_lo", KD * S, F32R)]
        ring = [sb("ring_hi", 2 * KD * CW, F32R), sb("ring_lo", 2 * KD * CW, F32R)]
        kpe = [sb("kpe_hi", S, F32R), sb("kpe_lo", S, F32R)]
        head_w = [sb("head_w_hi", 1024, F32R), sb("head_w_lo", 1024, F32R)]
        p_t = [sb("p_t_hi", PLE, F32R), sb("p_t_lo", PLE, F32R)]
        ident_r = sb("ident_r", P, F32R)
        tri_r = sb("tri_r", P, F32R)
        xr = sb("xr", T * D)
        raw = sb("raw", RAW_SLOTS * CW)
        p0 = sb("p0", 1024)
        p1 = sb("p1", 1024)
        cs = sb("cs", 1024)
        t2 = sb("t2", 1024)
        gz = sb("gz", 1024)
        ident = sb("ident", P)
        tri = sb("tri", P)
        small = sb("small", 128)
        pos_i = sb("pos_i", T, I32)
        frq = sb("frq", NFREQ)
        wis = sb("wis", T * IDX_HEADS)
        bits_u = sb("bits_u", 6 * SPREAD, U32)
        psum = ctx.enter_context(nc.psum_tensor("psum", [P, 8 * CW], F32))

        sem = {n: ctx.enter_context(nc.semaphore(n)) for n in DMA_SEMS + PLAIN_SEMS}
        z_dram = [nc.dram_tensor("z_scratch%d" % l, [D, S], F32, kind="Internal").ap() for l in range(2)]
        x2_dram = nc.dram_tensor("x2_scratch", [S, D], F32, kind="Internal").ap()
        q_dram = nc.dram_tensor("q_scratch", [S, D], F32, kind="Internal").ap()
        kv_dram = nc.dram_tensor("kv_scratch", [S, CW], F32, kind="Internal").ap()
        cs_dram = nc.dram_tensor("cs_scratch", [P, 1024], F32, kind="Internal").ap()

        ms = small[:, 0:8]
        mean = small[:, 8:16]
        rs = small[:, 16:24]
        lat_ms, lat_mean, lat_rs = small[:, 24:28], small[:, 28:32], small[:, 32:36]
        minus_half = small[:, 36:38]
        minus_one = small[:, 38:39]
        posf = small[:, 40:48]
        nb, sm, ri = small[:, 51:54], small[:, 54:57], small[:, 57:60]
        cnt = small[:, 64:64 + SPREAD]
        need = small[:, 72:72 + SPREAD]
        reach = small[:, 88:88 + SPREAD]
        u_bits, u_mask, u_cand, u_inc, u_minus, u_mask2 = (bits_u[:, k * SPREAD:(k + 1) * SPREAD] for k in range(6))
        rows = [p0, p1, cs]

        def bank(b, n=CW):
            return psum[:, b * CW:b * CW + n]

        def act_tile(part, t):
            return act[part][:].rearrange("p (d s) -> p d s", s=S)[:, :, t * P:(t + 1) * P]

        def act_at(part, d, c0, n):
            return act[part][:, d * S + c0:d * S + c0 + n]

        def w_at(part, buf, d, c0, n):
            if buf == SMALL:
                return head_w[part][:, d * P + c0:d * P + c0 + n]
            at = (buf * KD + d) * CW + c0
            return ring[part][:, at:at + n]

        CT0 = KD * CW
        PT0, V0, Q0, K0, PE0 = 0, 3072, 5120, 6144, 7168
        def pt_at(part, buf, kt, c0, n):
            at = PT0 + buf * 2048 + kt * 256 + c0
            return act[part][:, at:at + n]
        def pt_tiles(part, buf, qb, kt, kts):
            at = PT0 + buf * 2048 + kt * 256
            return act[part][:, at:at + kts * 256].rearrange("p (k c) -> p k c", c=256)[
                :, :, (qb % 2) * P:(qb % 2 + 1) * P]
        def region(part, at, c0, n):
            return act[part][:, at + c0:at + c0 + n]
        def kT1(part, g, c0, n):
            return act[part][:, 4096 + g * 1024 + c0:4096 + g * 1024 + c0 + n]
        def v1(part, g, c0, n):
            return act[part][:, 6144 + g * 1024 + c0:6144 + g * 1024 + c0 + n]
        def qT1(part, slot, c0, n):
            return (kpe, head_w)[slot][part][:, c0:c0 + n]
        def mask_at(t):
            if t < T - 1:
                return ring[0][:, KD * CW + SCORE_AT[t]:KD * CW + SCORE_AT[t + 1]]
            return ring[1][:, KD * CW:KD * CW + S]
        def qi_at(t, h):
            return head_w[t % 2][:, h * P:(h + 1) * P]
        def relu_slot(k, n):
            if n > CW:
                return (gz, t2)[k % 2][:, 0:n]
            return (gz, t2)[k // 2 % 2][:, k % 2 * CW:k % 2 * CW + n]
        def score_at(t, c0=0, n=None):
            n = (t + 1) * P - c0 if n is None else n
            return xr[:, SCORE_AT[t] + c0:SCORE_AT[t] + c0 + n]

        def small_dest(s, part):
            k = s.n["piece"]
            w = head_w[part]
            if s.kind == "ple_w":
                return [((head_w if s.n["res"] == "headW" else kpe)[part][:, k * CW:(k + 1) * CW], 0, CW)]
            if k == 0:
                pairs = []
                for r in range(2):
                    pairs += [(w[:, r * 256:r * 256 + 192], r * 192, 192),
                              (w[:, r * 256 + 192:r * 256 + 224], r * 192 + 160, 32),
                              (w[:, r * 256 + 224:r * 256 + 256], r * 192 + 128, 32)]
                return pairs
            if k == 1:
                return [(w[:, 512:768], 0, 256)]
            return [(p_t[part][:], 0, 256), (w[:, 768:1024], 256, 256)]

        def split_dest(s, part):
            dest = s.n["dest"]
            if dest == "kpeT":
                ap = kpe[part][:, s.n["j"] * CW:(s.n["j"] + 1) * CW]
            elif dest == "cT":
                t = s.n["t"]
                return ring[part][:, CT0:CT0 + 4 * S].rearrange("p (f s) -> p f s", s=S)[:, :, t * P:(t + 1) * P]
            elif dest == "qT":
                ap = qT1(part, s.n["slot2"], s.n["j"] * CW, CW)
            else:
                ap = kT1(part, s.n["g"], s.n["j"] * CW, CW)
            return ap.rearrange("p (a b) -> p a b", b=P)

        def in4(ap):
            return ap.rearrange("p (a b) -> p a b", b=P)

        block = ctx.enter_context(nc.Block())

        @block.sync
        def _(sp):
            for s in steps:
                k, n = s.kind, s.n
                if k == "start":
                    sp.dma_start(gz[:], gains["in0"].partition_broadcast(P)).then_inc(sem["gain"], 16)
                elif k == "small_loads":
                    sp.dma_start(frq[:], freqs.partition_broadcast(P)).then_inc(sem["const_ld"], 16)
                    sp.dma_start(pos_i[:], positions.rearrange("b (t p) -> p (b t)", p=P),
                                 allow_slow_non_contiguous=True).then_inc(sem["const_ld"], 16)
                    sp.dma_start(t2[:, 0:RANK], q_norm.partition_broadcast(P)).then_inc(sem["lat_ld"], 16)
                    sp.dma_start(t2[:, RANK:2 * RANK], kv_norm.partition_broadcast(P)).then_inc(sem["lat_ld"], 16)
                elif k == "load_x":
                    t = n["t"]
                    sp.dma_start(xr[:, t * D:(t + 1) * D], x[t * P:(t + 1) * P, :]).then_inc(sem["x_ld%d" % t], 16)
                elif k in ("w", "w_first", "head_w", "ple_w"):
                    slot = n["g"] % RAW_SLOTS
                    if n["raw_free"]:
                        sp.wait_ge(sem[n["raw_free"][0]], n["raw_free"][1])
                    dst = raw[:, slot * CW:(slot + 1) * CW]
                    ld = sem["raw_ld%d" % slot]
                    if k in ("w", "w_first"):
                        d = n["d"]
                        sp.dma_start(dst[:, 0:n["cols"]],
                                     weights[n["src"]][d * P:(d + 1) * P, n["c0"]:n["c0"] + n["cols"]]).then_inc(ld, 16)
                    elif k == "ple_w":
                        r, j = n["piece"], n["j"]
                        sp.dma_start(dst, ple_proj[n["lay"], r * P:(r + 1) * P, j * CW:(j + 1) * CW]).then_inc(ld, 16)
                    elif n["piece"] == 0:
                        h = n["h"]
                        sp.dma_start(dst[:, 0:384].rearrange("p (r c) -> p r c", r=2),
                                     w_uq.rearrange("(r p) c -> p r c", p=P)[:, :, h * 192:(h + 1) * 192]).then_inc(ld, 16)
                    elif n["piece"] == 1:
                        h = n["h"]
                        sp.dma_start(dst[:, 0:256].rearrange("p (r c) -> p r c", r=2),
                                     w_uk.rearrange("(r p) c -> p r c", p=P)[:, :, h * P:(h + 1) * P]).then_inc(ld, 16)
                    else:
                        h = n["h"]
                        sp.dma_start(dst.rearrange("p (r c) -> p r c", r=2),
                                     w_uv.rearrange("(r p) c -> p r c", p=P)[:, :, h * P:(h + 2) * P]).then_inc(ld, 16)
                elif k == "gain":
                    sp.wait_ge(sem[n["reader"][0]], n["reader"][1])
                    sp.dma_start(gz[:], gains[n["which"]].partition_broadcast(P)).then_inc(sem["gain"], 16)
                elif k == "tables":
                    sp.wait_ge(sem["trig"], s.after["trig"])
                    sp.dma_start(cs_dram, cs[:]).then_inc(sem["cs_st"], 16)
                elif k == "cs_load":
                    sp.wait_ge(sem["b_full"], n["pn"])
                    sp.wait_ge(sem["cs_st"], 16)
                    sp.dma_start(cs[:], cs_dram).then_inc(sem["cs_ld"], 16)
                elif k == "proj" and n["name"] == "z":
                    sp.wait_ge(sem["zs"], s.after["zs"])
                    f = n["base"] + (n["job"] % 4) * P
                    half = n["job"] // 4
                    sp.dma_start(z_dram[n["lay"]][f:f + P, half * CW:(half + 1) * CW],
                                 (gz, p0)[n["lay"]][:, n["slot"] * CW:(n["slot"] + 1) * CW]).then_inc(sem["z_st%d" % n["slot"]], 16)
                elif k == "proj" and n["name"] in ("q", "kv"):
                    sp.wait_ge(sem["rot"], s.after["rot"])
                    if n["name"] == "kv":
                        sp.wait_ge(sem["vcopy"], s.after["vcopy"])
                    t = n["job"]
                    dst = (kv_dram[t * P:(t + 1) * P, :] if n["name"] == "kv"
                           else q_dram[t * P:(t + 1) * P, n["base"]:n["base"] + CW])
                    sp.dma_start(dst, p1[:, n["slot"] * CW:(n["slot"] + 1) * CW]).then_inc(sem["st%d" % n["slot"]], 16)
                elif k == "z_load":
                    sp.wait_ge(sem[n["reader"][0]], n["reader"][1])
                    sp.wait_ge(sem["z_st0"], n["stored"][0])
                    sp.wait_ge(sem["z_st1"], n["stored"][1])
                    h = n["h"]
                    sp.dma_start(gz[:], z_dram[n["lay"]][h * P:(h + 1) * P, :]).then_inc(sem["z_ld"], 16)
                elif k == "xin":
                    sp.wait_ge(sem["b_full"], n["rows_free"])
                    if n["wait_add"] is not None:
                        sp.wait_ge(sem["xadd"], n["wait_add"])
                    if n["lay"] == 1:
                        sp.wait_ge(sem["x2_st"], n["x2"])
                    t, j = n["t"], n["j"]
                    src = x if n["lay"] == 0 else x2_dram
                    sp.dma_start(p1[:, n["slot"] * CW:(n["slot"] + 1) * CW],
                                 src[t * P:(t + 1) * P, j * CW:(j + 1) * CW]).then_inc(sem["xin%d" % n["slot"]], 16)
                elif k == "p_load":
                    sp.wait_ge(sem[n["reader"][0]], n["reader"][1])
                    t = n["t"]
                    sp.dma_start(t2[:, n["slot"] * PLE:(n["slot"] + 1) * PLE],
                                 p[n["lay"], t * P:(t + 1) * P, :]).then_inc(sem["p_ld%d" % n["slot"]], 16)
                elif k == "save_x":
                    sp.wait_ge(sem["xadd"], n["ready"])
                    t = n["t"]
                    sp.dma_start(x2_dram[t * P:(t + 1) * P, :], xr[:, t * D:(t + 1) * D]).then_inc(sem["x2_st"], 16)
                elif k == "t2_load":
                    sp.wait_ge(sem[n["reader"][0]], n["reader"][1])
                    sp.wait_ge(sem["st0"], n["stored"][0])
                    sp.wait_ge(sem["st1"], n["stored"][1])
                    i = n["i"]
                    src = {"q": q_dram[:, i * P:(i + 1) * P] if n["what"] == "q" else None,
                           "k": kv_dram[:, (i % 2) * P:(i % 2) * P + P],
                           "v": kv_dram[:, 256 + (i % 2) * P:256 + (i % 2) * P + P]}[n["what"]]
                    sp.dma_start(t2[:].rearrange("p (t c) -> p t c", c=P),
                                 src.rearrange("(t p) c -> p t c", p=P)).then_inc(sem["t2_ld"], 16)
                elif k == "k0_load":
                    sp.wait_ge(sem["st0"], n["stored"][0])
                    sp.wait_ge(sem["st1"], n["stored"][1])
                    sp.dma_start(p1[:].rearrange("p (t c) -> p t c", c=P),
                                 kv_dram[:, 0:P].rearrange("(t p) c -> p t c", p=P)).then_inc(sem["k0_ld"], 16)
                elif k == "store_out":
                    sp.wait_ge(sem["fin"], n["fin"])
                    t = n["t"]
                    sp.dma_start(out[t * P:(t + 1) * P, :], xr[:, t * D:(t + 1) * D]).then_inc(sem["out_st"], 16)
            sp.wait_ge(sem["out_st"], total["out_st"])

        @block.gpsimd
        def _(pool):
            chain = [0]

            def linked(ins):
                chain[0] += 1
                ins.then_inc(sem["pool_chain"], 1)
                pool.wait_ge(sem["pool_chain"], chain[0])

            for s in steps:
                k, n = s.kind, s.n
                if k == "start":
                    linked(nc.gpsimd.memset(ident[:], 0.0))
                    linked(nc.gpsimd.affine_select(out=ident[:], in_=ident[:], compare_op=ALU.not_equal, fill=1.0,
                                                   base=0, pattern=[[-1, P]], channel_multiplier=1))
                    linked(nc.gpsimd.memset(tri[:], 0.0))
                    linked(nc.gpsimd.affine_select(out=tri[:], in_=tri[:], compare_op=ALU.is_ge, fill=NEG,
                                                   base=0, pattern=[[-1, P]], channel_multiplier=1))
                    linked(nc.gpsimd.tensor_copy(ident_r[:], ident[:]))
                    linked(nc.gpsimd.tensor_copy(tri_r[:], tri[:]))
                    linked(nc.gpsimd.memset(minus_one, -1.0))
                    nc.gpsimd.memset(minus_half, -0.5).then_inc(sem["consts"], 1)
                    pool.wait_ge(sem["consts"], 1)
                elif k in ("w", "head_w", "ple_w"):
                    slot = n["g"] % RAW_SLOTS
                    pool.wait_ge(sem["raw_ld%d" % slot], s.after["raw_ld%d" % slot])
                    if n["reader"]:
                        pool.wait_ge(sem[n["reader"][0]], n["reader"][1])
                    src = raw[:, slot * CW:(slot + 1) * CW]
                    if k == "w":
                        pairs = [[(w_at(part, n["buf"], n["d"], 0, n["cols"]), 0, n["cols"])] for part in range(2)]
                    else:
                        pairs = [small_dest(s, part) for part in range(2)]
                    for dst, c0, cols in pairs[0]:
                        last = nc.gpsimd.tensor_copy(dst, src[:, c0:c0 + cols])
                    linked(last)
                    for (dst, c0, cols), (hi, _, _) in zip(pairs[1], pairs[0]):
                        last = nc.gpsimd.tensor_tensor(dst, src[:, c0:c0 + cols], hi.bitcast(F32), ALU.subtract)
                    last.then_inc(sem["w"], 1)
                elif k == "E":
                    row = rows[n["ps"]][:, 0:(n["qb"] + 1) * P]
                    pool.wait_ge(sem["ex"], s.after["ex"])
                    one_over = ri[:, n["ps"]:n["ps"] + 1]
                    linked(nc.gpsimd.tensor_tensor(one_over, sm[:, n["ps"]:n["ps"] + 1], minus_one, ALU.pow))
                    nc.gpsimd.tensor_scalar(row, row, one_over, 1.0, ALU.mult, ALU.mult).then_inc(sem["pn"], 1)
                elif k in ("norm_a", "final"):
                    t = n["t"]
                    pool.wait_ge(sem["sq"], s.after["sq"])
                    linked(nc.gpsimd.tensor_scalar(mean[:, t:t + 1], ms[:, t:t + 1], 1.0 / D, EPS, ALU.mult, ALU.add))
                    nc.gpsimd.tensor_tensor(rs[:, t:t + 1], mean[:, t:t + 1], minus_half[:, 0:1],
                                            ALU.pow).then_inc(sem["rstd"], 1)
                elif k == "proj" and n["name"] == "c":
                    c = 2 * n["slot"]
                    pool.wait_ge(sem["sq"], s.after["sq"])
                    linked(nc.gpsimd.tensor_scalar(lat_mean[:, c:c + 2], lat_ms[:, c:c + 2], 1.0 / RANK, EPS,
                                                   ALU.mult, ALU.add))
                    nc.gpsimd.tensor_tensor(lat_rs[:, c:c + 2], lat_mean[:, c:c + 2], minus_half,
                                            ALU.pow).then_inc(sem["rstd"], 1)

        @block.scalar
        def _(act_e):
            def split_hi(s, j, dst, src):
                act_e.wait_ge(sem["b_full"], s.before["b_full"] + j + 1)
                nc.scalar.activation(dst, src, ACT.Copy).then_inc(sem["hi"], 1)

            for s in steps:
                k, n = s.kind, s.n
                if k in ("norm_a", "final"):
                    t = n["t"]
                    act_e.wait_ge(sem[n["ready"][0]] if k == "norm_a" else sem["xadd"],
                                  n["ready"][1] if k == "norm_a" else n["ready"])
                    dst = rows[n["slot"] if k == "norm_a" else 0]
                    nc.scalar.activation(dst[:], xr[:, t * D:(t + 1) * D], ACT.Square,
                                         accum_out=ms[:, t:t + 1]).then_inc(sem["sq"], 1)
                elif k == "w_first":
                    slot = n["g"] % RAW_SLOTS
                    act_e.wait_ge(sem["raw_ld%d" % slot], s.after["raw_ld%d" % slot])
                    nc.scalar.activation(w_at(0, n["buf"], n["d"], 0, CW), raw[:, slot * CW:(slot + 1) * CW],
                                         ACT.Copy).then_inc(sem["w_hi"], 1)
                elif k == "norm_b":
                    t = n["t"]
                    for j in range(2):
                        split_hi(s, j, act_tile(0, t)[:, 4 * j:4 * j + 4, :], in4(bank(s.banks[j])))
                elif k == "split4":
                    split_hi(s, 0, split_dest(s, 0), in4(bank(s.banks[0])))
                elif k == "qi_split":
                    for j in range(2):
                        split_hi(s, j, head_w[n["slot"]][:, j * CW:(j + 1) * CW], bank(s.banks[j]))
                elif k == "tables":
                    for i in range(2):
                        act_e.wait_ge(sem["stage"], s.before["stage"] + i + 1)
                        nc.scalar.activation(cs[:, (1 - i) * CW:(2 - i) * CW], p1[:, i * CW:(i + 1) * CW],
                                             ACT.Sin).then_inc(sem["trig"], 1)
                elif k == "table_t":
                    for j in range(2):
                        act_e.wait_ge(sem["b_full"], s.before["b_full"] + j + 1)
                        nc.scalar.activation(t2[:, j * CW:(j + 1) * CW], bank(s.banks[j]), ACT.Copy,
                                             scale=MLA_SCALE).then_inc(sem["csq"], 1)
                elif k == "bit":
                    act_e.wait_ge(sem["cand"], s.after["cand"])
                    act_e.wait_ge(sem["lo"], s.before["lo"])
                    for t in ACT_TILES:
                        i = SEARCH.index(t)
                        if s.before["tally"] or t != ACT_TILES[0]:
                            act_e.wait_ge(sem["tally"], s.before["tally"] + ACT_TILES.index(t))
                        nc.scalar.activation(bank(6, (t + 1) * P), score_at(t), ACT.Sign,
                                             bias=u_minus.bitcast(F32)[:, i:i + 1],
                                             accum_out=cnt[:, i:i + 1]).then_inc(sem["tally"], 1)
                elif k == "silu_room":
                    act_e.wait_ge(sem["rot"], n["rot"])
                elif k == "proj":
                    name, b = n["name"], s.banks[0]
                    if name == "z":
                        slot = n["slot"]
                        act_e.wait_ge(sem["a_full"], s.after["a_full"])
                        if s.before["z_st%d" % slot]:
                            act_e.wait_ge(sem["z_st%d" % slot], s.before["z_st%d" % slot])
                        nc.scalar.activation((gz, p0)[n["lay"]][:, slot * CW:(slot + 1) * CW], bank(b),
                                             ACT.Silu).then_inc(sem["zs"], 1)
                    elif name in ("kpe", "kiwi"):
                        act_e.wait_ge(sem["a_full"], s.after["a_full"])
                        if name == "kpe":
                            act_e.wait_ge(sem["trig"], s.before["trig"])
                        else:
                            act_e.wait_ge(sem["xn"], s.before["xn"])
                        nc.scalar.activation((p1, gz)[n["lay"]][:, n["slot"] * CW:(n["slot"] + 1) * CW], bank(b),
                                             ACT.Copy).then_inc(sem["fk"], 1)
                    elif name == "c":
                        act_e.wait_ge(sem["a_full"], s.after["a_full"])
                        for r in range(2):
                            c = n["job"] * D + CW + r * RANK
                            nc.scalar.activation(xr[:, c:c + RANK], bank(b)[:, r * RANK:(r + 1) * RANK], ACT.Square,
                                                 accum_out=lat_ms[:, 2 * n["slot"] + r:2 * n["slot"] + r + 1]).then_inc(sem["sq"], 1)
                    elif name == "gate":
                        act_e.wait_ge(sem["a_full"], s.after["a_full"])
                        act_e.wait_ge(sem["xadd"], n["wait_add"])
                        nc.scalar.activation(p1[:, n["slot"] * CW:(n["slot"] + 1) * CW], bank(b),
                                             ACT.Sigmoid).then_inc(sem["sg"], 1)
                    elif name == "kv":
                        act_e.wait_ge(sem["a_full"], s.after["a_full"])
                        if n["st_before"]:
                            act_e.wait_ge(sem["st%d" % n["slot"]], n["st_before"])
                        c = n["slot"] * CW + 256
                        nc.scalar.activation(p1[:, c:c + 256], bank(b)[:, 256:512], ACT.Copy).then_inc(sem["vcopy"], 1)
                elif k == "p_split":
                    split_hi(s, 0, p_t[0][:], bank(s.banks[0], PLE))
                elif k == "hproj":
                    b, j, name = s.banks[0], n["j"], n["name"]
                    if name == "pe":
                        act_e.wait_ge(sem["stage"], s.after["stage"])
                    at = {"q": Q0, "pe": PE0, "k": K0, "v": V0}[name]
                    act_e.wait_ge(sem["b_full"], s.after["b_full"])
                    nc.scalar.activation(region(0, at, j * CW, CW), bank(b), ACT.Copy,
                                         scale=MLA_SCALE if name == "q" else 1.0).then_inc(sem["hi"], 1)
                elif k == "idx":
                    for j in range(2):
                        act_e.wait_ge(sem["b_full"], s.before["b_full"] + j + 1)
                        last_use = s.before["sc"] + j - (1 if n["keys"] > CW else 3)
                        if n["k"] >= 4:
                            act_e.wait_ge(sem["sc"], last_use)
                        elif n["k"] + j == 0:
                            act_e.wait_ge(sem[n["gfree"][0]], n["gfree"][1])
                        nc.scalar.activation(relu_slot(n["k"] + j, n["keys"]), bank(s.banks[j], n["keys"]), ACT.Relu,
                                             scale=IDX_SCALE).then_inc(sem["relu"], 1)
                elif k == "E":
                    ps, keys = n["ps"], (n["qb"] + 1) * P
                    src = bank(n["bank"], keys) if n["lay"] == 0 else rows[ps][:, 0:keys]
                    act_e.wait_ge(sem["nb"], n["nb"])
                    if n["lay"] == 0 and ps == 2:
                        act_e.wait_ge(sem["cs_st"], 16)
                    nc.scalar.activation(rows[ps][:, 0:keys], src, ACT.Exp, bias=nb[:, ps:ps + 1],
                                         scale=1.0 if n["lay"] == 0 else -1.0,
                                         accum_out=sm[:, ps:ps + 1]).then_inc(sem["ex"], 1)
                elif k == "T":
                    for j, b in enumerate(s.banks):
                        kts = min(4, n["qb"] + 1 - 4 * j)
                        split_hi(s, j, pt_tiles(0, n["pbuf"], n["qb"], 4 * j, kts), in4(bank(b, kts * P)))
                elif k == "og_split":
                    t = n["t"]
                    act_e.wait_ge(sem["og"], s.after["og"])
                    act_e.wait_ge(sem["b_full"], n["act_free"])
                    nc.scalar.activation(act_tile(0, t), in4(xr[:, t * D:(t + 1) * D]), ACT.Copy).then_inc(sem["hi"], 1)
                elif k == "v_split":
                    act_e.wait_ge(sem["t2_ld"], n["ld"])
                    act_e.wait_ge(sem["a_full"], n["act_free"])
                    nc.scalar.activation(v1(0, n["g"], 0, S), t2[:], ACT.Copy).then_inc(sem["hi"], 1)

        @block.vector
        def _(dve):
            chain = [0]

            def linked(ins):
                chain[0] += 1
                ins.then_inc(sem["dve_chain"], 1)
                dve.wait_ge(sem["dve_chain"], chain[0])

            def split_lo(s, j, dst, src, hi):
                dve.wait_ge(sem["hi"], s.before["hi"] + j + 1)
                nc.vector.tensor_tensor(dst, src, hi.bitcast(F32), ALU.subtract).then_inc(sem["lo"], 1)

            def rotate(s, src, groups, half, c_ap, s_ap, dsts):
                pa = p0[:, 0:2 * groups * half].rearrange("p (g u e) -> p g u e", u=2, e=half)
                pb = p0[:, CW:CW + 2 * groups * half].rearrange("p (g u e) -> p g u e", u=2, e=half)
                if s.before["rot"]:
                    dve.wait_ge(sem["rot"], s.before["rot"])
                nc.vector.tensor_tensor(pa, src, c_ap, ALU.mult)
                nc.vector.tensor_tensor(pb, src, s_ap, ALU.mult).then_inc(sem["rot_in"], 1)
                dve.wait_ge(sem["rot_in"], s.after["rot_in"])
                for dst in dsts:
                    nc.vector.tensor_tensor(dst[:, :, 0, :], pa[:, :, 0, :], pb[:, :, 1, :], ALU.subtract)
                    last = nc.vector.tensor_tensor(dst[:, :, 1, :], pa[:, :, 1, :], pb[:, :, 0, :], ALU.add)
                last.then_inc(sem["rot"], 1)

            cos_all = cs[:, 0:CW].rearrange("p (t e) -> p t e", e=HALF)
            sin_all = cs[:, CW:2 * CW].rearrange("p (t e) -> p t e", e=HALF)

            def trig_tile(tab, t, step, groups):
                v = tab[:, t, 0::step]
                return v.unsqueeze(1).unsqueeze(1).to_broadcast([P, groups, 2, HALF // step])

            def trig_tiles(tab, t0):
                v = tab[:, t0:t0 + 4, 0::2]
                return v.unsqueeze(2).to_broadcast([P, 4, 2, HALF // 2])

            for s in steps:
                k, n = s.kind, s.n
                if k == "norm_a":
                    t, slot = n["t"], n["slot"]
                    dve.wait_ge(sem["rstd"], s.after["rstd"])
                    dve.wait_ge(sem["gain"], n["gain"])
                    nc.vector.scalar_tensor_tensor(rows[slot][:], xr[:, t * D:(t + 1) * D], rs[:, t:t + 1], gz[:],
                                                   ALU.mult, ALU.mult).then_inc(sem["xn"], 1)
                elif k == "w_first":
                    slot = n["g"] % RAW_SLOTS
                    dve.wait_ge(sem["w_hi"], s.after["w_hi"])
                    nc.vector.tensor_tensor(w_at(1, n["buf"], n["d"], 0, CW), raw[:, slot * CW:(slot + 1) * CW],
                                            w_at(0, n["buf"], n["d"], 0, CW).bitcast(F32),
                                            ALU.subtract).then_inc(sem["w0"], 1)
                elif k == "final":
                    t = n["t"]
                    dve.wait_ge(sem["rstd"], s.after["rstd"])
                    dve.wait_ge(sem["gain"], n["gain"])
                    rw = xr[:, t * D:(t + 1) * D]
                    nc.vector.scalar_tensor_tensor(rw, rw, rs[:, t:t + 1], gz[:], ALU.mult, ALU.mult).then_inc(sem["fin"], 1)
                elif k == "norm_b":
                    t = n["t"]
                    for j in range(2):
                        split_lo(s, j, act_tile(1, t)[:, 4 * j:4 * j + 4, :], in4(bank(s.banks[j])),
                                 act_tile(0, t)[:, 4 * j:4 * j + 4, :])
                elif k == "split4":
                    split_lo(s, 0, split_dest(s, 1), in4(bank(s.banks[0])), split_dest(s, 0))
                elif k == "qi_split":
                    for j in range(2):
                        at = head_w[n["slot"]][64:128, j * CW:(j + 1) * CW]
                        split_lo(s, j, at, bank(s.banks[j])[64:128, :], at)
                elif k == "tables":
                    c1, c2, c3 = two_pi_parts()
                    back = t2[:, 0:CW]
                    dve.wait_ge(sem["const_ld"], 32)
                    dve.wait_ge(sem["hi"], s.before["hi"])
                    dve.wait_ge(sem["xn"], s.before["xn"])
                    linked(nc.vector.tensor_copy(posf, pos_i[:]))
                    ang = t2[:, CW:2 * CW]
                    for t in range(T):
                        last = nc.vector.tensor_scalar(ang[:, t * NFREQ:(t + 1) * NFREQ], frq[:], posf[:, t:t + 1],
                                                       None, ALU.mult)
                    linked(last)
                    for i in range(2):
                        turns = p1[:, i * CW:(i + 1) * CW]
                        linked(nc.vector.tensor_scalar(turns, ang, 1.0 / TWO_PI, 0.25 * i, ALU.mult, ALU.add))
                        linked(nc.vector.tensor_scalar(turns, turns, 12582912.0, -12582912.0, ALU.add, ALU.add))
                        linked(nc.vector.scalar_tensor_tensor(back, turns, -c1, ang, ALU.mult, ALU.add))
                        linked(nc.vector.scalar_tensor_tensor(back, turns, -c2, back, ALU.mult, ALU.add))
                        linked(nc.vector.scalar_tensor_tensor(back, turns, -c3, back, ALU.mult, ALU.add))
                        nc.vector.tensor_scalar(turns, back, 0.25 * i * TWO_PI, None, ALU.add).then_inc(sem["stage"], 1)
                elif k == "table_t":
                    dve.wait_ge(sem["hi"], s.before["hi"])
                    for j in range(2):
                        st = p1[:, j * CW:(j + 1) * CW].rearrange("p (t u e) -> p t u e", t=4, u=4)
                        co, si = cos_all[:, 4 * j:4 * j + 4, 0::2], sin_all[:, 4 * j:4 * j + 4, 0::2]
                        nc.vector.tensor_copy(st[:, :, 0, :], co)
                        nc.vector.tensor_copy(st[:, :, 1, :], co)
                        nc.vector.tensor_scalar(st[:, :, 2, :], si, -1.0, None, ALU.mult)
                        nc.vector.tensor_copy(st[:, :, 3, :], si).then_inc(sem["stage"], 1)
                elif k == "proj":
                    name, b = n["name"], s.banks[0]
                    if name in ("qi", "kv", "q"):
                        dve.wait_ge(sem["a_full"], s.after["a_full"])
                        slot, job = n["slot"], n["job"]
                        st = p1[:, slot * CW:(slot + 1) * CW]
                        if name == "qi":
                            dve.wait_ge(sem["cs_ld"], n["cs"])
                            dve.wait_ge(sem["hi"], s.before["hi"])
                            dup = p1[:].rearrange("p (g r u e) -> p g r u e", r=2, u=2, e=32)
                            rotate(s, bank(b).rearrange("p (g u e) -> p g u e", u=2, e=32), 8, 32,
                                   trig_tile(cos_all, job, 2, 8), trig_tile(sin_all, job, 2, 8),
                                   [dup[:, :, r] for r in range(2)])
                        else:
                            g = 4 if name == "q" else 2
                            if name == "kv":
                                dve.wait_ge(sem["vcopy"], s.after["vcopy"])
                            if n["st_before"]:
                                dve.wait_ge(sem["st%d" % slot], n["st_before"])
                            rotate(s, bank(b, g * HD).rearrange("p (g u e) -> p g u e", u=2, e=HALF), g, HALF,
                                   trig_tile(cos_all, job, 1, g), trig_tile(sin_all, job, 1, g),
                                   [st[:, 0:g * HD].rearrange("p (g u e) -> p g u e", u=2, e=HALF)])
                    elif name == "c":
                        dve.wait_ge(sem["rstd"], s.after["rstd"])
                        dve.wait_ge(sem["lat_ld"], 32)
                        for r in range(2):
                            c = n["job"] * D + r * RANK
                            last = nc.vector.scalar_tensor_tensor(
                                xr[:, c:c + RANK], bank(b)[:, r * RANK:(r + 1) * RANK],
                                lat_rs[:, 2 * n["slot"] + r:2 * n["slot"] + r + 1], t2[:, r * RANK:(r + 1) * RANK],
                                ALU.mult, ALU.mult)
                        last.then_inc(sem["xn"], 1)
                    elif name == "wo":
                        dve.wait_ge(sem["a_full"], s.after["a_full"])
                        dve.wait_ge(sem["xin%d" % n["slot"]], n["xin"])
                        c = n["job"] * D + n["j"] * CW
                        nc.vector.tensor_tensor(xr[:, c:c + CW], bank(b), p1[:, n["slot"] * CW:(n["slot"] + 1) * CW],
                                                ALU.add).then_inc(sem["xadd"], 1)
                elif k == "key_back":
                    b, job = s.banks[0], n["job"]
                    dve.wait_ge(sem["b_full"], s.after["b_full"])
                    if n["lay"] == 0:
                        dve.wait_ge(sem["trig"], n["trig"])
                    v = in4(bank(b))
                    if n["lay"] == 1:
                        nc.vector.tensor_scalar(
                            wis[:].rearrange("p (t h) -> p t h", h=IDX_HEADS)[:, 4 * job:4 * job + 4, :],
                            v[:, :, IDX_DIM:IDX_DIM + IDX_HEADS], W_IDX_SCALE, None, ALU.mult).then_inc(sem["widx"], 1)
                    dup = (p1, t2)[n["lay"]][:, job * CW:(job + 1) * CW].rearrange(
                        "p (t r u e) -> p t r u e", t=4, r=2, u=2)
                    rotate(s, v[:, :, 0:64].rearrange("p t (u e) -> p t u e", u=2), 4, 32,
                           trig_tiles(cos_all, 4 * job), trig_tiles(sin_all, 4 * job),
                           [dup[:, :, r] for r in range(2)])
                elif k == "pp":
                    dve.wait_ge(sem["sg"], n["sg"])
                    dve.wait_ge(sem["b_full"], s.after["b_full"])
                    st = p1[:, n["slot"] * CW:(n["slot"] + 1) * CW]
                    nc.vector.tensor_tensor(st, bank(s.banks[0]), st, ALU.mult).then_inc(sem["pp"], 1)
                    dve.wait_ge(sem["pp"], s.after["pp"])
                    c = n["t"] * D + n["j"] * CW
                    nc.vector.tensor_tensor(xr[:, c:c + CW], xr[:, c:c + CW], st, ALU.add).then_inc(sem["xadd"], 1)
                elif k == "p_split":
                    split_lo(s, 0, p_t[1][:], bank(s.banks[0], PLE), p_t[0][:])
                elif k == "hproj":
                    b, j, name = s.banks[0], n["j"], n["name"]
                    if name == "pe":
                        dve.wait_ge(sem["b_full"], s.after["b_full"])
                        dve.wait_ge(sem["csq"], n["csq"])
                        nc.vector.tensor_tensor(bank(b), bank(b), t2[:, j * CW:(j + 1) * CW],
                                                ALU.mult).then_inc(sem["stage"], 1)
                    at = {"q": Q0, "pe": PE0, "k": K0, "v": V0}[name]
                    if name == "q":
                        dve.wait_ge(sem["hi"], s.after["hi"])
                        nc.vector.scalar_tensor_tensor(region(1, at, j * CW, CW), bank(b), MLA_SCALE,
                                                       region(0, at, j * CW, CW).bitcast(F32),
                                                       ALU.mult, ALU.subtract).then_inc(sem["lo"], 1)
                    else:
                        split_lo(s, 0, region(1, at, j * CW, CW), bank(b), region(0, at, j * CW, CW))
                elif k == "idx":
                    t = n["t"]
                    dst = score_at(t)
                    dve.wait_ge(sem["widx"], s.before["widx"])
                    for j in range(2):
                        h = n["h"] + j
                        dve.wait_ge(sem["relu"], s.before["relu"] + j + 1)
                        if n["k"] + j == 0:
                            dve.wait_ge(sem["x2_st"], n["x2"])
                        else:
                            dve.wait_ge(sem["sc"], s.before["sc"] + j)
                        src = relu_slot(n["k"] + j, n["keys"])
                        wcol = wis[:, t * IDX_HEADS + h:t * IDX_HEADS + h + 1]
                        if h == 0:
                            nc.vector.tensor_scalar(dst, src, wcol, None, ALU.mult).then_inc(sem["sc"], 1)
                        else:
                            nc.vector.scalar_tensor_tensor(dst, src, wcol, dst, ALU.mult, ALU.add).then_inc(sem["sc"], 1)
                elif k == "idx_mask":
                    dve.wait_ge(sem["sc"], s.after["sc"])
                    dst = score_at(n["t"], n["t"] * P, P)
                    linked(nc.vector.tensor_tensor(dst, dst, tri[:], ALU.add))
                elif k == "bit":
                    bit = n["bit"]
                    cand = u_cand.bitcast(F32)
                    if bit == 31:
                        linked(nc.vector.memset(cand, 0.0))
                        for i, t in enumerate(SEARCH):
                            linked(nc.vector.memset(reach[:, i:i + 1],
                                                    2.0 * TOPK - (t + 1) * P if t in ACT_TILES else float(TOPK)))
                        nc.vector.memset(u_minus.bitcast(F32), 0.0).then_inc(sem["cand"], 1)
                    else:
                        linked(nc.vector.scalar_tensor_tensor(u_cand, u_bits, 1 << bit, u_mask,
                                                              ALU.bitwise_or, ALU.bitwise_xor))
                        nc.vector.scalar_tensor_tensor(u_minus, u_bits, 1 << bit, u_mask2,
                                                       ALU.bitwise_or, ALU.bitwise_xor).then_inc(sem["cand"], 1)
                    for i, t in enumerate(SEARCH):
                        if t not in ACT_TILES:
                            linked(nc.vector.tensor_scalar(gz[:, 0:(t + 1) * P], score_at(t), cand[:, i:i + 1], 0.0,
                                                           ALU.is_ge, ALU.add, accum_out=cnt[:, i:i + 1]))
                elif k == "bit_end":
                    bit = n["bit"]
                    dve.wait_ge(sem["tally"], n["tally"])
                    linked(nc.vector.tensor_tensor(u_inc, cnt, reach, ALU.is_ge))
                    if bit == 31:
                        linked(nc.vector.tensor_scalar(u_bits, u_inc, 31, None, ALU.logical_shift_left))
                        um, um2 = u_mask.bitcast(I32), u_mask2.bitcast(I32)
                        linked(nc.vector.tensor_scalar(um2, u_bits.bitcast(I32), -(1 << 31), 31,
                                                       ALU.bitwise_xor, ALU.arith_shift_right))
                        linked(nc.vector.tensor_scalar(um, um2, -(1 << 31), None, ALU.bitwise_or))
                        linked(nc.vector.tensor_scalar(um2, um, -(1 << 31), None, ALU.bitwise_xor))
                    else:
                        linked(nc.vector.scalar_tensor_tensor(u_bits, u_inc, bit, u_bits,
                                                              ALU.logical_shift_left, ALU.bitwise_or))
                elif k == "last_step":
                    linked(nc.vector.tensor_scalar(u_inc, u_bits, 0xFFFF, None, ALU.bitwise_and))
                    linked(nc.vector.tensor_scalar(u_cand, u_bits, 16, None, ALU.logical_shift_right))
                    linked(nc.vector.tensor_scalar(u_inc, u_inc, 1.0, None, ALU.add))
                    linked(nc.vector.tensor_scalar(u_minus, u_inc, 16, None, ALU.logical_shift_right))
                    linked(nc.vector.tensor_tensor(u_cand, u_cand, u_minus, ALU.add))
                    linked(nc.vector.tensor_scalar(u_inc, u_inc, 0xFFFF, None, ALU.bitwise_and))
                    linked(nc.vector.scalar_tensor_tensor(u_minus, u_cand, 16, u_inc,
                                                          ALU.logical_shift_left, ALU.bitwise_or))
                    linked(nc.vector.tensor_tensor(u_cand, u_minus, u_mask, ALU.bitwise_xor))
                    for i, t in enumerate(SEARCH):
                        linked(nc.vector.tensor_scalar(gz[:, 0:(t + 1) * P], score_at(t),
                                                       u_cand.bitcast(F32)[:, i:i + 1], 0.0,
                                                       ALU.is_ge, ALU.add, accum_out=cnt[:, i:i + 1]))
                    linked(nc.vector.tensor_scalar(u_inc, cnt, TOPK - 0.5, None, ALU.is_gt))
                    linked(nc.vector.tensor_scalar(u_inc.bitcast(I32), u_inc.bitcast(I32), 31, 31,
                                                   ALU.logical_shift_left, ALU.arith_shift_right))
                    linked(nc.vector.tensor_tensor(u_minus, u_minus, u_bits, ALU.bitwise_xor))
                    linked(nc.vector.tensor_tensor(u_minus, u_minus, u_inc, ALU.bitwise_and))
                    linked(nc.vector.tensor_tensor(u_bits, u_bits, u_minus, ALU.bitwise_xor))
                elif k == "above":
                    linked(nc.vector.tensor_tensor(u_cand, u_bits, u_mask, ALU.bitwise_xor))
                    thr = u_cand.bitcast(F32)
                    for i, t in enumerate(SEARCH):
                        linked(nc.vector.tensor_scalar(gz[:, 0:(t + 1) * P], score_at(t), thr[:, i:i + 1], 0.0,
                                                        ALU.is_gt, ALU.add, accum_out=cnt[:, i:i + 1]))
                    linked(nc.vector.tensor_scalar(need, cnt, -1.0, float(TOPK), ALU.mult, ALU.add))
                elif k == "sel":
                    t = n["t"]
                    i, keys = SEARCH.index(t), (t + 1) * P
                    thr = u_cand.bitcast(F32)[:, i:i + 1]
                    eq, order = gz[:, 0:keys], cs[:, 0:keys]
                    if t > FULL:
                        dve.wait_ge(sem["found"], s.before["found"])
                    linked(nc.vector.tensor_scalar(eq, score_at(t), thr, None, ALU.is_equal))
                    linked(nc.vector.tensor_tensor_scan(order, eq, eq, 0.0, ALU.add, ALU.max))
                    linked(nc.vector.scalar_tensor_tensor(eq, order, need[:, i:i + 1], eq, ALU.is_le, ALU.mult))
                    nc.vector.scalar_tensor_tensor(score_at(t), score_at(t), thr, eq, ALU.is_gt,
                                                   ALU.add).then_inc(sem["found"], 1)
                elif k == "mask":
                    t = n["t"]
                    if n["first"]:
                        dve.wait_ge(sem["a_full"], n["a_full"])
                        dve.wait_ge(sem["found"], s.before["found"])
                        dve.wait_ge(sem["z_st0"], s.before["z_st0"])
                        dve.wait_ge(sem["z_st1"], s.before["z_st1"])
                    if t < FULL:
                        if t:
                            nc.vector.memset(mask_at(t)[:, 0:t * P].bitcast(F32), 0.0)
                        linked(nc.vector.tensor_copy(mask_at(t)[:, t * P:(t + 1) * P], tri[:]))
                    else:
                        linked(nc.vector.tensor_scalar(mask_at(t), score_at(t), -1.0, -NEG, ALU.add, ALU.mult))
                elif k == "S":
                    ps, keys = n["ps"], (n["qb"] + 1) * P
                    dve.wait_ge(sem["a_full"], s.after["a_full"])
                    src = bank(s.banks[0], keys)
                    if n["lay"] == 0:
                        nc.vector.tensor_reduce(nb[:, ps:ps + 1], src, AX_X, ALU.max, negate=True).then_inc(sem["nb"], 1)
                    else:
                        nc.vector.tensor_tensor_reduce(rows[ps][:, 0:keys], src, mask_at(n["qb"]).bitcast(F32),
                                                       -DSA_SCALE, 3.4e38, ALU.add, ALU.min,
                                                       nb[:, ps:ps + 1]).then_inc(sem["nb"], 1)
                elif k == "T":
                    for j, b in enumerate(s.banks):
                        kts = min(4, n["qb"] + 1 - 4 * j)
                        parts = [pt_tiles(part, n["pbuf"], n["qb"], 4 * j, kts) for part in range(2)]
                        split_lo(s, j, parts[1], in4(bank(b, kts * P)), parts[0])
                elif k == "PV":
                    h, g = n["h"], n["g"]
                    dve.wait_ge(sem["b_full"], s.after["b_full"])
                    dve.wait_ge(sem["z_ld"], n["z_ld"])
                    dst = xr[:].rearrange("p (t c) -> p t c", c=D)[:, 2 * g:2 * g + 2, h * P:(h + 1) * P]
                    nc.vector.tensor_tensor(dst, in4(bank(s.banks[0], 256)), in4(gz[:, g * 256:(g + 1) * 256]),
                                            ALU.mult).then_inc(sem["og"], 1)
                elif k == "og_split":
                    t = n["t"]
                    dve.wait_ge(sem["hi"], s.after["hi"])
                    nc.vector.tensor_tensor(act_tile(1, t), in4(xr[:, t * D:(t + 1) * D]), act_tile(0, t).bitcast(F32),
                                            ALU.subtract).then_inc(sem["lo"], 1)
                elif k == "v_split":
                    dve.wait_ge(sem["hi"], s.after["hi"])
                    nc.vector.tensor_tensor(v1(1, n["g"], 0, S), t2[:], v1(0, n["g"], 0, S).bitcast(F32),
                                            ALU.subtract).then_inc(sem["lo"], 1)

        @block.tensor
        def _(pe):
            def product(dst, lhs, rhs, start, stop):
                nc.tensor.matmul(dst, lhs(1), rhs(0), start=start, stop=False)
                nc.tensor.matmul(dst, lhs(0), rhs(1), start=False, stop=False)
                return nc.tensor.matmul(dst, lhs(0), rhs(0), start=False, stop=stop)

            def bank_free(s, j=0):
                for name, v in s.free[j]:
                    pe.wait_ge(sem[name], v)

            for s in steps:
                k, n = s.kind, s.n
                if k == "norm_b":
                    pe.wait_ge(sem["xn"], n["xn"])
                    pe.wait_ge(sem["consts"], 1)
                    for j in range(2):
                        bank_free(s, j)
                        for i in range(4):
                            c = (4 * j + i) * P
                            last = nc.tensor.transpose(bank(s.banks[j])[:, i * P:(i + 1) * P],
                                                       rows[n["slot"]][:, c:c + P], ident[:])
                        last.then_inc(sem["b_full"], 1)
                elif k == "split4":
                    pe.wait_ge(sem[n["ready"][0]], n["ready"][1])
                    bank_free(s)
                    if n["src"] == "xr":
                        src = xr[:, n["t"] * D:n["t"] * D + CW]
                    else:
                        src = (t2 if n["src"] == "t2" else p1)[:, n["j"] * CW:(n["j"] + 1) * CW]
                    for i in range(4):
                        last = nc.tensor.transpose(bank(s.banks[0])[:, i * P:(i + 1) * P], src[:, i * P:(i + 1) * P],
                                                   ident[:])
                    last.then_inc(sem["b_full"], 1)
                elif k == "qi_split":
                    pe.wait_ge(sem["rot"], n["rot"])
                    for j in range(2):
                        bank_free(s, j)
                        for i in range(4):
                            c = (4 * j + i) * P
                            last = nc.tensor.transpose(bank(s.banks[j])[:, i * P:(i + 1) * P], p1[:, c:c + P], ident[:])
                        last.then_inc(sem["b_full"], 1)
                elif k == "key_back":
                    pe.wait_ge(sem["fk"], n["fk"])
                    bank_free(s)
                    for i in range(4):
                        c = n["job"] * CW + i * P
                        last = nc.tensor.transpose(bank(s.banks[0])[:, i * P:(i + 1) * P],
                                                   (p1, gz)[n["lay"]][:, c:c + P], ident[:])
                    last.then_inc(sem["b_full"], 1)
                elif k == "table_t":
                    for j in range(2):
                        pe.wait_ge(sem["stage"], s.before["stage"] + 1 + j)
                        bank_free(s, j)
                        for i in range(4):
                            c = j * CW + i * P
                            last = nc.tensor.transpose(bank(s.banks[j])[:, i * P:(i + 1) * P], p1[:, c:c + P], ident[:])
                        last.then_inc(sem["b_full"], 1)
                elif k == "proj":
                    name, b, buf = n["name"], s.banks[0], n["buf"]
                    bank_free(s)
                    pe.wait_ge(sem["lo"], n["act"])
                    if n["half"] is not None:
                        half, m = n["half"], n["job"] % 4 if name == "z" else 0
                        for d in range(KD):
                            pe.wait_ge(sem[n["w_ready"][d][0]], n["w_ready"][d][1])
                            last = product(bank(b), lambda part: w_at(part, buf, d, m * P, P),
                                           lambda part: act_at(part, d, half * CW, CW), d == 0, d == KD - 1)
                    else:
                        t = n["job"]
                        for d in range(KD):
                            pe.wait_ge(sem[n["w_ready"][d][0]], n["w_ready"][d][1])
                            last = product(bank(b), lambda part: act_at(part, d, t * P, P),
                                           lambda part: w_at(part, buf, d, 0, CW), d == 0, d == KD - 1)
                    last.then_inc(sem["a_full"], 1)
                elif k == "p_split":
                    pe.wait_ge(sem["p_ld%d" % n["slot"]], n["p_ld"])
                    bank_free(s)
                    for i in range(2):
                        c = n["slot"] * PLE + i * P
                        last = nc.tensor.transpose(bank(s.banks[0])[:, i * P:(i + 1) * P], t2[:, c:c + P], ident[:])
                    last.then_inc(sem["b_full"], 1)
                elif k == "pp":
                    pe.wait_ge(sem["lo"], n["ready"])
                    pe.wait_ge(sem["w"], n["w_ready"])
                    bank_free(s)
                    wp = head_w if n["j"] == 0 else kpe
                    for r in range(2):
                        last = product(bank(s.banks[0]), lambda part: p_t[part][:, r * P:(r + 1) * P],
                                       lambda part: wp[part][:, r * CW:(r + 1) * CW], r == 0, r == 1)
                    last.then_inc(sem["b_full"], 1)
                elif k == "hproj":
                    b, j, name = s.banks[0], n["j"], n["name"]
                    pe.wait_ge(sem["w"], n["w_ready"])
                    pe.wait_ge(sem["lo"], n["c_ready"])
                    bank_free(s)
                    if name in ("q", "pe", "k"):
                        off, step, lat = {"q": (0, 256, 0), "pe": (128, 256, 0), "k": (512, 128, 2)}[name]
                        for r in range(2):
                            last = product(bank(b), lambda part: head_w[part][:, off + r * step:off + r * step + P],
                                           lambda part: ring[part][:, CT0 + (lat + r) * S + j * CW:CT0 + (lat + r) * S + (j + 1) * CW],
                                           r == 0, r == 1)
                    else:
                        for i in range(2):
                            kt = 2 * j + i
                            for r in range(2):
                                last = product(bank(b)[:, i * 256:(i + 1) * 256],
                                               lambda part: ring[part][:, CT0 + (2 + r) * S + kt * P:CT0 + (2 + r) * S + (kt + 1) * P],
                                               lambda part: p_t[part][:] if r == 0 else head_w[part][:, 768:1024],
                                               r == 0, r == 1)
                    last.then_inc(sem["b_full"], 1)
                elif k == "idx":
                    t = n["t"]
                    pe.wait_ge(sem["lo"], n["q_ready"])
                    bank_free(s, 0)
                    bank_free(s, 1)
                    for k0 in range(0, n["keys"], CW):
                        kn = min(CW, n["keys"] - k0)
                        for j in range(2):
                            at = s.banks[j] * CW + k0
                            for part in (1, 0):
                                last = nc.tensor.matmul(psum[:, at:at + kn], qi_at(t, n["h"] + j),
                                                        kpe[part][:, k0:k0 + kn], start=part == 1, stop=part == 0)
                            if k0 + kn == n["keys"]:
                                last.then_inc(sem["b_full"], 1)
                elif k == "S":
                    lay, qb = n["lay"], n["qb"]
                    pe.wait_ge(sem["lo"], n["q_ready"])
                    bank_free(s)
                    keys = (qb + 1) * P
                    for c0 in range(0, keys, CW):
                        cn = min(CW, keys - c0)
                        dst = psum[:, s.banks[0] * CW + c0:s.banks[0] * CW + c0 + cn]
                        if lay == 0:
                            diag = c0 + cn == keys
                            product(dst, lambda part: region(part, Q0, qb * P, P),
                                    lambda part: region(part, K0, c0, cn), True, False)
                            last = product(dst, lambda part: region(part, PE0, qb * P, P),
                                           lambda part: kpe[part][:, c0:c0 + cn], False, not diag)
                            if diag:
                                last = nc.tensor.matmul(dst[:, cn - P:cn], ident_r[:], tri_r[:], start=False, stop=True)
                        else:
                            g = n["h"] // GROUP
                            last = product(dst, lambda part: qT1(part, n["h"] % 2, qb * P, P),
                                           lambda part: kT1(part, g, c0, cn), True, True)
                    last.then_inc(sem["a_full"], 1)
                elif k == "T":
                    pe.wait_ge(sem["pn"], n["pn"])
                    for j, b in enumerate(s.banks):
                        bank_free(s, j)
                        for i in range(min(4, n["qb"] + 1 - 4 * j)):
                            c = (4 * j + i) * P
                            last = nc.tensor.transpose(bank(b)[:, i * P:(i + 1) * P], rows[n["ps"]][:, c:c + P], ident[:])
                        last.then_inc(sem["b_full"], 1)
                elif k == "PV":
                    g, lay = n["g"], n["lay"]
                    pe.wait_ge(sem["lo"], n["ready"])
                    bank_free(s)
                    kts = 2 * g + 2
                    for kt in range(kts):
                        c0 = max(0, kt - 2 * g) * P
                        vals = ((lambda part: region(part, V0, kt * 256 + n["h"] % 2 * P, P)) if lay == 0
                                else (lambda part: v1(part, n["h"] // GROUP, kt * P, P)))
                        last = product(bank(s.banks[0])[:, c0:256], vals,
                                       lambda part: pt_at(part, n["pbuf"], kt, c0, 256 - c0), kt == 0, kt == kts - 1)
                    last.then_inc(sem["b_full"], 1)


NAMES = ["x", "p", "positions", "norm_in", "mla_w_in", "mla_q_norm", "mla_kv_norm", "mla_w_uq", "mla_w_uk",
         "mla_w_uv", "mla_w_out", "dsa_w_in", "dsa_w_out", "ple_w_proj", "ple_norm", "ple_w_gate", "final_norm"]


def kernel(**inputs):
    import concourse.bacc as bacc
    from concourse.bass_utils import run_bass_kernel_spmd as run

    nc = bacc.Bacc("TRN2", target_bir_lowering=False, num_devices=1)
    arrays = {n: np.ascontiguousarray(inputs[n]) for n in NAMES}
    half = np.float32(NFREQ)
    arrays["freqs"] = (1.0 / (np.float32(10000.0) ** (np.arange(NFREQ, dtype=np.float32) / half))).astype(np.float32)
    h = {n: nc.dram_tensor("in_" + n, a.shape, mybir.dt.from_np(a.dtype), kind="ExternalInput").ap()
         for n, a in arrays.items()}
    out = nc.dram_tensor("out", (1, S, D), F32, kind="ExternalOutput").ap()
    build(nc, h["x"][0], h["p"].rearrange("l b s c -> (l b) s c"), h["positions"], h["norm_in"],
          h["mla_w_in"][0], h["mla_q_norm"][0], h["mla_kv_norm"][0], h["mla_w_uq"][0],
          h["mla_w_uk"][0].rearrange("c h n -> c (h n)"), h["mla_w_uv"][0].rearrange("c h n -> c (h n)"),
          h["mla_w_out"][0], h["dsa_w_in"][0], h["dsa_w_out"][0], h["ple_w_proj"], h["ple_norm"], h["ple_w_gate"],
          h["final_norm"], h["freqs"], out[0])
    r = run(nc, [{"in_" + n: a for n, a in arrays.items()}], core_ids=[0])
    return r.results[0]["out"]
```
